# Optimizing a Trainium2 kernel written in Bass

```python
import math
import jax
import jax.numpy as jnp
from jax import lax
import numpy as np
import jax, jax.numpy as jnp

D_MODEL = 1024
BATCH = 1
SEQ = 256
DEPTH = 2

HEAD_DIM = 64
Q_BLOCK = 128
EPS = 1e-6
NEG = -1e30

NUM_BUCKETS = 32
MAX_DISTANCE = 128
BIAS_HEADS = 16

NSA_HEADS = 8
NSA_KV_HEADS = 2
NSA_GROUP = NSA_HEADS // NSA_KV_HEADS
CMP_BLOCK = 32
CMP_STRIDE = 16
CMP_HIDDEN = 128
SEL_BLOCK = 64
SEL_TOPN = 16
WINDOW = 512
FORCE_BONUS = 1e3

DIFF_HEADS = 4
DIFF_VDIM = 2 * HEAD_DIM

MOBA_HEADS = 16
MOBA_BLOCK = 256
MOBA_TOPK = 3
MOBA_QCHUNK = 32

D_FF = 4 * D_MODEL

NSA_Q = NSA_HEADS * HEAD_DIM
NSA_KV = NSA_KV_HEADS * HEAD_DIM
NSA_GATES = 3 * NSA_HEADS
DIFF_QK = DIFF_HEADS * 2 * HEAD_DIM
DIFF_V = DIFF_HEADS * DIFF_VDIM
D_MIX = NSA_Q + DIFF_V
EVEN_SIZES = (NSA_Q,) + (NSA_KV,) * 6 + (NSA_GATES, DIFF_QK, DIFF_QK, DIFF_V)
EVEN_PROJ = sum(EVEN_SIZES)
ODD_PROJ = 3 * MOBA_HEADS * HEAD_DIM
ODD_MIX = MOBA_HEADS * HEAD_DIM


def rms_norm(x, g):
    xf = x.astype(jnp.float32)
    y = xf * lax.rsqrt(jnp.mean(xf * xf, axis=-1, keepdims=True) + EPS)
    return (y * g.astype(jnp.float32)).astype(x.dtype)

def t5_bucket(rel):
    n = jnp.maximum(rel, 0)
    max_exact = NUM_BUCKETS // 2
    large = max_exact + (jnp.log(jnp.maximum(n, 1).astype(jnp.float32) / max_exact)
                         / math.log(MAX_DISTANCE / max_exact)
                         * (NUM_BUCKETS - max_exact)).astype(jnp.int32)
    large = jnp.minimum(large, NUM_BUCKETS - 1)
    return jnp.where(n < max_exact, n, large)

def masked_softmax(logits, mask):
    l = jnp.where(mask, logits.astype(jnp.float32), NEG)
    m = jnp.max(l, axis=-1, keepdims=True)
    p = jnp.where(mask, jnp.exp(l - m), 0.0)
    return p / jnp.maximum(jnp.sum(p, axis=-1, keepdims=True), 1e-30)

def to_heads(t, n):
    b, s, _ = t.shape
    return t.reshape(b, s, n, -1).transpose(0, 2, 1, 3)

def compress_kv(kv, pos, w1, w2):
    b, g, s, d = kv.shape
    nc = (s - CMP_BLOCK) // CMP_STRIDE + 1
    tok = jnp.arange(nc)[:, None] * CMP_STRIDE + jnp.arange(CMP_BLOCK)[None, :]
    blk = kv[:, :, tok] + pos
    hid = jax.nn.gelu(blk.reshape(b, g, nc, CMP_BLOCK * d) @ w1)
    return hid @ w2

def nsa_attention(q, kc, vc, ks, vs, kw, vw, gates, tbl_h):
    b, g, r, s, d = q.shape
    nc = kc.shape[2]
    ns = s // SEL_BLOCK
    n_sel = min(SEL_TOPN, ns)
    scale = d ** -0.5
    tbl_gr = tbl_h.reshape(g, r, NUM_BUCKETS)
    cmp_end = jnp.arange(nc) * CMP_STRIDE + CMP_BLOCK - 1
    tok = jnp.arange(nc)[:, None] * CMP_STRIDE + jnp.arange(CMP_BLOCK)[None, :]
    overlap = jax.nn.one_hot(tok // SEL_BLOCK, ns, dtype=jnp.float32).sum(axis=1) / CMP_BLOCK
    ks_blk = ks.reshape(b, g, ns, SEL_BLOCK, d)
    vs_blk = vs.reshape(b, g, ns, SEL_BLOCK, d)
    kw_pad = jnp.pad(kw, ((0, 0), (0, 0), (WINDOW, 0), (0, 0)))
    vw_pad = jnp.pad(vw, ((0, 0), (0, 0), (WINDOW, 0), (0, 0)))
    span = WINDOW + Q_BLOCK
    bi = jnp.arange(b)[:, None, None, None]
    gi = jnp.arange(g)[None, :, None, None]
    gi6 = jnp.arange(g)[None, :, None, None, None, None]
    ri6 = jnp.arange(r)[None, None, :, None, None, None]
    blk_ids = jnp.arange(ns)

    def block(j):
        q0 = j * Q_BLOCK
        t = q0 + jnp.arange(Q_BLOCK)
        qb = lax.dynamic_slice_in_dim(q, q0, Q_BLOCK, axis=3)
        gb = lax.dynamic_slice_in_dim(gates, q0, Q_BLOCK, axis=4)
        rel_c = t[:, None] - cmp_end[None, :]
        lc = jnp.einsum('bgrqd,bgcd->bgrqc', qb, kc) * scale + tbl_gr[:, :, t5_bucket(rel_c)]
        pc = masked_softmax(lc, rel_c >= 0)
        oc = jnp.einsum('bgrqc,bgcd->bgrqd', pc.astype(vc.dtype), vc)
        imp = jnp.einsum('bgrqc,cn->bgqn', pc, overlap)
        cur = t // SEL_BLOCK
        eligible = blk_ids[None, :] <= cur[:, None]
        forced = ((blk_ids[None, :] == 0) | (blk_ids[None, :] == cur[:, None])
                  | (blk_ids[None, :] == cur[:, None] - 1))
        score = jnp.where(eligible, imp + jnp.where(forced, FORCE_BONUS, 0.0), -1.0)
        _, sel = lax.top_k(score, n_sel)
        k_sel = ks_blk[bi, gi, sel]
        v_sel = vs_blk[bi, gi, sel]
        pos_s = sel[..., None] * SEL_BLOCK + jnp.arange(SEL_BLOCK)
        rel_s = t[None, None, :, None, None] - pos_s
        bias_s = tbl_gr[gi6, ri6, t5_bucket(rel_s)[:, :, None]]
        ls = jnp.einsum('bgrqd,bgqnkd->bgrqnk', qb, k_sel) * scale + bias_s
        ms = jnp.broadcast_to((rel_s >= 0)[:, :, None], ls.shape)
        ps = masked_softmax(ls.reshape(b, g, r, Q_BLOCK, -1),
                            ms.reshape(b, g, r, Q_BLOCK, -1)).reshape(ls.shape)
        o_s = jnp.einsum('bgrqnk,bgqnkd->bgrqd', ps.astype(v_sel.dtype), v_sel)
        kwb = lax.dynamic_slice_in_dim(kw_pad, q0, span, axis=2)
        vwb = lax.dynamic_slice_in_dim(vw_pad, q0, span, axis=2)
        pos_w = q0 - WINDOW + jnp.arange(span)
        rel_w = t[:, None] - pos_w[None, :]
        mask_w = (rel_w >= 0) & (rel_w < WINDOW) & (pos_w[None, :] >= 0)
        lw = jnp.einsum('bgrqd,bgkd->bgrqk', qb, kwb) * scale + tbl_gr[:, :, t5_bucket(rel_w)]
        pw = masked_softmax(lw, mask_w)
        ow = jnp.einsum('bgrqk,bgkd->bgrqd', pw.astype(vwb.dtype), vwb)
        return (gb[:, 0][..., None] * oc + gb[:, 1][..., None] * o_s
                + gb[:, 2][..., None] * ow)

    out = lax.map(block, jnp.arange(s // Q_BLOCK))
    return out.transpose(1, 0, 4, 2, 3, 5).reshape(b, s, g * r * d)

def diff_attention(q, k, v, lam, lam_init, subln_g, tbl_h):
    b, s = q.shape[:2]
    q = q.transpose(0, 3, 2, 1, 4)
    k = k.transpose(0, 3, 2, 1, 4)
    v = v.transpose(0, 2, 1, 3)
    kpos = jnp.arange(s)
    scale = HEAD_DIM ** -0.5

    def block(j):
        q0 = j * Q_BLOCK
        t = q0 + jnp.arange(Q_BLOCK)
        qb = lax.dynamic_slice_in_dim(q, q0, Q_BLOCK, axis=3)
        rel = t[:, None] - kpos[None, :]
        logits = jnp.einsum('bmhqd,bmhkd->bmhqk', qb, k) * scale + tbl_h[:, t5_bucket(rel)]
        p = masked_softmax(logits, rel >= 0)
        a = p[:, 0] - lam * p[:, 1]
        return jnp.einsum('bhqk,bhkv->bhqv', a.astype(v.dtype), v)

    out = lax.map(block, jnp.arange(s // Q_BLOCK))
    out = out.transpose(1, 0, 3, 2, 4).reshape(b, s, DIFF_HEADS, DIFF_VDIM)
    out = rms_norm(out, subln_g) * (1.0 - lam_init)
    return out.reshape(b, s, DIFF_HEADS * DIFF_VDIM)

def moba_attention(q, k, v, tbl_h):
    b, h, s, d = q.shape
    nb = -(-s // MOBA_BLOCK)
    pad = nb * MOBA_BLOCK - s
    k_pad = jnp.pad(k, ((0, 0), (0, 0), (0, pad), (0, 0)))
    v_pad = jnp.pad(v, ((0, 0), (0, 0), (0, pad), (0, 0)))
    kb = k_pad.reshape(b, h, nb, MOBA_BLOCK, d)
    vb = v_pad.reshape(b, h, nb, MOBA_BLOCK, d)
    k_mean = jnp.mean(kb.astype(jnp.float32), axis=3).astype(k.dtype)
    n_sel = min(MOBA_TOPK, nb)
    scale = d ** -0.5
    bi = jnp.arange(b)[:, None, None, None]
    hi = jnp.arange(h)[None, :, None, None]
    hi5 = jnp.arange(h)[None, :, None, None, None]
    blk_ids = jnp.arange(nb)

    def block(j):
        q0 = j * MOBA_QCHUNK
        t = q0 + jnp.arange(MOBA_QCHUNK)
        c = q0 // MOBA_BLOCK
        qb = lax.dynamic_slice_in_dim(q, q0, MOBA_QCHUNK, axis=2)
        gate = jnp.einsum('bhqd,bhnd->bhqn', qb, k_mean).astype(jnp.float32)
        past = blk_ids < c
        _, sel = lax.top_k(jnp.where(past, gate, NEG), n_sel)
        valid = sel < c
        k_sel = kb[bi, hi, sel]
        v_sel = vb[bi, hi, sel]
        pos_s = sel[..., None] * MOBA_BLOCK + jnp.arange(MOBA_BLOCK)
        bias_s = tbl_h[hi5, t5_bucket(t[None, None, :, None, None] - pos_s)]
        ls = jnp.einsum('bhqd,bhqnkd->bhqnk', qb, k_sel) * scale + bias_s
        ms = jnp.broadcast_to(valid[..., None], ls.shape)
        k_own = lax.dynamic_slice_in_dim(k_pad, c * MOBA_BLOCK, MOBA_BLOCK, axis=2)
        v_own = lax.dynamic_slice_in_dim(v_pad, c * MOBA_BLOCK, MOBA_BLOCK, axis=2)
        rel_o = t[:, None] - (c * MOBA_BLOCK + jnp.arange(MOBA_BLOCK))[None, :]
        lo = jnp.einsum('bhqd,bhkd->bhqk', qb, k_own) * scale + tbl_h[:, t5_bucket(rel_o)]
        mo = jnp.broadcast_to(rel_o >= 0, lo.shape)
        n_g = n_sel * MOBA_BLOCK
        logits = jnp.concatenate([ls.reshape(b, h, MOBA_QCHUNK, n_g), lo], axis=-1)
        mask = jnp.concatenate([ms.reshape(b, h, MOBA_QCHUNK, n_g), mo], axis=-1)
        p = masked_softmax(logits, mask)
        ps = p[..., :n_g].reshape(ls.shape).astype(v.dtype)
        po = p[..., n_g:].astype(v.dtype)
        return (jnp.einsum('bhqnk,bhqnkd->bhqd', ps, v_sel)
                + jnp.einsum('bhqk,bhkd->bhqd', po, v_own))

    out = lax.map(block, jnp.arange(s // MOBA_QCHUNK))
    return out.transpose(1, 0, 3, 2, 4).reshape(b, s, h * d)

def even_mixer(hn, w_in, w_out, pos_k, w1_k, w2_k, pos_v, w1_v, w2_v,
               lam_q1, lam_k1, lam_q2, lam_k2, subln_g, bias_table, lam_init):
    b, s, _ = hn.shape
    parts = jnp.split(hn @ w_in, np.cumsum(EVEN_SIZES)[:-1].tolist(), axis=-1)
    q, kc, vc, ks, vs, kw, vw, g, dq, dk, dv = parts
    qn = to_heads(q, NSA_HEADS).reshape(b, NSA_KV_HEADS, NSA_GROUP, s, HEAD_DIM)
    kc = compress_kv(to_heads(kc, NSA_KV_HEADS), pos_k, w1_k, w2_k)
    vc = compress_kv(to_heads(vc, NSA_KV_HEADS), pos_v, w1_v, w2_v)
    gates = jax.nn.sigmoid(g.astype(jnp.float32)).astype(hn.dtype)
    gates = gates.reshape(b, s, 3, NSA_KV_HEADS, NSA_GROUP).transpose(0, 2, 3, 4, 1)
    o_a = nsa_attention(qn, kc, vc, to_heads(ks, NSA_KV_HEADS), to_heads(vs, NSA_KV_HEADS),
                        to_heads(kw, NSA_KV_HEADS), to_heads(vw, NSA_KV_HEADS), gates,
                        bias_table[:, :NSA_HEADS].T)
    lam = (jnp.exp(jnp.sum((lam_q1 * lam_k1).astype(jnp.float32)))
           - jnp.exp(jnp.sum((lam_q2 * lam_k2).astype(jnp.float32))) + lam_init)
    o_b = diff_attention(dq.reshape(b, s, DIFF_HEADS, 2, HEAD_DIM),
                         dk.reshape(b, s, DIFF_HEADS, 2, HEAD_DIM),
                         dv.reshape(b, s, DIFF_HEADS, DIFF_VDIM), lam, lam_init, subln_g,
                         bias_table[:, NSA_HEADS:NSA_HEADS + DIFF_HEADS].T)
    return jnp.concatenate([o_a, o_b], axis=-1) @ w_out

def odd_mixer(hn, w_in, w_out, bias_table):
    q, k, v = jnp.split(hn @ w_in, 3, axis=-1)
    o = moba_attention(to_heads(q, MOBA_HEADS), to_heads(k, MOBA_HEADS),
                       to_heads(v, MOBA_HEADS), bias_table[:, :MOBA_HEADS].T)
    return o @ w_out

def sqrelu_mlp(hn, w1, w2):
    return jnp.square(jax.nn.relu(hn @ w1)) @ w2

def first_inputs(seed: int = 0) -> dict:
    key = jax.random.key(seed)
    k = jax.random.split(key, 22)
    ne = (DEPTH + 1) // 2
    no = DEPTH // 2
    f32 = jnp.float32

    def nrm(i, shape, scale):
        return jax.random.normal(k[i], shape, f32) * scale

    return {
        'x': nrm(0, (BATCH, SEQ, D_MODEL), 1.0),
        'bias_table': nrm(1, (NUM_BUCKETS, BIAS_HEADS), 0.5),
        'norm_mix': 1.0 + nrm(2, (DEPTH, D_MODEL), 0.1),
        'norm_mlp': 1.0 + nrm(3, (DEPTH, D_MODEL), 0.1),
        'norm_final': 1.0 + nrm(4, (D_MODEL,), 0.1),
        'mlp_w1': nrm(5, (DEPTH, D_MODEL, D_FF), D_MODEL ** -0.5),
        'mlp_w2': nrm(6, (DEPTH, D_FF, D_MODEL), D_FF ** -0.5),
        'ev_w_in': nrm(7, (ne, D_MODEL, EVEN_PROJ), D_MODEL ** -0.5),
        'ev_w_out': nrm(8, (ne, D_MIX, D_MODEL), D_MIX ** -0.5),
        'ev_cmp_pos_k': nrm(9, (ne, CMP_BLOCK, HEAD_DIM), 0.1),
        'ev_cmp_w1_k': nrm(10, (ne, CMP_BLOCK * HEAD_DIM, CMP_HIDDEN), (CMP_BLOCK * HEAD_DIM) ** -0.5),
        'ev_cmp_w2_k': nrm(11, (ne, CMP_HIDDEN, HEAD_DIM), CMP_HIDDEN ** -0.5),
        'ev_cmp_pos_v': nrm(12, (ne, CMP_BLOCK, HEAD_DIM), 0.1),
        'ev_cmp_w1_v': nrm(13, (ne, CMP_BLOCK * HEAD_DIM, CMP_HIDDEN), (CMP_BLOCK * HEAD_DIM) ** -0.5),
        'ev_cmp_w2_v': nrm(14, (ne, CMP_HIDDEN, HEAD_DIM), CMP_HIDDEN ** -0.5),
        'ev_lam_q1': nrm(15, (ne, HEAD_DIM), 0.1),
        'ev_lam_k1': nrm(16, (ne, HEAD_DIM), 0.1),
        'ev_lam_q2': nrm(17, (ne, HEAD_DIM), 0.1),
        'ev_lam_k2': nrm(18, (ne, HEAD_DIM), 0.1),
        'ev_subln': 1.0 + nrm(19, (ne, DIFF_VDIM), 0.1),
        'od_w_in': nrm(20, (no, D_MODEL, ODD_PROJ), D_MODEL ** -0.5),
        'od_w_out': nrm(21, (no, ODD_MIX, D_MODEL), ODD_MIX ** -0.5),
    }

def first_block(x, bias_table, norm_mix, norm_mlp, norm_final, mlp_w1, mlp_w2,
              ev_w_in, ev_w_out, ev_cmp_pos_k, ev_cmp_w1_k, ev_cmp_w2_k,
              ev_cmp_pos_v, ev_cmp_w1_v, ev_cmp_w2_v, ev_lam_q1, ev_lam_k1,
              ev_lam_q2, ev_lam_k2, ev_subln, od_w_in, od_w_out):
    for i in range(DEPTH):
        hn = rms_norm(x, norm_mix[i])
        if i % 2 == 0:
            e = i // 2
            lam_init = 0.8 - 0.6 * math.exp(-0.3 * i)
            mix = even_mixer(hn, ev_w_in[e], ev_w_out[e], ev_cmp_pos_k[e], ev_cmp_w1_k[e],
                             ev_cmp_w2_k[e], ev_cmp_pos_v[e], ev_cmp_w1_v[e], ev_cmp_w2_v[e],
                             ev_lam_q1[e], ev_lam_k1[e], ev_lam_q2[e], ev_lam_k2[e],
                             ev_subln[e], bias_table, lam_init)
        else:
            o = i // 2
            mix = odd_mixer(hn, od_w_in[o], od_w_out[o], bias_table)
        x = x + mix
        x = x + sqrelu_mlp(rms_norm(x, norm_mlp[i]), mlp_w1[i], mlp_w2[i])
    return rms_norm(x, norm_final)


DEPTH_2 = 1

CHUNK = 64
D_RNN = 1280
H_RNN = 16
RNN_BLOCK = D_RNN // H_RNN
CONV_A = 4
LRU_C = 8.0
H_ATT = 16
D_ATT = H_ATT * HEAD_DIM
D_FF_2 = 3 * D_MODEL
CONV_F = 3
N_BRANCH = 2
D_IN = 2 * D_RNN + 3 * D_ATT + H_ATT + N_BRANCH * D_MODEL
RMS_EPS = 1e-6


def rms_norm_2(x, gain):
    xf = x.astype(jnp.float32)
    y = xf * lax.rsqrt(jnp.mean(xf * xf, axis=-1, keepdims=True) + RMS_EPS)
    return (y * gain.astype(jnp.float32)).astype(x.dtype)

def causal_dwconv(x, w, b):
    k_w, c = w.shape
    y = lax.conv_general_dilated(
        x, w[:, None, :].astype(x.dtype), window_strides=(1,), padding=[(k_w - 1, 0)],
        dimension_numbers=("NWC", "WIO", "NWC"), feature_group_count=c)
    return y + b.astype(x.dtype)

def rg_lru(xc, w_a, b_a, w_x, b_x, lam):
    bsz, s, _ = xc.shape
    xb = xc.reshape(bsz, s, H_RNN, RNN_BLOCK)
    r = jax.nn.sigmoid(jnp.einsum("bshi,hij->bshj", xb, w_a).reshape(bsz, s, D_RNN) + b_a)
    i = jax.nn.sigmoid(jnp.einsum("bshi,hij->bshj", xb, w_x).reshape(bsz, s, D_RNN) + b_x)
    log_a = -LRU_C * r.astype(jnp.float32) * jax.nn.softplus(-lam.astype(jnp.float32))
    a = jnp.exp(log_a)
    b_term = jnp.sqrt(-jnp.expm1(2.0 * log_a)) * (i * xc).astype(jnp.float32)

    def combine(left, right):
        a1, h1 = left
        a2, h2 = right
        return a1 * a2, a2 * h1 + h2

    _, h = lax.associative_scan(combine, (a, b_term), axis=1)
    return h.astype(xc.dtype)

def forgetting_attention(q, k, v, f_logit):
    bsz, s, _ = q.shape
    q = q.reshape(bsz, s, H_ATT, HEAD_DIM).transpose(0, 2, 1, 3)
    k = k.reshape(bsz, s, H_ATT, HEAD_DIM).transpose(0, 2, 1, 3)
    v = v.reshape(bsz, s, H_ATT, HEAD_DIM).transpose(0, 2, 1, 3)
    cum = jnp.cumsum(jax.nn.log_sigmoid(f_logit.astype(jnp.float32)), axis=1).transpose(0, 2, 1)
    scale = 1.0 / math.sqrt(HEAD_DIM)
    outs = []
    for blk in range(s // Q_BLOCK):
        qs, qe = blk * Q_BLOCK, (blk + 1) * Q_BLOCK
        sc = jnp.einsum("bhqd,bhkd->bhqk", q[:, :, qs:qe], k[:, :, :qe]).astype(jnp.float32) * scale
        sc = sc + cum[:, :, qs:qe, None] - cum[:, :, None, :qe]
        allowed = jnp.arange(qe)[None, :] <= jnp.arange(qs, qe)[:, None]
        sc = jnp.where(allowed, sc, -jnp.inf)
        p = jax.nn.softmax(sc, axis=-1).astype(v.dtype)
        outs.append(jnp.einsum("bhqk,bhkd->bhqd", p, v[:, :, :qe]))
    o = jnp.concatenate(outs, axis=2)
    return o.transpose(0, 2, 1, 3).reshape(bsz, s, D_ATT)

def second_inputs(seed: int = 0) -> dict:
    key = jax.random.key(seed)
    ks = jax.random.split(key, 24)
    f32 = jnp.float32
    nrm = lambda k, shape, fan_in: jax.random.normal(k, shape, f32) * (fan_in ** -0.5)
    gain = lambda k: 1.0 + 0.05 * jax.random.normal(k, (DEPTH_2, D_MODEL), f32)
    small = lambda k, shape: 0.01 * jax.random.normal(k, shape, f32)
    u = jax.random.uniform(ks[9], (DEPTH_2, D_RNN), f32, 0.9, 0.999)
    a0 = u ** (1.0 / LRU_C)
    lru_lambda = jnp.log(a0) - jnp.log1p(-a0)
    return {
        "x": jax.random.normal(ks[0], (BATCH, SEQ, D_MODEL), f32),
        "mix_norm_pre": gain(ks[1]),
        "mix_norm_post": gain(ks[2]),
        "w_in": nrm(ks[3], (DEPTH_2, D_MODEL, D_IN), D_MODEL),
        "conv_a_w": nrm(ks[4], (DEPTH_2, CONV_A, D_RNN), CONV_A),
        "conv_a_b": small(ks[5], (DEPTH_2, D_RNN)),
        "w_rg_a": nrm(ks[6], (DEPTH_2, H_RNN, RNN_BLOCK, RNN_BLOCK), RNN_BLOCK),
        "b_rg_a": small(ks[7], (DEPTH_2, D_RNN)),
        "w_rg_x": nrm(ks[8], (DEPTH_2, H_RNN, RNN_BLOCK, RNN_BLOCK), RNN_BLOCK),
        "b_rg_x": small(ks[10], (DEPTH_2, D_RNN)),
        "lru_lambda": lru_lambda,
        "b_forget": jax.random.uniform(ks[11], (DEPTH_2, H_ATT), f32, 1.0, 4.0),
        "b_merge": small(ks[12], (DEPTH_2, N_BRANCH, D_MODEL)),
        "w_proj_a": nrm(ks[13], (DEPTH_2, D_RNN, D_MODEL), D_RNN),
        "w_proj_b": nrm(ks[14], (DEPTH_2, D_ATT, D_MODEL), D_ATT),
        "w_out": nrm(ks[15], (DEPTH_2, D_MODEL, D_MODEL), D_MODEL),
        "ffn_norm_pre": gain(ks[16]),
        "ffn_norm_post": gain(ks[17]),
        "w_up": nrm(ks[18], (DEPTH_2, D_MODEL, 2 * D_FF_2), D_MODEL),
        "conv_f_w": nrm(ks[19], (DEPTH_2, CONV_F, 2 * D_FF_2), CONV_F),
        "conv_f_b": small(ks[20], (DEPTH_2, 2 * D_FF_2)),
        "w_down": nrm(ks[21], (DEPTH_2, D_FF_2, D_MODEL), D_FF_2),
    }

def second_block(x, mix_norm_pre, mix_norm_post, w_in, conv_a_w, conv_a_b, w_rg_a, b_rg_a,
              w_rg_x, b_rg_x, lru_lambda, b_forget, b_merge, w_proj_a, w_proj_b, w_out,
              ffn_norm_pre, ffn_norm_post, w_up, conv_f_w, conv_f_b, w_down):
    offs = np.cumsum([D_RNN, D_RNN, D_ATT, D_ATT, D_ATT, H_ATT, D_MODEL]).tolist()
    for layer in range(DEPTH_2):
        h = rms_norm_2(x, mix_norm_pre[layer])
        proj = jnp.einsum("bsd,de->bse", h, w_in[layer])
        xa, ga, q, k, v, f_logit, g_a, g_b = jnp.split(proj, offs, axis=-1)
        xc = causal_dwconv(xa, conv_a_w[layer], conv_a_b[layer])
        hr = rg_lru(xc, w_rg_a[layer], b_rg_a[layer], w_rg_x[layer], b_rg_x[layer], lru_lambda[layer])
        y_a = jax.nn.gelu(ga) * hr
        y_b = forgetting_attention(q, k, v, f_logit + b_forget[layer])
        merged = (jax.nn.sigmoid(g_a + b_merge[layer, 0]) * jnp.einsum("bse,ed->bsd", y_a, w_proj_a[layer])
                  + jax.nn.sigmoid(g_b + b_merge[layer, 1]) * jnp.einsum("bse,ed->bsd", y_b, w_proj_b[layer]))
        mix_out = jnp.einsum("bsd,de->bse", merged, w_out[layer])
        x = x + rms_norm_2(mix_out, mix_norm_post[layer])
        h = rms_norm_2(x, ffn_norm_pre[layer])
        up = jnp.einsum("bsd,df->bsf", h, w_up[layer])
        up = causal_dwconv(up, conv_f_w[layer], conv_f_b[layer])
        gate, val = jnp.split(up, 2, axis=-1)
        ffn_out = jnp.einsum("bsf,fd->bsd", jax.nn.gelu(gate) * val, w_down[layer])
        x = x + rms_norm_2(ffn_out, ffn_norm_post[layer])
    return x


def setup_inputs(seed=0):
    out = dict(first_inputs(seed))
    for name, value in second_inputs(seed + 1).items():
        if name != "x":
            out[name + "_2"] = value
    return out


def reference(
    x, bias_table, norm_mix, norm_mlp, norm_final, mlp_w1, mlp_w2, ev_w_in, ev_w_out,
    ev_cmp_pos_k, ev_cmp_w1_k, ev_cmp_w2_k, ev_cmp_pos_v, ev_cmp_w1_v, ev_cmp_w2_v, ev_lam_q1,
    ev_lam_k1, ev_lam_q2, ev_lam_k2, ev_subln, od_w_in, od_w_out, mix_norm_pre_2,
    mix_norm_post_2, w_in_2, conv_a_w_2, conv_a_b_2, w_rg_a_2, b_rg_a_2, w_rg_x_2, b_rg_x_2,
    lru_lambda_2, b_forget_2, b_merge_2, w_proj_a_2, w_proj_b_2, w_out_2, ffn_norm_pre_2,
    ffn_norm_post_2, w_up_2, conv_f_w_2, conv_f_b_2, w_down_2,
):
    x = first_block(
        x, bias_table, norm_mix, norm_mlp, norm_final, mlp_w1, mlp_w2, ev_w_in, ev_w_out,
        ev_cmp_pos_k, ev_cmp_w1_k, ev_cmp_w2_k, ev_cmp_pos_v, ev_cmp_w1_v, ev_cmp_w2_v,
        ev_lam_q1, ev_lam_k1, ev_lam_q2, ev_lam_k2, ev_subln, od_w_in, od_w_out,
    )
    return second_block(
        x, mix_norm_pre_2, mix_norm_post_2, w_in_2, conv_a_w_2, conv_a_b_2, w_rg_a_2, b_rg_a_2,
        w_rg_x_2, b_rg_x_2, lru_lambda_2, b_forget_2, b_merge_2, w_proj_a_2, w_proj_b_2,
        w_out_2, ffn_norm_pre_2, ffn_norm_post_2, w_up_2, conv_f_w_2, conv_f_b_2, w_down_2,
    )


_drawn_inputs = setup_inputs


def setup_inputs(seed=0):
    import zlib

    import numpy as np

    out = dict(_drawn_inputs(seed))
    spreads = {}
    factors = {'ev_cmp_pos_k': 8.0,
     'conv_a_b_2': 3.462,
     'b_rg_a_2': 55.718,
     'b_rg_x_2': 21.714,
     'b_merge_2': 8.0,
     'conv_f_b_2': 6.736}
    for name, (base, spread) in spreads.items():
        noise = np.random.default_rng([zlib.crc32(name.encode()), seed]).standard_normal(out[name].shape)
        drawn = base * np.exp(spread * noise) if base else spread * noise
        out[name] = jnp.asarray(drawn.astype(out[name].dtype))
    for name, factor in factors.items():
        out[name] = (out[name] * factor).astype(out[name].dtype)
    return out
```

```python
import math
from contextlib import ExitStack

import concourse.bass as bass
from concourse import mybir
import numpy as np

F32 = mybir.dt.float32
F32R = mybir.dt.float32r
ALU = mybir.AluOpType
ACT = mybir.ActivationFunctionType

P = 128
T = 256
TB = T // P
D = 1024
NX = D // P
KS = 8
NS = 256
HD = 64
BIG = 1e30
EPS = 1e-6
NSA_H, DIFF_H, MOBA_H, ATT_H = 8, 4, 16, 16
GATES = 3 * NSA_H
CMP_BLOCK, CMP_STRIDE = 32, 16
NC = (T - CMP_BLOCK) // CMP_STRIDE + 1
NC0 = (P - CMP_BLOCK) // CMP_STRIDE + 1
D_RNN, RNN_BLOCK = 1280, 80
NR = D_RNN // P
CONV_A, CONV_F = 4, 3
D_FF = 4096
NH1 = D_FF // P
D_FF2 = 3072
NH2 = D_FF2 // P
NUM_BUCKETS, MAX_DISTANCE = 32, 128
RING = 4
AHEAD = 3
REL = 384


class Stage:
    s, g = 0, 0

    def __init__(self, slabs, per_group=1):
        self.s0, self.g0, self.n, self.per = Stage.s, Stage.g, slabs, per_group
        Stage.s += slabs
        Stage.g += slabs // per_group


def stages():
    Stage.s = Stage.g = 0
    st = {}
    for name, n, per in (("a_in", 12, 1), ("a_out", 4, 1), ("a_up", 16, 1), ("a_dn", 16, 4),
                         ("m_in", 12, 1), ("m_out", 4, 1), ("m_up", 16, 1), ("m_dn", 16, 4),
                         ("r_xa", 5, 1), ("r_ga", 5, 1), ("r_pa", 8, 2), ("r_gate", 8, 1), ("r_f", 1, 1),
                         ("r_v", 4, 1), ("r_qk", 8, 1), ("r_pb", 4, 1), ("r_out", 4, 1),
                         ("f_up", 24, 1), ("f_dn", 12, 3)):
        st[name] = Stage(n, per)
    return st, Stage.s


PARAMS = {
    "norm_mix": (0, 0, 16), "norm_mlp": (0, 16, 16), "norm_final": (0, 32, 8), "mix_norm_pre_2": (0, 40, 8),
    "mix_norm_post_2": (0, 48, 8), "ffn_norm_pre_2": (0, 56, 8), "ffn_norm_post_2": (0, 64, 8),
    "conv_a_b_2": (0, 72, 10), "b_rg_a_2": (0, 82, 10), "b_rg_x_2": (0, 92, 10), "lru_lambda_2": (0, 102, 10),
    "b_merge_2": (0, 112, 16),
    "conv_a_w_2": (1, 0, 40), "ev_subln": (1, 40, 1), "conv_f_b_2": (1, 41, 48),
    "conv_f_w_2": (2, 0, 128),
    "ev_cmp_pos_k": (3, 0, 16), "ev_cmp_pos_v": (3, 16, 16),
}
CONV_F_TAIL = (3, 32, 16)
TILE_ROWS = (128, 89, 128, 48)


def bucket_rows():
    rel = 255 - np.arange(REL)
    n = np.maximum(rel, 0)
    half = NUM_BUCKETS // 2
    large = half + (np.log(np.maximum(n, 1).astype(np.float32) / np.float32(half))
                    / np.float32(math.log(MAX_DISTANCE / half)) * np.float32(NUM_BUCKETS - half)).astype(np.int32)
    bucket = np.where(n < half, n, np.minimum(large, NUM_BUCKETS - 1))
    return -(bucket[None, :] == np.arange(NUM_BUCKETS)[:, None]).astype(np.float32)


def rg_pieces():
    out = []
    for b in range(D_RNN // RNN_BLOCK):
        row = b * RNN_BLOCK
        end = row + RNN_BLOCK
        while row < end:
            n = min(end, (row // P + 1) * P) - row
            out.append((row // P, row % P, n, b, row - b * RNN_BLOCK))
            row += n
    return out


def rg_inputs(j):
    lo = (j * P) // RNN_BLOCK * RNN_BLOCK
    hi = -(-((j + 1) * P) // RNN_BLOCK) * RNN_BLOCK
    return list(range(lo // P, (hi - 1) // P + 1))


def build(nc, ctx, t, out):
    st, n_slabs = stages()
    pieces = rg_pieces()

    base = 16512
    top = [base]

    def place(name, shape, dt=F32, at=None):
        size = int(np.prod(shape[1:])) * 4
        if at is None:
            at = top[0]
            top[0] = -(-(at + size) // 32) * 32
        return nc.alloc_sbuf_tensor_at(name, shape, dt, offset=at)

    K = 1024
    raw = place("raw", [P, RING, KS, NS])
    w_hi = place("w_hi", [P, RING, KS, NS], F32R)
    w_lo = place("w_lo", [P, RING, KS, NS], F32R)
    x = place("x", [P, NX, T])
    ident = place("ident", [P, P])
    ones = place("ones", [P, P])
    par = place("par", [P, 4, P])
    rs = place("rs", [P, 2, T])
    sd = place("sd", [P, T])
    rs_tok = place("rs_tok", [P, TB])
    nmin = place("nmin", [P, 24 + 2 * DIFF_H, 2])
    psum_ = place("sums", [P, 24 + 2 * DIFF_H, 2])
    fac = place("fac", [P, 24 + 2 * DIFF_H, 2])
    small = place("small", [P, 64])
    fcq = place("f_cum_q", [P, TB, 16])
    fw = place("conv_f", [P, 4, 2 * NH2])
    act_hi = place("act_hi", [P, NX, T], F32R)
    act_lo = place("act_lo", [P, NX, T], F32R)
    tmp0 = top[0]
    arena = tmp0 + 8 * K
    assert arena + 70 * K <= 229344, arena + 70 * K

    def tm(name, shape, at, dt=F32):
        assert at + int(np.prod(shape[1:])) * 4 <= 8 * K
        return place(name, shape, dt, tmp0 + at)

    def ar(name, shape, at, dt=F32):
        assert arena + at + int(np.prod(shape[1:])) * 4 <= 229344, name
        return place(name, shape, dt, arena + int(at))

    sq = tm("sq", [P, NX, T], 0)
    up_r = tm("up_r", [P, 2, 2, T], 0)
    up_q = tm("up_q", [P, 2, 2, T], 4 * K)
    prob = tm("prob", [P, 3, 384], 0)
    prob_t = tm("prob_t", [P, 2, 384], 3 * 1536)
    hid_hi = ar("hid_hi", [P, NH1, T], 0, F32R)
    hid_lo = ar("hid_lo", [P, NH1, T], 32 * K, F32R)
    mix_hi = ar("mix_hi", [P, NX, T], 0, F32R)
    mix_lo = ar("mix_lo", [P, NX, T], 8 * K, F32R)
    cw1 = ar("cmp_w1", [P, 2, 16, P], 0)
    nb = ar("bias", [P, 16, T], 16 * K)
    aq = ar("a_q", [P, 4, T], 32 * K)
    cmp2 = ar("cmp_in", [P, 2, 2, T], 36 * K)
    skw = ar("a_skw", [P, 2, 2, T], 40 * K)
    sv = ar("a_sv", [P, TB, NS], 44 * K)
    dqk = ar("d_qk", [P, 8, T], 46 * K)
    dv = ar("d_v", [P, TB, 4 * P], 54 * K)
    gates = ar("gates", [P, TB, GATES], 58 * K)
    cw2 = ar("cmp_w2", [P, 2, P], 58 * K + 256)
    chid = ar("cmp_hid", [P, 2, 2 * NC], 59 * K + 256)
    kc = ar("kc", [P, 2, NC], 60 * K)
    vc = ar("vc", [P, P], 60 * K + 256)
    dob = ar("d_ob", [P, DIFF_H, T], 61 * K)
    lamv = ar("lam_v", [P, 4, HD], 65 * K)
    xin = ar("x_in", [P, TB, D], 32 * K)
    prow = ar("par_rows", [P, 4, P], 40 * K)
    buck = ar("bucket", [NUM_BUCKETS, REL], 42 * K)
    btab = ar("bias_table", [NUM_BUCKETS, 16], 44 * K)
    brow = ar("bias_row", [16, REL], 66.5 * K)
    dsq = ar("d_sq", [P, DIFF_H, T], 32 * K)
    mqk = ar("m_qk", [P, 16, T], 32 * K)
    mv = ar("m_v", [P, TB, D], 48 * K)
    xap = ar("xa_pad", [P, NR, T + CONV_A - 1], 0)
    rt = ar("rg_t", [P, NR, T], 0)
    xc = ar("xc", [P, NR, T], 10.25 * K)
    hr = ar("h_rnn", [P, NR, T], 10.25 * K)
    gw = ar("rg_w", [P, 2, NR, 3, P], 20.5 * K)
    ra = ar("rg_decay", [P, NR, T], 20.5 * K)
    rix = ar("rg_ix", [P, NR, T], 50.5 * K)
    rr = ar("rg_r1", [P, NR, T], 60.5 * K)
    ya_hi = ar("ya_hi", [P, NR, T], 20.5 * K, F32R)
    ya_lo = ar("ya_lo", [P, NR, T], 30.5 * K, F32R)
    mg = ar("merge", [P, NX, T], 50.5 * K)
    sgb = ar("sig_b", [P, NX, T], 58.5 * K)
    fqk = ar("f_qk", [P, 16, T], 0)
    fv = ar("f_v", [P, TB, D], 16 * K)
    nb2 = ar("f_bias", [P, 16, 384], 26 * K)
    fl = tm("f_logsig", [16, 6, T], 0)
    m2_hi = ar("m2_hi", [P, NX, T], 0, F32R)
    m2_lo = ar("m2_lo", [P, NX, T], 8 * K, F32R)
    mo = ar("mix_out", [P, NX, T], 58.5 * K)
    pt = tm("pair_tmp", [P, 4, 2, T], 0)
    pt2 = ar("post_tmp", [P, 2, 2, T], 66.5 * K)
    h2_hi = ar("h2_hi", [P, NH2, T], 0, F32R)
    h2_lo = ar("h2_lo", [P, NH2, T], 24 * K, F32R)
    upad = ar("up_pad", [P, 2, 2, T + CONV_F - 1], 48 * K)
    ucv = ar("up_conv", [P, 2, 2, T], 52.25 * K)
    xout = ar("x_out", [P, TB, D], 0)

    ps_g = ctx.enter_context(nc.psum_tensor("ps_gemm", [P, 2, 512], F32))
    ps_s = ctx.enter_context(nc.psum_tensor("ps_score", [P, 2, 512], F32))
    ps_t = ctx.enter_context(nc.psum_tensor("ps_trans", [P, 2, 512], F32))
    ps_o = ctx.enter_context(nc.psum_tensor("ps_out", [P, 2, 512], F32))

    def sem(name):
        return ctx.enter_context(nc.semaphore(name))

    raw_in = [sem(f"raw_in{i}") for i in range(RING)]
    hi_done = sem("hi_done")
    w_ready = sem("w_ready")
    slab_done = sem("slab_done")
    emptied = [sem(f"emptied{b}") for b in range(2)]
    ld = {n: sem(f"ld_{n}") for n in ("x", "par", "bias", "cw", "gw", "lam", "bf")}
    idn = sem("idn")
    par_t, par_ok = sem("par_t"), sem("par_ok")
    xt = sem("x_transposed")
    brow_ps, brow_ok, brow_out, nb_in, nb_ok = (sem(n) for n in ("brow_ps", "brow_ok", "brow_out", "nb_in", "nb_ok"))
    xh, xl = sem("act_hi_done"), sem("act_lo_done")
    sq_ok, stat_ok, sd_ok, rs_ok = sem("sq_ok"), sem("stat_ok"), sem("sd_ok"), sem("rs_ok")
    rsq_ok, rst_ps, rst_ok = sem("rsq_ok"), sem("rst_ps"), sem("rst_ok")
    x_new = sem("x_new")
    upr, hid_h, hid_l = sem("up_relu2"), sem("hid_hi_done"), sem("hid_lo_done")
    dve_c, act_c = sem("dve_chain"), sem("act_chain")
    att = [{n: sem(f"at{p}_{n}") for n in ("in", "score", "logit", "prob", "sum", "norm", "tr", "trc", "pv", "oh", "ol")}
           for p in range(3)]
    cmp_ps, cmp_b, cmp_h, cmp_ps2, cmp_ok = (sem(n) for n in ("cmp_ps", "cmp_b", "cmp_h", "cmp_ps2", "cmp_ok"))
    dn = {n: sem(f"dn_{n}") for n in ("o", "sq", "ps", "sd", "r", "o2", "hi", "lo")}
    lam_ok, lam_e = sem("lam_ok"), sem("lam_e")
    gz = sem("gw_zero")
    cva, cvd = sem("conv_a_act"), sem("conv_a_dve")
    rg = {n: sem(f"rg_{n}") for n in ("ps", "sig", "ix", "den", "sq", "a", "b1", "b2", "h")}
    sp_a, sp_d = sem("sp_act"), sem("sp_dve")
    yz, yg, yy, yh, yl = (sem(n) for n in ("ya_z", "ya_gelu", "ya_y", "ya_hi_done", "ya_lo_done"))
    gz2, gs2, gm2 = sem("gate_z"), sem("gate_sig"), sem("gate_m")
    fz, fa, fcum = sem("f_z"), sem("f_act"), sem("f_cum")
    fout, fin_, fcq_ps, fcq_ok, fnb = (sem(n) for n in ("f_cum_out", "f_bias_in", "f_cq_ps", "f_cq_ok", "f_nb"))
    pbm, pbh, pbl = sem("pb_m"), sem("pb_hi"), sem("pb_lo")
    post_t = sem("post_t")
    fuz, fuc, fud, fug, fup, fuh, ful = (sem(n) for n in ("fu_z", "fu_conv1", "fu_conv", "fu_gelu", "fu_prod", "fu_hi", "fu_lo"))
    zero_pad = sem("zero_pad")
    ot, oc, o_out = sem("out_t"), sem("out_c"), sem("out_dma")
    pool_c = sem("pool_chain")

    scr_b = nc.dram_tensor("bias_rows_scr", [16, REL], F32, kind="Internal").ap()
    scr_w = nc.dram_tensor("bias_wide_scr", [P, 16 * REL], F32, kind="Internal").ap()
    scr_c = nc.dram_tensor("cum_scr", [16, T], F32, kind="Internal").ap()

    def col(name, i=0, n=1):
        tile, row, rows = PARAMS[name]
        return par[:, tile, row + i:row + i + n]

    def conv_f_w(j, c):
        r = j * 2 * NH2 + c
        if r < P:
            return par[:, 2, r:r + 1]
        return par[:, CONV_F_TAIL[0], CONV_F_TAIL[1] + r - P:CONV_F_TAIL[1] + r - P + 1]

    eps_c, tiny_c, zero_c, one_c, lamn = (small[:, i:i + 1] for i in range(5))
    sub8 = small[:, 5:6]
    sp4 = small[:, 8:18]
    spw = small[:, 18:58]
    cposb = small[:, 58:60]
    b_f = small[0:16, 60:61]

    def out_count(g):
        return g // 2 + 3

    def x_ready(n, gi):
        if n == 0:
            return emptied[gi % 2], gi // 2 + 1
        if n in (5, 7):
            return x_new, (n - 5) // 2 * 4 + gi + 1
        g = st[{1: "a_out", 2: "a_dn", 3: "m_out", 4: "m_dn", 6: "r_out", 8: "f_dn"}[n]].g0 + gi
        return emptied[g % 2], out_count(g)

    PRE = {0: ("norm_mix", 0), 1: ("norm_mlp", 0), 2: ("norm_mix", 8), 3: ("norm_mlp", 8),
           5: ("mix_norm_pre_2", 0), 7: ("ffn_norm_pre_2", 0)}
    PRE_I = {n: i for i, n in enumerate(PRE)}
    TOK = {0: 0, 2: 1, 5: 2}

    def att_units(p):
        units = []

        def full(q, k, bias, **kw):
            units.append(dict(q=q, k=[k[:, 0:P], k[:, 0:T]],
                              blocks=[(0, P), (P, T)], bias=bias,
                              tiles=[(0, P), (P, P), (2 * P, P)], init=3e38, cmp=False, **kw))

        if p == 0:
            for h in range(NSA_H):
                g, lo = h // 4, (h % 2) * HD
                q = aq[lo:lo + HD, h // 2, :]
                keys = kc[lo:lo + HD, g, :]
                end = CMP_BLOCK - 1
                vg = vc[:, g * HD:(g + 1) * HD]
                units.append(dict(
                    q=q, k=[keys[:, 0:NC0], keys], blocks=[(0, NC0), (P, NC)],
                    bias=[nb[:, h, P + end:P + end + (NC0 - 1) * CMP_STRIDE + 1:CMP_STRIDE],
                          nb[:, h, end:end + (NC - 1) * CMP_STRIDE + 1:CMP_STRIDE]],
                    tiles=[(0, NC0), (P, NC)], init=BIG / 10, cmp=True, gate=h, out=h // 2, rows=(lo, lo + HD),
                    start=True, stop=False, last=False,
                    pv=[(vg[0:NC0, :], NC0, (0, P), (0, P)), (vg[0:NC, :], NC, (P, T), (P, T))]))
                for b in range(2):
                    v = [sv[:, tb, b * P + g * HD:b * P + (g + 1) * HD] for tb in range(TB)]
                    full(q, skw[lo:lo + HD, b, g, :], [nb[:, h, P:T], nb[:, h, :]], gate=8 * (b + 1) + h,
                         out=h // 2, rows=(lo, lo + HD), start=False, stop=(b == 1), last=(b == 1 and h % 2 == 1),
                         pv=[(v[0], P, (0, T), (0, T)), (v[1], P, (T, 384), (P, T))])
            for h in range(DIFF_H):
                for m in range(2):
                    lo = m * HD
                    v = [dv[:, tb, h * P:(h + 1) * P] for tb in range(TB)]
                    full(dqk[lo:lo + HD, h, :], dqk[lo:lo + HD, 4 + h, :],
                         [nb[:, NSA_H + h, P:T], nb[:, NSA_H + h, :]], diff=m, out=4 + h, rows=(0, P),
                         start=True, stop=True, last=True,
                         pv=None if m == 0 else [(v[0], P, (0, T), (0, T)), (v[1], P, (T, 384), (P, T))])
        else:
            qk, vv = (mqk, mv) if p == 1 else (fqk, fv)
            for h in range(16):
                lo = (h % 2) * HD
                v = [vv[:, tb, h * HD:(h + 1) * HD] for tb in range(TB)]
                bias = [nb[:, h, P:T], nb[:, h, :]] if p == 1 else [nb2[:, h, 0:P], nb2[:, h, P:384]]
                full(qk[lo:lo + HD, h // 2, :], qk[lo:lo + HD, 8 + h // 2, :], bias, out=h // 2, rows=(lo, lo + HD),
                     start=True, stop=True, last=(h % 2 == 1),
                     pv=[(v[0], P, (0, T), (0, T)), (v[1], P, (T, 384), (P, T))])
        n = 0
        for i, u in enumerate(units):
            u["i"] = i
            u["n"] = n
            if u["pv"] is not None:
                n += 1
            u["n_done"] = n
        return units

    UNITS = [att_units(p) for p in range(3)]

    def freed_by(units, i):
        u = units[i - 3]
        return u["n_done"] if u["pv"] is not None else None

    def raw_extra(slot, j):
        return 16 * sum(1 for s in (1, 4) if s % RING == slot and s <= j)

    def conv_cols(i, j, c):
        ch = (j % 2) * NH2 + 2 * (j // 2) + c
        tile, row, _ = PARAMS["conv_f_b_2"]
        return fw[:, 2, bass.ds(i * 4 + ch, 1)], fw[:, 3, bass.ds(i * 4 + ch, 1)]

    block = ctx.enter_context(nc.Block())

    @block.sync
    def _(sp):
        def slab(s, j, src, k=KS, n=NS):
            if not (isinstance(s, int) and s < RING):
                sp.wait_ge(w_ready, s - RING + 1)
            dst = raw[:, j % RING, 0:k, 0:n]
            if len(src.shape) == 4:
                dst = dst.rearrange("p k (a b) -> p k a b", a=2)
            sp.dma_start(dst, src).then_inc(raw_in[j % RING], 16)

        def rows(w):
            return w.rearrange("(k p) n -> p k n", p=P)

        w_a = rows(t["ev_w_in"][0])

        def a_slab(j):
            s = st["a_in"].s0 + j
            if j in (1, 4):
                c0 = 768 if j == 1 else 896
                for half in range(2):
                    if half == 0 and s >= RING:
                        sp.wait_ge(w_ready, s - RING + 1)
                    sp.dma_start(raw[:, s % RING, :, half * P:(half + 1) * P],
                                 w_a[:, :, c0 + half * 2 * P:c0 + half * 2 * P + P]).then_inc(raw_in[s % RING], 8 * 2)
                return
            c0 = {0: 512, 2: 0, 3: 256, 5: 1280, 6: 1304, 7: 1560, 8: 1816, 9: 2072, 10: 2328, 11: 2584}[j]
            n = GATES if j == 5 else NS
            slab(s, s, w_a[:, :, c0:c0 + n], n=n)

        sp.dma_start(xin[:, 0, :], t["x"][0, 0:P, :]).then_inc(ld["x"], 16)
        sp.dma_start(xin[:, 1, :], t["x"][0, P:T, :]).then_inc(ld["x"], 16)
        for name, (tile, row, n) in PARAMS.items():
            src = t[name]
            src = src.rearrange(" ".join("abcd"[:len(src.shape)]) + " -> (" + " ".join("abcd"[:len(src.shape)]) + ")") \
                if len(src.shape) > 1 else src
            src = src[0:n * P].rearrange("(r c) -> r c", c=P)
            sp.dma_start(prow[row:row + n, tile, :], src).then_inc(ld["par"], 16)
        tail = t["conv_f_w_2"].rearrange("a b c -> (a b c)")[P * P:144 * P].rearrange("(r c) -> r c", c=P)
        sp.dma_start(prow[CONV_F_TAIL[1]:CONV_F_TAIL[1] + 16, CONV_F_TAIL[0], :], tail).then_inc(ld["par"], 16)
        for j in range(RING):
            a_slab(j)
        sp.dma_start(buck[:, :], t["bucket"]).then_inc(ld["bias"], 16)
        sp.dma_start(btab[:, :], t["bias_table"]).then_inc(ld["bias"], 16)
        for i, name in enumerate(("ev_lam_q1", "ev_lam_k1", "ev_lam_q2", "ev_lam_k2")):
            sp.dma_start(lamv[:, i, :], t[name].to_broadcast([P, HD])).then_inc(ld["lam"], 16)
        for i, name in enumerate(("k", "v")):
            sp.dma_start(cw1[:, i, :, :], t[f"ev_cmp_w1_{name}"][0].rearrange("(m p) j -> p m j", p=P)).then_inc(ld["cw"], 16)
            for half in range(2):
                sp.dma_start(cw2[:, i, half * HD:(half + 1) * HD], t[f"ev_cmp_w2_{name}"][0]).then_inc(ld["cw"], 16)
        sp.dma_start(b_f, t["b_forget_2"].rearrange("a h -> h a"),).then_inc(ld["bf"], 16)
        sp.wait_ge(brow_ok, 1)
        sp.dma_start(scr_b, brow[:, :]).then_inc(brow_out, 16)
        sp.wait_ge(brow_out, 16)
        sp.dma_start(scr_w, bass.AP(tensor=scr_b.tensor, offset=0, ap=[[0, P], [1, 16 * REL]])).then_inc(brow_out, 16)
        sp.wait_ge(brow_out, 32)
        toeplitz = bass.AP(tensor=scr_w.tensor, offset=P - 1, ap=[[16 * REL - 1, P], [REL, 16], [1, T]])
        sp.dma_start(nb[:, :, :], toeplitz).then_inc(nb_in, 16)
        for j in range(RING, 12):
            a_slab(j)

        def cols(name, w, n, body):
            s0 = st[name].s0
            with sp.Fori(0, n // body) as i:
                for j in range(body):
                    slab(s0 + i * body + j, s0 + j, w[:, :, bass.ds(i * (body * NS) + j * NS, NS)])

        def groups(name, w, per, k, body):
            s0, n = st[name].s0, st[name].n
            with sp.Fori(0, n // body) as i:
                for j in range(body):
                    g, r = j // per, j % per
                    slab(s0 + i * body + j, s0 + j,
                         w[:, r * k:(r + 1) * k, bass.ds(i * (body // per * NS) + g * NS, NS)], k=k)

        for l, (pre, wi, wo) in enumerate((("a", None, "ev_w_out"), ("m", "od_w_in", "od_w_out"))):
            if wi:
                cols(pre + "_in", rows(t[wi][0]), 12, 4)
                sp.wait_ge(slab_done, st["m_in"].s0)
                sp.dma_start(nb[:, :, :], toeplitz).then_inc(nb_in, 16)
            for j in range(4):
                s = st[pre + "_out"].s0 + j
                slab(s, s, rows(t[wo][0])[:, :, j * NS:(j + 1) * NS])
            cols(pre + "_up", rows(t["mlp_w1"][l]), 16, 4)
            groups(pre + "_dn", rows(t["mlp_w2"][l]), 4, KS, 8)
        w_r = rows(t["w_in_2"][0])
        for j in range(5):
            s = st["r_xa"].s0 + j
            slab(s, s, w_r[:, :, j * NS:(j + 1) * NS])
        sp.wait_ge(gz, 1)
        for i, name in enumerate(("w_rg_a_2", "w_rg_x_2")):
            for (c, r, n, b, r0) in pieces:
                first = b * RNN_BLOCK - (c - 1) * P
                sp.dma_start(gw[r:r + n, i, c, :, :].rearrange("p a b -> p (a b)")[:, first:first + RNN_BLOCK],
                             t[name][0, b, r0:r0 + n, :]).then_inc(ld["gw"], 16)
        for j in range(5):
            s = st["r_ga"].s0 + j
            slab(s, s, w_r[:, :, D_RNN + j * NS:D_RNN + (j + 1) * NS])
        groups("r_pa", rows(t["w_proj_a_2"][0]), 2, NR // 2, 8)
        QKV = 2 * D_RNN
        GA = QKV + 3 * D + ATT_H
        for j in range(8):
            s = st["r_gate"].s0 + j
            slab(s, s, w_r[:, :, GA + j * NS:GA + (j + 1) * NS])
        s = st["r_f"].s0
        slab(s, s, w_r[:, :, QKV + 3 * D:GA], n=ATT_H)
        for j in range(4):
            s = st["r_v"].s0 + j
            slab(s, s, w_r[:, :, QKV + 2 * D + j * NS:QKV + 2 * D + (j + 1) * NS])
        sp.wait_ge(fcum, 1)
        sp.dma_start(scr_c, fl[:, 5, :]).then_inc(fout, 16)
        sp.wait_ge(fout, 16)
        bc = scr_c.rearrange("h k -> (h k)")
        for c0, n in ((0, P), (P, T)):
            sp.dma_start(nb2[:, :, c0:c0 + n], bass.AP(tensor=scr_c.tensor, offset=0, ap=[[0, P], [T, 16], [1, n]]))\
                .then_inc(fin_, 16)
        cols("r_qk", w_r[:, :, QKV:QKV + 2 * D], 8, 4)
        for name, w in (("r_pb", "w_proj_b_2"), ("r_out", "w_out_2")):
            for j in range(4):
                s = st[name].s0 + j
                slab(s, s, rows(t[w][0])[:, :, j * NS:(j + 1) * NS])
        w_u = rows(t["w_up_2"][0]).rearrange("p k (v n) -> p k v n", v=2)
        with sp.Fori(0, 6) as i:
            for j in range(4):
                slab(st["f_up"].s0 + i * 4 + j, st["f_up"].s0 + j,
                     w_u[:, :, j % 2, bass.ds(i * 2 * NS + j // 2 * NS, NS)])
        groups("f_dn", rows(t["w_down_2"][0]), 3, KS, 12)
        for tb in range(TB):
            sp.wait_ge(oc, 2 * tb + 2)
            sp.dma_start(out[0, tb * P:(tb + 1) * P, :], xout[:, tb, :]).then_inc(o_out, 16)
        sp.wait_ge(o_out, 32)

    @block.gpsimd
    def _(pool):
        pool.memset(ident[:, :], 0.0).then_inc(pool_c, 1)
        pool.memset(ones[:, :], 1.0).then_inc(idn, 1)
        pool.wait_ge(pool_c, 1)
        pool.affine_select(out=ident[:, :], in_=ident[:, :], compare_op=ALU.not_equal, fill=1.0, base=0,
                           pattern=[[-1, P]], channel_multiplier=1).then_inc(idn, 1)

        def squares(n, src=x):
            if n:
                pool.wait_ge(stat_ok, n)
            for gi in range(4):
                pool.wait_ge(*x_ready(n, gi))
                pool.tensor_tensor(sq[:, 2 * gi:2 * gi + 2, :], src[:, 2 * gi:2 * gi + 2, :],
                                   src[:, 2 * gi:2 * gi + 2, :], ALU.mult).then_inc(sq_ok, 1)

        squares(0)
        pool.wait_ge(nb_in, 16)
        pool.affine_select(out=nb[:, :, P:T], in_=nb[:, :, P:T], compare_op=ALU.is_ge, fill=BIG, base=0,
                           pattern=[[0, 16], [-1, P]], channel_multiplier=1).then_inc(nb_ok, 1)
        squares(1)
        squares(2)
        pool.wait_ge(nb_in, 32)
        pool.affine_select(out=nb[:, :, P:T], in_=nb[:, :, P:T], compare_op=ALU.is_ge, fill=BIG, base=0,
                           pattern=[[0, 16], [-1, P]], channel_multiplier=1).then_inc(nb_ok, 1)
        squares(3)
        squares(4)
        squares(5)
        pool.wait_ge(slab_done, st["m_dn"].s0 + st["m_dn"].n)
        for i in range(2):
            ins = pool.memset(gw[:, i, :, :, :], 0.0)
        ins.then_inc(gz, 1)
        pool.memset(xap[:, :, 0:CONV_A - 1], 0.0).then_inc(zero_pad, 1)
        for j in range(NR):
            pool.wait_ge(rg["sig"], j + 1)
            pool.tensor_tensor(rix[:, j, :], rix[:, j, :], xc[:, j, :], ALU.mult).then_inc(rg["ix"], 1)
        pool.wait_ge(rg["sq"], 1)
        pool.tensor_tensor(rt[:, :, :], rt[:, :, :], rr[:, :, :], ALU.mult).then_inc(rg["b1"], 1)
        pool.wait_ge(rg["b1"], 1)
        pool.tensor_tensor(rt[:, :, :], rt[:, :, :], rix[:, :, :], ALU.mult).then_inc(rg["b2"], 1)
        pool.wait_ge(fin_, 32)
        pool.wait_ge(fcq_ok, 1)
        pool.tensor_tensor(nb2[:, :, 0:P], nb2[:, :, 0:P], fcq[:, 0, :].unsqueeze(2).to_broadcast([P, 16, P]),
                           ALU.subtract).then_inc(pool_c, 1)
        pool.tensor_tensor(nb2[:, :, P:384], nb2[:, :, P:384], fcq[:, 1, :].unsqueeze(2).to_broadcast([P, 16, T]),
                           ALU.subtract).then_inc(pool_c, 1)
        pool.wait_ge(pool_c, 3)
        for c0 in (0, T):
            pool.affine_select(out=nb2[:, :, c0:c0 + P], in_=nb2[:, :, c0:c0 + P], compare_op=ALU.is_ge, fill=BIG,
                               base=0, pattern=[[0, 16], [-1, P]], channel_multiplier=1).then_inc(fnb, 1)
        squares(6, mo)
        pool.wait_ge(slab_done, st["r_out"].s0 + 4)
        pool.memset(upad[:, :, :, 0:CONV_F - 1], 0.0).then_inc(zero_pad, 1)
        squares(7)
        squares(8, mo)

    @block.scalar
    def _(act):
        def split_hi(s, j):
            if isinstance(s, int) and s >= n_slabs:
                return
            slot = j % RING
            extra = raw_extra(slot, j)
            act.wait_ge(raw_in[slot], (s - j + (j // RING + 1) * RING) * (16 // RING) + extra)
            if not (isinstance(s, int) and s < RING):
                act.wait_ge(slab_done, s - RING + 1)
            act.activation(w_hi[:, slot, :, :], raw[:, slot, :, :], ACT.Copy).then_inc(hi_done, 1)

        def split_x(n):
            name, c0 = PRE[n]
            for gi in range(4):
                act.wait_ge(*x_ready(n, gi))
                for c in (2 * gi, 2 * gi + 1):
                    ins = act.activation(act_hi[:, c, :], x[:, c, :], ACT.Copy, scale=col(name, c0 + c))
                ins.then_inc(xh, 1)

        def root(n):
            act.wait_ge(stat_ok, n + 1)
            act.activation(sd[:, :], ps_s[:, 0, 0:T], ACT.Sqrt, scale=1.0 / D, bias=eps_c).then_inc(sd_ok, 1)

        def tok(s, g, dst, func=ACT.Copy, n=NS):
            act.wait_ge(slab_done, s + 1)
            for tb in range(TB):
                ins = act.activation(dst[:, tb, :], ps_g[:, g % 2, tb * NS:tb * NS + n], func, scale=rs_tok[:, tb:tb + 1])
            ins.then_inc(emptied[g % 2], 1)

        def attention(p, after=None):
            a, units = att[p], UNITS[p]
            n_units = len(units)
            pairs = 0
            for i in range(n_units + 2):
                if i < n_units:
                    u = units[i]
                    act.wait_ge(a["logit"], i + 1)
                    for b, (c0, n) in enumerate(u["blocks"]):
                        ins = act.activation(prob[:, i % 3, c0:c0 + n], prob[:, i % 3, c0:c0 + n], ACT.Exp, scale=-1.0,
                                             bias=nmin[:, i, b:b + 1], accum_out=psum_[:, i, b:b + 1])
                    ins.then_inc(a["prob"], 1)
                if 1 <= i <= n_units:
                    u = units[i - 1]
                    if u["pv"] is not None:
                        n = u["n"]
                        act.wait_ge(a["tr"], n + 1)
                        if n >= 2:
                            act.wait_ge(a["pv"], n - 1)
                        r = max(k for _, k in u["tiles"])
                        if u["cmp"]:
                            act.activation(prob_t[0:NC0, n % 2, 0:P], ps_t[0:NC0, n % 2, 0:P], ACT.Copy)
                            act.activation(prob_t[0:NC, n % 2, P:T], ps_t[0:NC, n % 2, P:T], ACT.Copy).then_inc(a["trc"], 1)
                        else:
                            act.activation(prob_t[:, n % 2, :], ps_t[:, n % 2, 0:384], ACT.Copy).then_inc(a["trc"], 1)
                if i >= 2:
                    u = units[i - 2]
                    if u["pv"] is not None and u["last"]:
                        act.wait_ge(a["pv"], u["n"] + 1)
                        o = u["out"]
                        if "diff" in u:
                            act.activation(dob[:, o - 4, :], ps_o[:, o % 2, 0:T], ACT.Copy).then_inc(a["oh"], 1)
                        else:
                            hi = (mix_hi if p < 2 else act_hi)
                            act.activation(hi[:, o, :], ps_o[:, o % 2, 0:T], ACT.Copy).then_inc(a["oh"], 1)

        for s in range(AHEAD):
            split_hi(s, s)
        act.wait_ge(par_ok, 1)
        split_x(0)
        root(0)
        for s in range(12):
            split_hi(s + AHEAD, s + AHEAD)
            g = st["a_in"].g0 + s
            if s in (4, 5, 10, 11):
                if s == 4:
                    act.wait_ge(rst_ok, 1)
                dst = {4: sv[:, :, :], 5: gates[:, :, :], 10: dv[:, :, 0:NS], 11: dv[:, :, NS:2 * NS]}[s]
                tok(s, g, dst, ACT.Sigmoid if s == 5 else ACT.Copy, GATES if s == 5 else NS)
        act.wait_ge(lam_ok, 1)
        act.activation(small[:, 6:8], small[:, 6:8], ACT.Exp).then_inc(lam_e, 1)
        act.wait_ge(cmp_b, 1)
        for i in range(2):
            ins = act.activation(chid[:, i, :], ps_s[:, i, 0:2 * NC], ACT.Gelu_apprx_tanh, bias=cposb[:, i:i + 1])
        ins.then_inc(cmp_h, 1)
        attention(0)
        act.wait_ge(att[0]["oh"], 8)
        act.activation(dsq[:, :, :], dob[:, :, :], ACT.Square).then_inc(dn["sq"], 1)
        act.wait_ge(dn["ps"], 1)
        act.activation(dsq[:, :, :].rearrange("p (a b) n -> p a (b n)", a=2), ps_o[:, :, :], ACT.Sqrt, scale=1.0 / P, bias=eps_c).then_inc(dn["sd"], 1)
        act.wait_ge(dn["o2"], 1)
        act.activation(mix_hi[:, 4:8, :], dob[:, :, :], ACT.Copy).then_inc(dn["hi"], 1)

        def out_stage(name, n):
            for j in range(4):
                s = st[name].s0 + j
                split_hi(s + AHEAD, s + AHEAD)
            split_x(n)

        def mlp_up(name, n):
            root(n)
            s0, g0 = st[name].s0, st[name].g0
            with act.Fori(0, 4) as i:
                for j in range(4):
                    split_hi(s0 + i * 4 + j + AHEAD, s0 + j + AHEAD)
                    g = g0 + j
                    act.wait_ge(emptied[g % 2], out_count(g) + i * 2)
                    act.activation(hid_hi[:, bass.ds(i * 8 + j * 2, 2), :], up_r[:, j % 2, :, :], ACT.Square)\
                        .then_inc(hid_h, 1)

        def mlp_dn(name, n):
            s0 = st[name].s0
            with act.Fori(0, 2) as i:
                for j in range(8):
                    split_hi(s0 + i * 8 + j + AHEAD, s0 + j + AHEAD)
            if n in PRE:
                split_x(n)

        out_stage("a_out", 1)
        mlp_up("a_up", 1)
        mlp_dn("a_dn", 2)
        root(2)
        with act.Fori(0, 2) as i:
            for j in range(4):
                split_hi(st["m_in"].s0 + i * 4 + j + AHEAD, st["m_in"].s0 + j + AHEAD)
        act.wait_ge(rst_ok, 2)
        for j in range(4):
            s = st["m_in"].s0 + 8 + j
            split_hi(s + AHEAD, s + AHEAD)
            tok(s, st["m_in"].g0 + 8 + j, mv[:, :, j * NS:(j + 1) * NS])
        attention(1)
        out_stage("m_out", 3)
        mlp_up("m_up", 3)
        mlp_dn("m_dn", 4)
        root(4)
        split_x(5)
        root(5)
        act.wait_ge(sp_d, 1)
        act.activation(spw[:, 0:10], spw[:, 0:10], ACT.Exp).then_inc(sp_a, 1)
        for j in range(5):
            s = st["r_xa"].s0 + j
            split_hi(s + AHEAD, s + AHEAD)
            act.wait_ge(emptied[(st["r_xa"].g0 + j) % 2], out_count(st["r_xa"].g0 + j))
            for c in (2 * j, 2 * j + 1):
                ins = act.activation(xc[:, c, :], xap[:, c, CONV_A - 1:], ACT.Identity,
                                     scale=col("conv_a_w_2", (CONV_A - 1) * NR + c), bias=col("conv_a_b_2", c))
            ins.then_inc(cva, 1)
        act.wait_ge(sp_d, 2)
        for j in range(NR):
            act.wait_ge(rg["ps"], j + 1)
            act.activation(rt[:, j, :], ps_s[:, j % 2, 0:T], ACT.Sigmoid, bias=col("b_rg_a_2", j)).then_inc(act_c, 1)
            act.activation(rix[:, j, :], ps_s[:, j % 2, T:2 * T], ACT.Sigmoid, bias=col("b_rg_x_2", j)).then_inc(rg["sig"], 1)
            act.wait_ge(act_c, j + 1)
            act.activation(rt[:, j, :], rt[:, j, :], ACT.Tanh, scale=sp4[:, j:j + 1]).then_inc(rg["den"], 1)
        act.wait_ge(rg["a"], 1)
        act.activation(rt[:, :, :], rt[:, :, :], ACT.Sqrt, scale=4.0).then_inc(rg["sq"], 1)
        for j in range(5):
            s = st["r_ga"].s0 + j
            split_hi(s + AHEAD, s + AHEAD)
            g = st["r_ga"].g0 + j
            act.wait_ge(emptied[g % 2], out_count(g))
            act.activation(pt[:, j % 2, :, :], pt[:, j % 2, :, :], ACT.Gelu_apprx_tanh).then_inc(yg, 1)
            act.wait_ge(yy, j + 1)
            act.activation(ya_hi[:, 2 * j:2 * j + 2, :], pt[:, 2 + j % 2, :, :], ACT.Copy).then_inc(yh, 1)
        with act.Fori(0, 1) as i:
            for j in range(8):
                split_hi(st["r_pa"].s0 + j + AHEAD, st["r_pa"].s0 + j + AHEAD)
        for j in range(8):
            s = st["r_gate"].s0 + j
            split_hi(s + AHEAD, s + AHEAD)
            g = st["r_gate"].g0 + j
            act.wait_ge(emptied[g % 2], out_count(g))
            for c in (0, 1):
                dst = pt[:, j % 2, c, :] if j < 4 else sgb[:, 2 * (j - 4) + c, :]
                ins = act.activation(dst, pt[:, j % 2, c, :], ACT.Sigmoid, bias=col("b_merge_2", 2 * j + c))
            ins.then_inc(gs2, 1)
        split_hi(st["r_f"].s0 + AHEAD, st["r_f"].s0 + AHEAD)
        act.wait_ge(fz, 1)
        act.wait_ge(ld["bf"], 16)
        act.activation(fl[:, 1, :], fl[:, 0, :], ACT.Identity, bias=b_f).then_inc(fa, 1)
        act.wait_ge(fz, 2)
        act.activation(fl[:, 3, :], fl[:, 3, :], ACT.Exp).then_inc(fa, 1)
        act.wait_ge(fa, 2)
        act.activation(fl[:, 4, :], fl[:, 3, :], ACT.Ln, bias=one_c[0:16, :]).then_inc(fa, 1)
        for j in range(4):
            s = st["r_v"].s0 + j
            split_hi(s + AHEAD, s + AHEAD)
            tok(s, st["r_v"].g0 + j, fv[:, :, j * NS:(j + 1) * NS])
        with act.Fori(0, 2) as i:
            for j in range(4):
                split_hi(st["r_qk"].s0 + i * 4 + j + AHEAD, st["r_qk"].s0 + j + AHEAD)
        attention(2)
        for j in range(4):
            s = st["r_pb"].s0 + j
            split_hi(s + AHEAD, s + AHEAD)
            g = st["r_pb"].g0 + j
            act.wait_ge(emptied[g % 2], out_count(g))
            act.activation(m2_hi[:, 2 * j:2 * j + 2, :], mg[:, 2 * j:2 * j + 2, :], ACT.Copy).then_inc(pbh, 1)
        for j in range(4):
            s = st["r_out"].s0 + j
            split_hi(s + AHEAD, s + AHEAD)
        root(6)
        split_x(7)
        root(7)
        s0, g0 = st["f_up"].s0, st["f_up"].g0
        with act.Fori(0, 6) as i:
            for j in range(4):
                split_hi(s0 + i * 4 + j + AHEAD, s0 + j + AHEAD)
                g = g0 + j
                act.wait_ge(emptied[g % 2], out_count(g) + i * 2)
                for c in range(2):
                    wcol, bcol = conv_cols(i, j, c)
                    ins = act.activation(ucv[:, j % 2, c, :], upad[:, j % 2, c, CONV_F - 1:], ACT.Identity,
                                         scale=wcol, bias=bcol)
                ins.then_inc(fuc, 1)
                if j % 2 == 0:
                    act.wait_ge(fud, i * 16 + j * 4 + 4)
                    act.activation(ucv[:, 0, :, :], ucv[:, 0, :, :], ACT.Gelu_apprx_tanh).then_inc(fug, 1)
                else:
                    act.wait_ge(fup, i * 2 + j // 2 + 1)
                    act.activation(h2_hi[:, bass.ds(i * 4 + (j // 2) * 2, 2), :], ucv[:, 1, :, :], ACT.Copy).then_inc(fuh, 1)
        for j in range(12):
            split_hi(st["f_dn"].s0 + j + AHEAD, st["f_dn"].s0 + j + AHEAD)
        root(8)
        for q in range(4):
            act.wait_ge(ot, q + 1)
            act.activation(xout[:, q // 2, (q % 2) * 512:(q % 2) * 512 + 512], ps_g[:, q % 2, :], ACT.Copy).then_inc(oc, 1)

    @block.vector
    def _(dve):
        chain = [0]

        def link(ins):
            chain[0] += 1
            ins.then_inc(dve_c, 1)
            dve.wait_ge(dve_c, chain[0])

        def split_lo(s, j):
            if isinstance(s, int) and s >= n_slabs:
                return
            slot = j % RING
            dve.wait_ge(hi_done, s + 1)
            dve.tensor_tensor(w_lo[:, slot, :, :], raw[:, slot, :, :], w_hi[:, slot, :, :].bitcast(F32), ALU.subtract)\
                .then_inc(w_ready, 1)

        def split_x(n):
            name, c0 = PRE[n]
            for gi in range(4):
                dve.wait_ge(xh, PRE_I[n] * 4 + gi + 1)
                for c in (2 * gi, 2 * gi + 1):
                    ins = dve.scalar_tensor_tensor(out=act_lo[:, c, :], in0=x[:, c, :], scalar=col(name, c0 + c),
                                                   in1=act_hi[:, c, :].bitcast(F32), op0=ALU.mult, op1=ALU.subtract)
                ins.then_inc(xl, 1)

        def inv_rms(n):
            dve.wait_ge(sd_ok, n + 1)
            dve.reciprocal(rs[:, 1, :], sd[:, :]).then_inc(rs_ok, 1)
            dve.wait_ge(rs_ok, n + 1)
            if n in TOK:
                dve.tensor_scalar(rs[:, 0, :], rs[:, 1, :], -0.125, None, ALU.mult).then_inc(rsq_ok, 1)
                dve.wait_ge(rst_ps, TOK[n] + 1)
                dve.tensor_copy(rs_tok[:, :], ps_s[:, 1, 0:TB]).then_inc(rst_ok, 1)
                dve.wait_ge(rsq_ok, TOK[n] + 1)

        def bcast(ap, n=2):
            return ap.unsqueeze(1).to_broadcast([P, n, T])

        def pair(g):
            return ps_g[:, g % 2, :].rearrange("p (a n) -> p a n", a=2)

        def attention(p):
            a, units = att[p], UNITS[p]
            n_units = len(units)
            for i in range(n_units + 2):
                if i < n_units:
                    u = units[i]
                    dve.wait_ge(a["score"], i + 1)
                    if i >= 3 and freed_by(units, i):
                        dve.wait_ge(a["tr"], freed_by(units, i))
                    if p == 0 and i == 0:
                        dve.wait_ge(nb_ok, 1)
                    for b, (c0, n) in enumerate(u["blocks"]):
                        ins = dve.tensor_tensor_reduce(
                            out=prob[:, i % 3, c0:c0 + n], in0=ps_s[:, i % 2, c0:c0 + n], in1=u["bias"][b],
                            scale=1.0, scalar=u["init"], op0=ALU.add, op1=ALU.min, accum_out=nmin[:, i, b:b + 1])
                    ins.then_inc(a["logit"], 1)
                if 1 <= i <= n_units:
                    k = i - 1
                    u = units[k]
                    dve.wait_ge(a["prob"], k + 1)
                    if u["cmp"]:
                        link(dve.tensor_scalar(psum_[:, k, :], psum_[:, k, :], 1e-30, None, ALU.max))
                    link(dve.reciprocal(fac[:, k, :], psum_[:, k, :]))
                    if "gate" in u:
                        link(dve.tensor_tensor(fac[:, k, :], fac[:, k, :], gates[:, :, u["gate"]], ALU.mult))
                    if u.get("diff") == 1:
                        link(dve.tensor_scalar(fac[:, k, :], fac[:, k, :], lamn, None, ALU.mult))
                    for b, (c0, n) in enumerate(u["blocks"]):
                        if u.get("diff") == 1:
                            ins = dve.scalar_tensor_tensor(
                                out=prob[:, k % 3, c0:c0 + n], in0=prob[:, k % 3, c0:c0 + n], scalar=fac[:, k, b:b + 1],
                                in1=prob[:, (k - 1) % 3, c0:c0 + n], op0=ALU.mult, op1=ALU.add)
                        else:
                            ins = dve.tensor_scalar(prob[:, k % 3, c0:c0 + n], prob[:, k % 3, c0:c0 + n],
                                                    fac[:, k, b:b + 1], None, ALU.mult)
                    if u.get("diff") == 0:
                        link(ins)
                    else:
                        ins.then_inc(a["norm"], 1)
                if i >= 2:
                    u = units[i - 2]
                    if u["pv"] is not None and u["last"] and "diff" not in u:
                        o = u["out"]
                        hi, lo = (mix_hi, mix_lo) if p < 2 else (act_hi, act_lo)
                        dve.wait_ge(a["oh"], o + 1)
                        dve.tensor_tensor(lo[:, o, :], ps_o[:, o % 2, 0:T], hi[:, o, :].bitcast(F32), ALU.subtract)\
                            .then_inc(a["ol"], 1)

        dve.memset(eps_c, EPS)
        dve.memset(one_c, 1.0)
        link(dve.memset(zero_c, 0.0))
        dve.wait_ge(par_t, 1)
        for k in range(4):
            ins = dve.tensor_copy(par[:, k, 0:TILE_ROWS[k]], ps_t[:, 0, k * P:k * P + TILE_ROWS[k]])
        ins.then_inc(par_ok, 1)
        dve.wait_ge(par_ok, 1)
        for gi in range(4):
            dve.wait_ge(xt, gi + 1)
            dve.tensor_copy(x[:, 2 * gi:2 * gi + 2, :], pair(gi)).then_inc(emptied[gi % 2], 1)
        for j in range(CONV_F):
            for c0, c1 in ((0, 2 * NH2),):
                r = j * 2 * NH2
                if r + 2 * NH2 <= P:
                    dve.tensor_copy(fw[:, j, :], par[:, 2, r:r + 2 * NH2])
                else:
                    n = P - r
                    dve.tensor_copy(fw[:, j, 0:n], par[:, 2, r:P])
                    dve.tensor_copy(fw[:, j, n:], par[:, CONV_F_TAIL[0], CONV_F_TAIL[1]:CONV_F_TAIL[1] + 16])
        link(dve.tensor_copy(fw[:, 3, :], col("conv_f_b_2", 0, 2 * NH2)))
        for s in range(AHEAD - 1):
            split_lo(s, s)
        split_x(0)
        dve.wait_ge(ld["lam"], 64)
        for i in range(2):
            ins = dve.tensor_tensor_reduce(out=lamv[:, 2 * i, :], in0=lamv[:, 2 * i, :], in1=lamv[:, 2 * i + 1, :],
                                           scale=1.0, scalar=0.0, op0=ALU.mult, op1=ALU.add,
                                           accum_out=small[:, 6 + i:7 + i])
        ins.then_inc(lam_ok, 1)
        dve.tensor_scalar(sub8, col("ev_subln"), 1.0 - 0.2, None, ALU.mult)
        dve.wait_ge(brow_ps, 1)
        dve.tensor_copy(brow[:, :], ps_o[0:16, 0, 0:REL]).then_inc(brow_ok, 1)
        inv_rms(0)
        q_pair = bcast(rs[:, 0, :])
        k_pair = bcast(rs[:, 1, :])
        for s in range(12):
            split_lo(s + AHEAD - 1, s + AHEAD - 1)
            g = st["a_in"].g0 + s
            if s in (4, 5, 10, 11):
                continue
            dve.wait_ge(slab_done, s + 1)
            if s == 0:
                for i in range(2):
                    for gg in range(2):
                        rws = slice(gg * HD, (gg + 1) * HD)
                        dve.tensor_tensor(cmp2[0:HD, i, gg, :], ps_g[rws, g % 2, i * T:(i + 1) * T], rs[rws, 1, :], ALU.mult)
                        ins = dve.tensor_tensor(cmp2[HD:P, i, gg, 0:T - 1], ps_g[rws, g % 2, i * T + 1:(i + 1) * T],
                                                rs[rws, 1, 1:T], ALU.mult)
            elif s == 1:
                for i in range(2):
                    for gg in range(2):
                        rws = slice(gg * HD, (gg + 1) * HD)
                        for half in range(2):
                            ins = dve.tensor_tensor(skw[half * HD:(half + 1) * HD, i, gg, :],
                                                    ps_g[rws, g % 2, i * T:(i + 1) * T], rs[rws, 1, :], ALU.mult)
            elif s in (2, 3):
                ins = dve.tensor_tensor(aq[:, 2 * (s - 2):2 * (s - 2) + 2, :], pair(g), q_pair, ALU.mult)
            else:
                ins = dve.tensor_tensor(dqk[:, 2 * (s - 6):2 * (s - 6) + 2, :], pair(g), q_pair if s < 8 else k_pair, ALU.mult)
            ins.then_inc(emptied[g % 2], 1)
        dve.wait_ge(lam_e, 1)
        link(dve.tensor_tensor(lamn, small[:, 7:8], small[:, 6:7], ALU.subtract))
        link(dve.tensor_scalar(lamn, lamn, 0.2, None, ALU.subtract))
        dve.wait_ge(cmp_ps, 1)
        dve.tensor_copy(cposb, ps_o[:, 1, 0:2]).then_inc(cmp_b, 1)
        dve.wait_ge(cmp_ps2, 1)
        dve.tensor_copy(kc[:, :, :], ps_s[:, 0, 128:128 + 2 * NC].rearrange("p (g c) -> p g c", g=2))
        dve.tensor_copy(vc[0:NC, :], ps_s[0:NC, 0, 256:384]).then_inc(cmp_ok, 1)
        attention(0)
        dve.wait_ge(dn["sd"], 1)
        dve.reciprocal(dsq[:, :, :], dsq[:, :, :]).then_inc(dn["r"], 1)
        dve.wait_ge(dn["r"], 1)
        dve.scalar_tensor_tensor(out=dob[:, :, :], in0=dob[:, :, :], scalar=sub8, in1=dsq[:, :, :], op0=ALU.mult,
                                 op1=ALU.mult).then_inc(dn["o2"], 1)
        dve.wait_ge(dn["hi"], 1)
        dve.tensor_tensor(mix_lo[:, 4:8, :], dob[:, :, :], mix_hi[:, 4:8, :].bitcast(F32), ALU.subtract).then_inc(dn["lo"], 1)

        def add_x(g, gi):
            dve.tensor_tensor(x[:, 2 * gi:2 * gi + 2, :], pair(g), x[:, 2 * gi:2 * gi + 2, :], ALU.add)\
                .then_inc(emptied[g % 2], 1)

        def out_stage(name, n):
            for j in range(4):
                s, g = st[name].s0 + j, st[name].g0 + j
                split_lo(s + AHEAD - 1, s + AHEAD - 1)
                dve.wait_ge(slab_done, s + 1)
                add_x(g, j)
            split_x(n)

        def mlp_up(name, n, l):
            inv_rms(n)
            s0, g0 = st[name].s0, st[name].g0
            with dve.Fori(0, 4) as i:
                for j in range(4):
                    split_lo(s0 + i * 4 + j + AHEAD - 1, s0 + j + AHEAD - 1)
                    g = g0 + j
                    dve.wait_ge(slab_done, s0 + i * 4 + j + 1)
                    dve.scalar_tensor_tensor(out=up_r[:, j % 2, :, :], in0=pair(g), scalar=0.0, in1=k_pair, op0=ALU.max,
                                             op1=ALU.mult).then_inc(emptied[g % 2], 1)
                    dve.wait_ge(emptied[g % 2], out_count(g) + i * 2)
                    dve.tensor_tensor(up_q[:, j % 2, :, :], up_r[:, j % 2, :, :], up_r[:, j % 2, :, :], ALU.mult)\
                        .then_inc(upr, 1)
                    dve.wait_ge(upr, l * 16 + i * 4 + j + 1)
                    dve.wait_ge(hid_h, l * 16 + i * 4 + j + 1)
                    c = bass.ds(i * 8 + j * 2, 2)
                    dve.tensor_tensor(hid_lo[:, c, :], up_q[:, j % 2, :, :], hid_hi[:, c, :].bitcast(F32), ALU.subtract)\
                        .then_inc(hid_l, 1)

        def mlp_dn(name, n):
            s0, g0 = st[name].s0, st[name].g0
            with dve.Fori(0, 2) as i:
                for j in range(8):
                    split_lo(s0 + i * 8 + j + AHEAD - 1, s0 + j + AHEAD - 1)
                    if j % 4 == 3:
                        g = g0 + j // 4
                        dve.wait_ge(slab_done, s0 + i * 8 + j + 1)
                        c = bass.ds(i * 4 + j // 4 * 2, 2)
                        dve.tensor_tensor(x[:, c, :], pair(g), x[:, c, :], ALU.add).then_inc(emptied[g % 2], 1)
            if n in PRE:
                split_x(n)

        def qk_stage(name, dst):
            s0, g0 = st[name].s0, st[name].g0
            with dve.Fori(0, 2) as i:
                for j in range(4):
                    split_lo(s0 + i * 4 + j + AHEAD - 1, s0 + j + AHEAD - 1)
                    g = g0 + j
                    dve.wait_ge(slab_done, s0 + i * 4 + j + 1)
                    dve.tensor_tensor(dst[:, bass.ds(i * 8 + 2 * j, 2), :], pair(g),
                                      rs[:, bass.ds(i, 1), :].to_broadcast([P, 2, T]), ALU.mult).then_inc(emptied[g % 2], 1)

        out_stage("a_out", 1)
        mlp_up("a_up", 1, 0)
        mlp_dn("a_dn", 2)
        inv_rms(2)
        qk_stage("m_in", mqk)
        for j in range(4):
            s = st["m_in"].s0 + 8 + j
            split_lo(s + AHEAD - 1, s + AHEAD - 1)
        dve.wait_ge(nb_ok, 2)
        attention(1)
        out_stage("m_out", 3)
        mlp_up("m_up", 3, 1)
        mlp_dn("m_dn", 4)
        inv_rms(4)
        for gi in range(4):
            for c in (2 * gi, 2 * gi + 1):
                ins = dve.scalar_tensor_tensor(out=x[:, c, :], in0=x[:, c, :], scalar=col("norm_final", c), in1=rs[:, 1, :],
                                               op0=ALU.mult, op1=ALU.mult)
            ins.then_inc(x_new, 1)
        dve.wait_ge(x_new, 4)
        split_x(5)
        lam = col("lru_lambda_2", 0, 10)
        z, zz, s2, acc = (spw[:, 10 * k:10 * k + 10] for k in range(4))
        link(dve.tensor_scalar(zz, lam, -1.0, None, ALU.mult))
        dve.tensor_tensor(z, zz, lam, ALU.min).then_inc(sp_d, 1)
        dve.wait_ge(sp_a, 1)
        link(dve.tensor_scalar(zz, z, 2.0, None, ALU.add))
        link(dve.reciprocal(zz, zz))
        link(dve.tensor_tensor(z, z, zz, ALU.mult))
        link(dve.tensor_tensor(s2, z, z, ALU.mult))
        link(dve.tensor_scalar(acc, s2, 1.0 / 17, 1.0 / 15, ALU.mult, ALU.add))
        for k in (13, 11, 9, 7, 5, 3, 1):
            link(dve.tensor_tensor(acc, acc, s2, ALU.mult))
            link(dve.tensor_scalar(acc, acc, 1.0 / k, None, ALU.add))
        link(dve.tensor_tensor(acc, acc, z, ALU.mult))
        link(dve.tensor_scalar(zz, lam, -1.0, 0.0, ALU.mult, ALU.max))
        link(dve.scalar_tensor_tensor(out=acc, in0=acc, scalar=2.0, in1=zz, op0=ALU.mult, op1=ALU.add))
        dve.tensor_scalar(sp4, acc, 4.0, None, ALU.mult).then_inc(sp_d, 1)
        inv_rms(5)
        dve.wait_ge(zero_pad, 1)
        k = 0
        for j in range(5):
            s, g = st["r_xa"].s0 + j, st["r_xa"].g0 + j
            split_lo(s + AHEAD - 1, s + AHEAD - 1)
            dve.wait_ge(slab_done, s + 1)
            dve.tensor_tensor(xap[:, 2 * j:2 * j + 2, CONV_A - 1:], pair(g), k_pair, ALU.mult).then_inc(emptied[g % 2], 1)
            dve.wait_ge(cva, j + 1)
            dve.wait_ge(emptied[g % 2], out_count(g))
            for tap in range(CONV_A - 1):
                for c in (2 * j, 2 * j + 1):
                    if tap:
                        dve.wait_ge(cvd, k - 1)
                    dve.scalar_tensor_tensor(out=xc[:, c, :], in0=xap[:, c, tap:tap + T],
                                             scalar=col("conv_a_w_2", tap * NR + c), in1=xc[:, c, :], op0=ALU.mult,
                                             op1=ALU.add).then_inc(cvd, 1)
                    k += 1
        for j in range(NR):
            dve.wait_ge(rg["den"], j + 1)
            link(dve.tensor_scalar(rr[:, j, :], rt[:, j, :], 1.0, None, ALU.add))
            link(dve.reciprocal(rr[:, j, :], rr[:, j, :]))
        dve.wait_ge(rg["ps"], NR)
        dve.tensor_scalar(ra[:, :, :], rr[:, :, :], 2.0, -1.0, ALU.mult, ALU.add).then_inc(rg["a"], 1)
        dve.wait_ge(rg["b2"], 1)
        dve.wait_ge(rg["a"], 1)
        for j in range(NR):
            ins = dve.tensor_tensor_scan(hr[:, j, :], ra[:, j, :], rt[:, j, :], 0.0, ALU.mult, ALU.add)
        link(ins)
        for j in range(5):
            s, g = st["r_ga"].s0 + j, st["r_ga"].g0 + j
            split_lo(s + AHEAD - 1, s + AHEAD - 1)
            dve.wait_ge(slab_done, s + 1)
            dve.tensor_tensor(pt[:, j % 2, :, :], pair(g), k_pair, ALU.mult).then_inc(emptied[g % 2], 1)
            dve.wait_ge(yg, j + 1)
            dve.tensor_tensor(pt[:, 2 + j % 2, :, :], pt[:, j % 2, :, :], hr[:, 2 * j:2 * j + 2, :], ALU.mult).then_inc(yy, 1)
            dve.wait_ge(yh, j + 1)
            dve.tensor_tensor(ya_lo[:, 2 * j:2 * j + 2, :], pt[:, 2 + j % 2, :, :],
                              ya_hi[:, 2 * j:2 * j + 2, :].bitcast(F32), ALU.subtract).then_inc(yl, 1)
        for j in range(8):
            s, g = st["r_pa"].s0 + j, st["r_pa"].g0 + j // 2
            split_lo(s + AHEAD - 1, s + AHEAD - 1)
            if j % 2:
                dve.wait_ge(slab_done, s + 1)
                dve.tensor_copy(mg[:, j - 1:j + 1, :], pair(g)).then_inc(emptied[g % 2], 1)
        for j in range(8):
            s, g = st["r_gate"].s0 + j, st["r_gate"].g0 + j
            split_lo(s + AHEAD - 1, s + AHEAD - 1)
            dve.wait_ge(slab_done, s + 1)
            if 2 <= j < 6:
                dve.wait_ge(gm2, j - 1)
            elif j >= 6:
                dve.wait_ge(gs2, j - 1)
            dve.tensor_tensor(pt[:, j % 2, :, :], pair(g), k_pair, ALU.mult).then_inc(emptied[g % 2], 1)
            if j < 4:
                dve.wait_ge(gs2, j + 1)
                dve.tensor_tensor(mg[:, 2 * j:2 * j + 2, :], pt[:, j % 2, :, :], mg[:, 2 * j:2 * j + 2, :], ALU.mult)\
                    .then_inc(gm2, 1)
        s, g = st["r_f"].s0, st["r_f"].g0
        split_lo(s + AHEAD - 1, s + AHEAD - 1)
        dve.wait_ge(slab_done, s + 1)
        dve.wait_ge(gs2, 8)
        dve.tensor_tensor(fl[:, 0, :], ps_g[0:16, g % 2, 0:T], rs[0:16, 1, :], ALU.mult).then_inc(fz, 1)
        dve.wait_ge(fa, 1)
        link(dve.tensor_scalar(fl[:, 2, :], fl[:, 1, :], 0.0, None, ALU.min))
        dve.scalar_tensor_tensor(out=fl[:, 3, :], in0=fl[:, 2, :], scalar=2.0, in1=fl[:, 1, :], op0=ALU.mult,
                                 op1=ALU.subtract).then_inc(fz, 1)
        dve.memset(fl[:, 0, :], 1.0).then_inc(emptied[g % 2], 1)
        dve.wait_ge(emptied[g % 2], out_count(g))
        dve.wait_ge(fa, 3)
        link(dve.tensor_tensor(fl[:, 2, :], fl[:, 2, :], fl[:, 4, :], ALU.subtract))
        dve.tensor_tensor_scan(fl[:, 5, :], fl[:, 0, :], fl[:, 2, :], 0.0, ALU.mult, ALU.add).then_inc(fcum, 1)
        dve.wait_ge(fcq_ps, 1)
        dve.tensor_copy(fcq[:, :, :], ps_s[:, 0, 0:32].rearrange("p (b h) -> p b h", b=TB)).then_inc(fcq_ok, 1)
        for j in range(4):
            s = st["r_v"].s0 + j
            split_lo(s + AHEAD - 1, s + AHEAD - 1)
        qk_stage("r_qk", fqk)
        dve.wait_ge(fnb, 2)
        attention(2)
        for j in range(4):
            s, g = st["r_pb"].s0 + j, st["r_pb"].g0 + j
            split_lo(s + AHEAD - 1, s + AHEAD - 1)
            dve.wait_ge(slab_done, s + 1)
            c = slice(2 * j, 2 * j + 2)
            dve.tensor_tensor(sgb[:, c, :], pair(g), sgb[:, c, :], ALU.mult).then_inc(pbm, 1)
            dve.wait_ge(pbm, j + 1)
            dve.tensor_tensor(mg[:, c, :], sgb[:, c, :], mg[:, c, :], ALU.add).then_inc(emptied[g % 2], 1)
            dve.wait_ge(emptied[g % 2], out_count(g))
            dve.wait_ge(pbh, j + 1)
            dve.tensor_tensor(m2_lo[:, c, :], mg[:, c, :], m2_hi[:, c, :].bitcast(F32), ALU.subtract).then_inc(pbl, 1)

        def take(name, j, g):
            dve.tensor_copy(mo[:, 2 * j:2 * j + 2, :], pair(g)).then_inc(emptied[g % 2], 1)

        def post(n, name):
            inv_rms(n)
            for gi in range(4):
                b = gi % 2
                link(dve.tensor_tensor(pt2[:, b, :, :], mo[:, 2 * gi:2 * gi + 2, :], k_pair, ALU.mult))
                for c in (0, 1):
                    cc = 2 * gi + c
                    ins = dve.scalar_tensor_tensor(out=x[:, cc, :], in0=pt2[:, b, c, :], scalar=col(name, cc),
                                                   in1=x[:, cc, :], op0=ALU.mult, op1=ALU.add)
                ins.then_inc(x_new, 1)

        for j in range(4):
            s, g = st["r_out"].s0 + j, st["r_out"].g0 + j
            split_lo(s + AHEAD - 1, s + AHEAD - 1)
            dve.wait_ge(slab_done, s + 1)
            take("r_out", j, g)
        post(6, "mix_norm_post_2")
        split_x(7)
        inv_rms(7)
        dve.wait_ge(zero_pad, 2)
        s0, g0 = st["f_up"].s0, st["f_up"].g0
        with dve.Fori(0, 6) as i:
            for j in range(4):
                split_lo(s0 + i * 4 + j + AHEAD - 1, s0 + j + AHEAD - 1)
                g = g0 + j
                dve.wait_ge(slab_done, s0 + i * 4 + j + 1)
                dve.tensor_tensor(upad[:, j % 2, :, CONV_F - 1:], pair(g), k_pair, ALU.mult).then_inc(emptied[g % 2], 1)
                dve.wait_ge(emptied[g % 2], out_count(g) + i * 2)
                dve.wait_ge(fuc, i * 4 + j + 1)
                for tap in range(CONV_F - 1):
                    for c in range(2):
                        if tap:
                            dve.wait_ge(fud, i * 16 + j * 4 + c + 1)
                        ch = (j % 2) * NH2 + 2 * (j // 2) + c
                        dve.scalar_tensor_tensor(out=ucv[:, j % 2, c, :], in0=upad[:, j % 2, c, tap:tap + T],
                                                 scalar=fw[:, tap, bass.ds(i * 4 + ch, 1)], in1=ucv[:, j % 2, c, :],
                                                 op0=ALU.mult, op1=ALU.add).then_inc(fud, 1)
                if j % 2:
                    dve.wait_ge(fud, i * 16 + j * 4 + 4)
                    dve.wait_ge(fug, i * 2 + j // 2 + 1)
                    dve.tensor_tensor(ucv[:, 1, :, :], ucv[:, 0, :, :], ucv[:, 1, :, :], ALU.mult).then_inc(fup, 1)
                    dve.wait_ge(fup, i * 2 + j // 2 + 1)
                    dve.wait_ge(fuh, i * 2 + j // 2 + 1)
                    c = bass.ds(i * 4 + (j // 2) * 2, 2)
                    dve.tensor_tensor(h2_lo[:, c, :], ucv[:, 1, :, :], h2_hi[:, c, :].bitcast(F32), ALU.subtract)\
                        .then_inc(ful, 1)
        for j in range(12):
            s, g = st["f_dn"].s0 + j, st["f_dn"].g0 + j // 3
            split_lo(s + AHEAD - 1, s + AHEAD - 1)
            if j % 3 == 2:
                dve.wait_ge(slab_done, s + 1)
                take("f_dn", j // 3, g)
        post(8, "ffn_norm_post_2")

    @block.tensor
    def _(pe):
        def gemm(s, sj, g, gj, x_hi, x_lo, kc0=0, n_k=KS, first=True, last=True, tok_major=False, n=NS, m=None,
                 before_pair=None):
            slot, b = sj % RING, gj % 2
            pe.wait_ge(w_ready, s + 1)
            if first:
                pe.wait_ge(emptied[b], g)
            for k in range(n_k):
                if before_pair is not None and k % 2 == 0:
                    before_pair(k // 2)
                passes = ((w_hi, x_hi), (w_hi, x_lo), (w_lo, x_hi))
                for half in range(2):
                    if m is not None and half:
                        break
                    for q, (w, xx) in enumerate(passes):
                        if tok_major:
                            lhs = xx[:, kc0 + k, half * P:(half + 1) * P]
                            rhs = w[:, slot, k, 0:n]
                            dst = ps_g[:, b, half * NS:half * NS + n]
                        else:
                            mm = m or P
                            lhs = w[:, slot, k, half * P:half * P + mm]
                            rhs = xx[:, kc0 + k, :]
                            dst = ps_g[0:mm, b, half * T:(half + 1) * T]
                        ins = pe.matmul(dst, lhs, rhs, start=(first and k == 0 and half == 0 and q == 0),
                                        stop=(last and k == n_k - 1 and q == 2), skip_group_check=True)
            ins.then_inc(slab_done, 1)

        def gwait(g):
            return out_count(g) - 1

        def x_in(n):
            def wait(pair):
                pe.wait_ge(xl, PRE_I[n] * 4 + pair + 1)
            return wait

        def stat(n):
            if n:
                pe.wait_ge(sd_ok, n)
            for c in range(NX):
                if c % 2 == 0:
                    pe.wait_ge(sq_ok, 4 * n + c // 2 + 1)
                ins = pe.matmul(ps_s[:, 0, 0:T], ones[:, :], sq[:, c, :], start=(c == 0), stop=(c == NX - 1))
            ins.then_inc(stat_ok, 1)

        def stat_tok(n):
            pe.wait_ge(rs_ok, n + 1)
            if TOK[n]:
                pe.wait_ge(rst_ok, TOK[n])
            for tb in range(TB):
                ins = pe.matmul(ps_s[:, 1, tb:tb + 1], rs[0:1, 1, tb * P:(tb + 1) * P], ones[0:1, 0:1], start=True,
                                stop=True)
            ins.then_inc(rst_ps, 1)

        def attention(p):
            a, units = att[p], UNITS[p]
            n_units = len(units)

            def scores(i):
                u = units[i]
                if i >= 2:
                    pe.wait_ge(a["logit"], i - 1)
                for b, (c0, n) in enumerate(u["blocks"]):
                    ins = pe.matmul(ps_s[:, i % 2, c0:c0 + n], u["q"][:, b * P:(b + 1) * P], u["k"][b], start=True, stop=True)
                ins.then_inc(a["score"], 1)

            def normed(i):
                return units[i]["n_done"]

            def transposes(i):
                u = units[i]
                if u["pv"] is None:
                    return
                n = u["n"]
                pe.wait_ge(a["norm"], normed(i))
                if n >= 2:
                    pe.wait_ge(a["trc"], n - 1)
                for q, (c0, k) in enumerate(u["tiles"]):
                    ins = pe.transpose(ps_t[0:k, n % 2, q * P:(q + 1) * P], prob[:, i % 3, c0:c0 + k], ident[:, :])
                ins.then_inc(a["tr"], 1)

            def values(i):
                u = units[i]
                if u["pv"] is None:
                    return
                n, o = u["n"], u["out"]
                pe.wait_ge(a["trc"], n + 1)
                if u["start"] and u["rows"][0] == 0 and o >= 2:
                    if p == 0 and o >= 4:
                        pe.wait_ge(a["oh"], o - 1)
                        pe.wait_ge(a["ol"], min(o - 1, 4))
                    else:
                        pe.wait_ge(a["ol"], o - 1)
                r0, r1 = u["rows"]
                for q, (v, k, (c0, c1), (o0, o1)) in enumerate(u["pv"]):
                    ins = pe.matmul(ps_o[r0:r1, o % 2, o0:o1], v, prob_t[0:k, n % 2, c0:c1],
                                    start=(u["start"] and q == 0), stop=(u["stop"] and q == 1), skip_group_check=True)
                ins.then_inc(a["pv"], 1)

            scores(0)
            for i in range(n_units + 1):
                if i + 1 < n_units:
                    scores(i + 1)
                if i < n_units:
                    transposes(i)
                if i >= 1:
                    values(i - 1)

        pe.wait_ge(idn, 2)
        pe.wait_ge(ld["par"], 16 * (len(PARAMS) + 1))
        for k in range(4):
            ins = pe.transpose(ps_t[:, 0, k * P:k * P + TILE_ROWS[k]], prow[0:TILE_ROWS[k], k, :],
                               ident[0:TILE_ROWS[k], 0:TILE_ROWS[k]])
        ins.then_inc(par_t, 1)
        pe.wait_ge(ld["x"], 32)
        for gi in range(4):
            if gi >= 2:
                pe.wait_ge(emptied[gi % 2], gi // 2)
            for c in range(2):
                for tb in range(TB):
                    ins = pe.transpose(ps_g[:, gi % 2, c * T + tb * P:c * T + (tb + 1) * P],
                                       xin[:, tb, (2 * gi + c) * P:(2 * gi + c + 1) * P], ident[:, :])
            ins.then_inc(xt, 1)
        pe.wait_ge(ld["bias"], 32)
        pe.matmul(ps_o[0:16, 0, 0:REL], btab[:, :], buck[:, :], start=True, stop=True).then_inc(brow_ps, 1)
        g0 = st["a_in"].g0
        for j in range(12):
            s, g = st["a_in"].s0 + j, g0 + j
            gemm(s, s, gwait(g), g, act_hi, act_lo, before_pair=x_in(0) if j == 0 else None, tok_major=j in (4, 5, 10, 11),
                 n=GATES if j == 5 else NS)
            if j == 0:
                stat(0)
                stat_tok(0)
        pe.wait_ge(ld["cw"], 16 * 6)
        pe.wait_ge(emptied[g0 % 2], out_count(g0))
        for i in range(2):
            pcol = par[:, 3, 16 * i:16 * i + 16]
            for m in range(16):
                pe.matmul(ps_s[:, i, 0:2 * NC].rearrange("p (g c) -> p g c", g=2), cw1[:, i, m, :],
                          cmp2[:, i, :, 2 * m:2 * m + (NC - 1) * CMP_STRIDE + 1:CMP_STRIDE],
                          start=(m == 0), stop=(m == 15))
        for i in range(2):
            for m in range(16):
                ins = pe.matmul(ps_o[:, 1, i:i + 1], cw1[:, i, m, :], par[:, 3, 16 * i + m:16 * i + m + 1],
                                start=(m == 0), stop=(m == 15))
        ins.then_inc(cmp_ps, 1)
        pe.wait_ge(cmp_h, 1)
        pe.matmul(ps_s[:, 0, 128:128 + 2 * NC], cw2[:, 0, :], chid[:, 0, :], start=True, stop=True)
        for gg in range(2):
            ins = pe.matmul(ps_s[0:NC, 0, 256 + gg * HD:256 + (gg + 1) * HD], chid[:, 1, gg * NC:(gg + 1) * NC],
                            cw2[:, 1, 0:HD], start=True, stop=True)
        ins.then_inc(cmp_ps2, 1)
        pe.wait_ge(cmp_ok, 1)
        for b in range(2):
            g = g0 + 10 + b
            pe.wait_ge(emptied[g % 2], out_count(g))
        attention(0)
        pe.wait_ge(dn["sq"], 1)
        pe.wait_ge(att[0]["ol"], 4)
        for h in range(DIFF_H):
            ins = pe.matmul(ps_o[:, h // 2, (h % 2) * T:(h % 2 + 1) * T], ones[:, :], dsq[:, h, :], start=True, stop=True)
        ins.then_inc(dn["ps"], 1)

        def out_stage(name, n, h, l, ready):
            for j in range(4):
                s, g = st[name].s0 + j, st[name].g0 + j
                gemm(s, s, gwait(g), g, h, l, before_pair=ready if j == 0 else None)

        def mlp(up, dn_, n, l):
            s0, g0 = st[up].s0, st[up].g0
            for j in range(4):
                gemm(s0 + j, s0 + j, gwait(g0 + j), g0 + j, act_hi, act_lo, before_pair=x_in(n) if j == 0 else None)
                if j == 0:
                    stat(n)
            with pe.Fori(1, 4) as i:
                for j in range(4):
                    gemm(s0 + i * 4 + j, s0 + j, gwait(g0 + j) + i * 2, g0 + j, act_hi, act_lo)
            s0, g0 = st[dn_].s0, st[dn_].g0
            with pe.Fori(0, 2) as i:
                for j in range(8):
                    def ready(pair, r=j % 4):
                        pe.wait_ge(hid_l, l * 16 + r * 4 + pair + 1)
                    gemm(s0 + i * 8 + j, s0 + j, gwait(g0 + j // 4) + i, g0 + j // 4, hid_hi, hid_lo, kc0=(j % 4) * 8,
                         first=j % 4 == 0, last=j % 4 == 3, before_pair=ready if j < 4 else None)

        def mix_in(p):
            def wait(pair):
                if p == 0 and pair >= 2:
                    pe.wait_ge(dn["lo"], 1)
                else:
                    pe.wait_ge(att[p]["ol"], 2 * pair + 2)
            return wait

        out_stage("a_out", 1, mix_hi, mix_lo, mix_in(0))
        mlp("a_up", "a_dn", 1, 0)
        s0, g0 = st["m_in"].s0, st["m_in"].g0
        for j in range(4):
            gemm(s0 + j, s0 + j, gwait(g0 + j), g0 + j, act_hi, act_lo, before_pair=x_in(2) if j == 0 else None)
            if j == 0:
                stat(2)
                stat_tok(2)
        for j in range(4, 8):
            gemm(s0 + j, s0 + j, gwait(g0 + j), g0 + j, act_hi, act_lo)
        for j in range(8, 12):
            gemm(s0 + j, s0 + j, gwait(g0 + j), g0 + j, act_hi, act_lo, tok_major=True)
        for b in range(2):
            pe.wait_ge(emptied[(g0 + 10 + b) % 2], out_count(g0 + 10 + b))
        attention(1)
        out_stage("m_out", 3, mix_hi, mix_lo, mix_in(1))
        mlp("m_up", "m_dn", 3, 1)
        stat(4)
        s0, g0 = st["r_xa"].s0, st["r_xa"].g0
        for j in range(5):
            gemm(s0 + j, s0 + j, gwait(g0 + j), g0 + j, act_hi, act_lo, before_pair=x_in(5) if j == 0 else None)
            if j == 0:
                stat(5)
                stat_tok(5)
        pe.wait_ge(ld["gw"], 16 * 2 * len(pieces))
        pe.wait_ge(rst_ok, 3)
        for j in range(NR):
            srcs = rg_inputs(j)
            pe.wait_ge(cvd, 6 * (srcs[-1] // 2) + 6)
            if j >= 2:
                pe.wait_ge(rg["sig"], j - 1)
            for i in range(2):
                for q, c in enumerate(srcs):
                    ins = pe.matmul(ps_s[:, j % 2, i * T:(i + 1) * T], gw[:, i, c, j - c + 1, :], xc[:, c, :],
                                    start=(q == 0), stop=(q == len(srcs) - 1))
            ins.then_inc(rg["ps"], 1)
        s0, g0 = st["r_ga"].s0, st["r_ga"].g0
        for j in range(5):
            gemm(s0 + j, s0 + j, gwait(g0 + j), g0 + j, act_hi, act_lo)
        s0, g0 = st["r_pa"].s0, st["r_pa"].g0
        pe.wait_ge(yl, 5)
        for j in range(8):
            gemm(s0 + j, s0 + j, gwait(g0 + j // 2), g0 + j // 2, ya_hi, ya_lo, kc0=(j % 2) * (NR // 2), n_k=NR // 2,
                 first=j % 2 == 0, last=j % 2 == 1)
        s0, g0 = st["r_gate"].s0, st["r_gate"].g0
        for j in range(8):
            gemm(s0 + j, s0 + j, gwait(g0 + j), g0 + j, act_hi, act_lo)
        s0, g0 = st["r_f"].s0, st["r_f"].g0
        gemm(s0, s0, gwait(g0), g0, act_hi, act_lo, m=ATT_H)
        s0, g0 = st["r_v"].s0, st["r_v"].g0
        for j in range(4):
            gemm(s0 + j, s0 + j, gwait(g0 + j), g0 + j, act_hi, act_lo, tok_major=True)
            if j == 0:
                pe.wait_ge(fcum, 1)
                pe.wait_ge(rg["sig"], NR)
                for tb in range(TB):
                    ins = pe.transpose(ps_s[:, 0, tb * 16:(tb + 1) * 16], fl[:, 5, tb * P:(tb + 1) * P], ident[0:16, 0:16])
                ins.then_inc(fcq_ps, 1)
        s0, g0 = st["r_qk"].s0, st["r_qk"].g0
        with pe.Fori(0, 2) as i:
            for j in range(4):
                gemm(s0 + i * 4 + j, s0 + j, gwait(g0 + j) + i * 2, g0 + j, act_hi, act_lo)
        for b in range(2):
            pe.wait_ge(emptied[(g0 + 6 + b) % 2], out_count(g0 + 6 + b))
        pe.wait_ge(fcq_ok, 1)
        attention(2)
        out_stage("r_pb", 6, act_hi, act_lo, mix_in(2))

        def m2_in(pair):
            pe.wait_ge(pbl, pair + 1)

        out_stage("r_out", 6, m2_hi, m2_lo, m2_in)
        stat(6)
        s0, g0 = st["f_up"].s0, st["f_up"].g0
        for j in range(4):
            gemm(s0 + j, s0 + j, gwait(g0 + j), g0 + j, act_hi, act_lo, before_pair=x_in(7) if j == 0 else None)
            if j == 0:
                stat(7)
        with pe.Fori(1, 6) as i:
            for j in range(4):
                gemm(s0 + i * 4 + j, s0 + j, gwait(g0 + j) + i * 2, g0 + j, act_hi, act_lo)
        s0, g0 = st["f_dn"].s0, st["f_dn"].g0
        for j in range(12):
            def ready(pair, r=j % 3):
                pe.wait_ge(ful, r * 4 + pair + 1)
            gemm(s0 + j, s0 + j, gwait(g0 + j // 3), g0 + j // 3, h2_hi, h2_lo, kc0=(j % 3) * 8, first=j % 3 == 0,
                 last=j % 3 == 2, before_pair=ready if j < 3 else None)
        stat(8)
        pe.wait_ge(x_new, 12)
        for q in range(4):
            if q >= 2:
                pe.wait_ge(oc, q - 1)
            for c in range(4):
                ins = pe.transpose(ps_g[:, q % 2, c * P:(c + 1) * P], x[:, (q % 2) * 4 + c, (q // 2) * P:(q // 2 + 1) * P],
                                   ident[:, :])
            ins.then_inc(ot, 1)


_NAMES = [
    "x", "bias_table", "norm_mix", "norm_mlp", "norm_final", "mlp_w1", "mlp_w2", "ev_w_in", "ev_w_out",
    "ev_cmp_pos_k", "ev_cmp_w1_k", "ev_cmp_w2_k", "ev_cmp_pos_v", "ev_cmp_w1_v", "ev_cmp_w2_v", "ev_lam_q1",
    "ev_lam_k1", "ev_lam_q2", "ev_lam_k2", "ev_subln", "od_w_in", "od_w_out", "mix_norm_pre_2",
    "mix_norm_post_2", "w_in_2", "conv_a_w_2", "conv_a_b_2", "w_rg_a_2", "b_rg_a_2", "w_rg_x_2", "b_rg_x_2",
    "lru_lambda_2", "b_forget_2", "b_merge_2", "w_proj_a_2", "w_proj_b_2", "w_out_2", "ffn_norm_pre_2",
    "ffn_norm_post_2", "w_up_2", "conv_f_w_2", "conv_f_b_2", "w_down_2",
]


def kernel(**inputs):
    import concourse.bacc as bacc
    from concourse.bass_utils import run_bass_kernel_spmd

    nc = bacc.Bacc("TRN2", target_bir_lowering=False, num_devices=1)
    arrays, t = {}, {}
    for name in _NAMES:
        a = np.ascontiguousarray(inputs[name])
        arrays[f"in_{name}"] = a
        t[name] = nc.dram_tensor(f"in_{name}", a.shape, mybir.dt.from_np(a.dtype), kind="ExternalInput").ap()
    rows = bucket_rows()
    arrays["bucket_rows"] = rows
    t["bucket"] = nc.dram_tensor("bucket_rows", rows.shape, F32, kind="ExternalInput").ap()
    out = nc.dram_tensor("out", (1, T, D), F32, kind="ExternalOutput").ap()
    with ExitStack() as ctx:
        build(nc, ctx, t, out)
    return run_bass_kernel_spmd(nc, [arrays], core_ids=[0]).results[0]["out"]
```

```python
import math
from contextlib import ExitStack

import concourse.bass as bass
from concourse import mybir
import numpy as np

F32 = mybir.dt.float32
F32R = mybir.dt.float32r
ALU = mybir.AluOpType
ACT = mybir.ActivationFunctionType

P = 128
T = 256
TB = T // P
D = 1024
NX = D // P
KS = 8
NS = 256
HD = 64
BIG = 1e30
EPS = 1e-6
NSA_H, DIFF_H, MOBA_H, ATT_H = 8, 4, 16, 16
GATES = 3 * NSA_H
CMP_BLOCK, CMP_STRIDE = 32, 16
NC = (T - CMP_BLOCK) // CMP_STRIDE + 1
NC0 = (P - CMP_BLOCK) // CMP_STRIDE + 1
D_RNN, RNN_BLOCK = 1280, 80
NR = D_RNN // P
CONV_A, CONV_F = 4, 3
D_FF = 4096
NH1 = D_FF // P
D_FF2 = 3072
NH2 = D_FF2 // P
NUM_BUCKETS, MAX_DISTANCE = 32, 128
PB = 5
LAG_N, LAG_T, LAG_V, LAG_HI, LAG_LO = 2, 3, 5, 6, 7
DN_PS = [2 * h + 9 for h in range(DIFF_H)]
DN_ROOT = DN_PS[-1] + 1
DN_R = [DN_ROOT + 2 + 2 * h for h in range(DIFF_H)]
DN_HI = [i + 1 for i in DN_R]
DN_LO = [i + 2 for i in DN_R]
RG_STEP = 1
CMP_STEP = 8
RING = 4
AHEAD = 3
REL = 384


class Stage:
    s, g = 0, 0

    def __init__(self, slabs, per_group=1):
        self.s0, self.g0, self.n, self.per = Stage.s, Stage.g, slabs, per_group
        Stage.s += slabs
        Stage.g += slabs // per_group


def stages():
    Stage.s = Stage.g = 0
    st = {}
    for name, n, per in (("a_in", 12, 1), ("a_out", 4, 1), ("a_up", 16, 1), ("a_dn", 16, 4),
                         ("m_in", 12, 1), ("m_out", 4, 1), ("m_up", 16, 1), ("m_dn", 16, 4),
                         ("r_xa", 5, 1), ("r_f", 1, 1), ("r_gate", 8, 1), ("r_ga", 5, 1), ("r_v", 4, 1),
                         ("r_pa", 8, 2), ("r_qk", 8, 1), ("r_pb", 4, 1), ("r_out", 4, 1),
                         ("f_up", 24, 1), ("f_dn", 12, 3)):
        st[name] = Stage(n, per)
    return st, Stage.s


PARAMS = {
    "norm_mix": (0, 0, 16), "norm_mlp": (0, 16, 16), "norm_final": (0, 32, 8), "mix_norm_pre_2": (0, 40, 8),
    "mix_norm_post_2": (0, 48, 8), "ffn_norm_pre_2": (0, 56, 8), "ffn_norm_post_2": (0, 64, 8),
    "conv_a_b_2": (0, 72, 10), "b_rg_a_2": (0, 82, 10), "b_rg_x_2": (0, 92, 10), "lru_lambda_2": (0, 102, 10),
    "b_merge_2": (0, 112, 16),
    "conv_a_w_2": (1, 0, 40), "ev_subln": (1, 40, 1), "conv_f_b_2": (1, 41, 48),
    "conv_f_w_2": (2, 0, 128),
    "ev_cmp_pos_k": (3, 0, 16), "ev_cmp_pos_v": (3, 16, 16),
}
CONV_F_TAIL = (3, 32, 16)
TILE_ROWS = (128, 89, 128, 48)


def bucket_rows():
    rel = 255 - np.arange(REL)
    n = np.maximum(rel, 0)
    half = NUM_BUCKETS // 2
    large = half + (np.log(np.maximum(n, 1).astype(np.float32) / np.float32(half))
                    / np.float32(math.log(MAX_DISTANCE / half)) * np.float32(NUM_BUCKETS - half)).astype(np.int32)
    bucket = np.where(n < half, n, np.minimum(large, NUM_BUCKETS - 1))
    return -(bucket[None, :] == np.arange(NUM_BUCKETS)[:, None]).astype(np.float32)


def rg_pieces():
    out = []
    for b in range(D_RNN // RNN_BLOCK):
        row = b * RNN_BLOCK
        end = row + RNN_BLOCK
        while row < end:
            n = min(end, (row // P + 1) * P) - row
            out.append((row // P, row % P, n, b, row - b * RNN_BLOCK))
            row += n
    return out


def rg_inputs(j):
    lo = (j * P) // RNN_BLOCK * RNN_BLOCK
    hi = -(-((j + 1) * P) // RNN_BLOCK) * RNN_BLOCK
    return list(range(lo // P, (hi - 1) // P + 1))


def build(nc, ctx, t, out):
    st, n_slabs = stages()
    pieces = rg_pieces()

    base = 16512
    top = [base]

    def place(name, shape, dt=F32, at=None):
        size = int(np.prod(shape[1:])) * 4
        if at is None:
            at = top[0]
            top[0] = -(-(at + size) // 32) * 32
        return nc.alloc_sbuf_tensor_at(name, shape, dt, offset=at)

    K = 1024
    raw = place("raw", [P, RING, KS, NS])
    w_hi = place("w_hi", [P, RING, KS, NS], F32R)
    w_lo = place("w_lo", [P, RING, KS, NS], F32R)
    x = place("x", [P, NX, T])
    ident = place("ident", [P, P])
    ones = place("ones", [P, P])
    par = place("par", [P, 4, P])
    rs = place("rs", [P, 2, T])
    sd = place("sd", [P, T])
    rs_f = place("rs_f", [P, T])
    gain_f = place("gain_f", [P, NX])
    eps_ones = place("eps_ones", [P, P])
    rs_tok = place("rs_tok", [P, TB])
    nmin = place("nmin", [P, 24 + 2 * DIFF_H, 2])
    psum_ = place("sums", [P, 24 + 2 * DIFF_H, 2])
    fac = place("fac", [P, 24 + 2 * DIFF_H, 2])
    small = place("small", [P, 64])
    fcq = place("f_cum_q", [P, TB, 16])
    fw = place("conv_f", [P, 4, 2 * NH2])
    act_hi = place("act_hi", [P, NX, T], F32R)
    act_lo = place("act_lo", [P, NX, T], F32R)
    tmp0 = top[0]
    arena = tmp0 + 8 * K
    assert arena + 70 * K <= 229344, arena + 70 * K

    def tm(name, shape, at, dt=F32):
        assert at + int(np.prod(shape[1:])) * 4 <= 8 * K
        return place(name, shape, dt, tmp0 + at)

    def ar(name, shape, at, dt=F32):
        assert arena + at + int(np.prod(shape[1:])) * 4 <= 229344, name
        return place(name, shape, dt, arena + int(at))

    sq = tm("sq", [P, 2, 2, T], 0)
    sq_sum = tm("sq_sum", [P, 2, 2, T], 4 * K)
    up_r = tm("up_r", [P, 2, 2, T], 0)
    up_q = tm("up_q", [P, 2, 2, T], 4 * K)
    prob = tm("prob", [P, PB, 384], 0)
    hid_hi = ar("hid_hi", [P, NH1, T], 0, F32R)
    hid_lo = ar("hid_lo", [P, NH1, T], 32 * K, F32R)
    mix_hi = ar("mix_hi", [P, NX, T], 0, F32R)
    mix_lo = ar("mix_lo", [P, NX, T], 8 * K, F32R)
    cw1 = ar("cmp_w1", [P, 2, 16, P], 0)
    nb = ar("bias", [P, 16, T], 16 * K)
    aq = ar("a_q", [P, 4, T], 32 * K)
    cmp2 = tm("cmp_in", [P, 2, 3, T], 0)
    skw = ar("a_skw", [P, 2, 2, T], 40 * K)
    sv = ar("a_sv", [P, TB, NS], 44 * K)
    dqk = ar("d_qk", [P, 8, T], 46 * K)
    dv = ar("d_v", [P, TB, 4 * P], 54 * K)
    gates = ar("gates", [P, TB, GATES], 58 * K)
    cw2 = ar("cmp_w2", [P, 2, P], 58 * K + 256)
    chid = ar("cmp_hid", [P, 2, 2 * NC], 36 * K)
    kc = ar("kc", [P, 2, NC], 60 * K)
    vc = ar("vc", [P, P], 60 * K + 256)
    dob = ar("d_ob", [P, DIFF_H, T], 61 * K)
    lamv = ar("lam_v", [P, 4, HD], 65 * K)
    xin = ar("x_in", [P, TB, D], 32 * K)
    prow = ar("par_rows", [P, 4, P], 40 * K)
    buck = ar("bucket", [NUM_BUCKETS, REL], 42 * K)
    btab = ar("bias_table", [NUM_BUCKETS, 16], 44 * K)
    brow = ar("bias_row", [16, REL], 66.5 * K)
    dsq = ar("d_sq", [P, DIFF_H, T], 46 * K)
    mqk = ar("m_qk", [P, 16, T], 32 * K)
    mv = ar("m_v", [P, TB, D], 48 * K)
    xap = ar("xa_pad", [P, NR, T + CONV_A - 1], 0)
    rt = ar("rg_t", [P, NR, T], 0)
    xc = ar("xc", [P, NR, T], 10.25 * K)
    rr = ar("rg_r1", [P, NR, T], 10.25 * K)
    gw = ar("rg_w", [P, 2, NR, 3, P], 20.5 * K)
    ra = ar("rg_decay", [P, NR, T], 20.5 * K)
    rix = ar("rg_ix", [P, NR, T], 50.5 * K)
    hr = ar("h_rnn", [P, NR, T], 50.5 * K)
    ya_hi = ar("ya_hi", [P, NR, T], 30.5 * K, F32R)
    ya_lo = ar("ya_lo", [P, NR, T], 40.5 * K, F32R)
    gt = ar("gelu_tmp", [P, 2, 2, T], 0)
    sga = tm("sig_a", [P, NX, T], 0)
    sgb = ar("sig_b", [P, NX, T], 60.5 * K)
    fl = tm("f_logsig", [16, 6, T], 0)
    fqk = ar("f_qk", [P, 16, T], 0)
    fv = ar("f_v", [P, TB, D], 16 * K)
    nb2 = ar("f_bias", [P, 16, 384], 27 * K)
    mg = ar("merge", [P, NX, T], 51 * K)
    prob_ts = [ar("prob_t", [P, 2, 384], 66.5 * K), ar("prob_t_f", [P, 2, 384], 24 * K)]
    m2_hi = ar("m2_hi", [P, NX, T], 0, F32R)
    m2_lo = ar("m2_lo", [P, NX, T], 8 * K, F32R)
    mo = ar("mix_out", [P, NX, T], 27 * K)
    pt2 = ar("post_tmp", [P, 2, 2, T], 36 * K)
    h2_hi = ar("h2_hi", [P, NH2, T], 0, F32R)
    h2_lo = ar("h2_lo", [P, NH2, T], 24 * K, F32R)
    upad = ar("up_pad", [P, 2, 2, T + CONV_F - 1], 48 * K)
    ucv = ar("up_conv", [P, 2, 2, T], 52.25 * K)
    hp = ar("up_prod", [P, 2, 2, T], 56.25 * K)
    fo = ar("ffn_out", [P, NX, T], 56.5 * K)
    pt3 = ar("post_tmp_f", [P, 2, 2, T], 64.5 * K)
    xout = ar("x_out", [P, TB, D], 0)

    ps_g = ctx.enter_context(nc.psum_tensor("ps_gemm", [P, 2, 512], F32))
    ps_s = ctx.enter_context(nc.psum_tensor("ps_score", [P, 2, 512], F32))
    ps_t = ctx.enter_context(nc.psum_tensor("ps_trans", [P, 2, 512], F32))
    ps_o = ctx.enter_context(nc.psum_tensor("ps_out", [P, 2, 512], F32))

    def sem(name):
        return ctx.enter_context(nc.semaphore(name))

    raw_in = [sem(f"raw_in{i}") for i in range(RING)]
    hi_done = sem("hi_done")
    w_ready = sem("w_ready")
    slab_done = sem("slab_done")
    emptied = [sem(f"emptied{b}") for b in range(2)]
    ld = {n: sem(f"ld_{n}") for n in ("x", "g", "par", "bias", "cw", "gw", "lam", "bf")}
    idn = sem("idn")
    par_t, par_ok = sem("par_t"), sem("par_ok")
    xt = sem("x_transposed")
    brow_ps, brow_ok, brow_out, nb_in, nb_ok = (sem(n) for n in ("brow_ps", "brow_ok", "brow_out", "nb_in", "nb_ok"))
    xh, xl = sem("act_hi_done"), sem("act_lo_done")
    sq_ok, stat_ok, sd_ok, rs_ok = sem("sq_ok"), sem("stat_ok"), sem("sd_ok"), sem("rs_ok")
    rsq_ok, rst_ps, rst_ok = sem("rsq_ok"), sem("rst_ps"), sem("rst_ok")
    x_new = sem("x_new")
    upr, hid_h, hid_l = sem("up_relu2"), sem("hid_hi_done"), sem("hid_lo_done")
    dve_c, act_c = sem("dve_chain"), sem("act_chain")
    att = [{n: sem(f"at{p}_{n}") for n in ("in", "score", "logit", "prob", "sum", "norm", "tr", "trc", "pv", "oh", "ol")}
           for p in range(3)]
    cmp_ps, cmp_b, cmp_h, cmp_ps2, cmp_ok = (sem(n) for n in ("cmp_ps", "cmp_b", "cmp_h", "cmp_ps2", "cmp_ok"))
    dn = {n: sem(f"dn_{n}") for n in ("o", "sq", "ps", "sd", "r", "o2", "hi", "lo")}
    lam_ok, lam_e = sem("lam_ok"), sem("lam_e")
    gz = sem("gw_zero")
    cva, cvd = sem("conv_a_act"), sem("conv_a_dve")
    rg = {n: sem(f"rg_{n}") for n in ("ps", "sig", "ix", "den", "sq", "a", "b1", "b2", "h")}
    rcp = sem("rg_recip")
    sp_a, sp_d = sem("sp_act"), sem("sp_dve")
    yg, yy, yh, yl = (sem(n) for n in ("ya_gelu", "ya_y", "ya_hi_done", "ya_lo_done"))
    gs2 = sem("gate_sig")
    sqg, sdf, rsf, x_mat, gain_ok = (sem(n) for n in ("sq_gain", "sd_f", "rs_f_ok", "x_mat", "gain_ok"))
    epso, sqg_used = sem("eps_ones_ok"), sem("sq_gain_used")
    fz, fa, fcum = sem("f_z"), sem("f_act"), sem("f_cum")
    fout, fin_, fcq_ps, fcq_ok, fnb = (sem(n) for n in ("f_cum_out", "f_bias_in", "f_cq_ps", "f_cq_ok", "f_nb"))
    pbm, pbh, pbl = sem("pb_m"), sem("pb_hi"), sem("pb_lo")
    fuz, fuc, fud, fug, fup, fuh, ful = (sem(n) for n in ("fu_z", "fu_conv1", "fu_conv", "fu_gelu", "fu_prod", "fu_hi", "fu_lo"))
    zero_pad = sem("zero_pad")
    ot, oc, o_out = sem("out_t"), sem("out_c"), sem("out_dma")
    pool_c = sem("pool_chain")

    scr_b = nc.dram_tensor("bias_rows_scr", [16, REL], F32, kind="Internal").ap()
    scr_w = nc.dram_tensor("bias_wide_scr", [16, 16 * REL], F32, kind="Internal").ap()
    scr_c = nc.dram_tensor("cum_scr", [16, T], F32, kind="Internal").ap()

    def col(name, i=0, n=1):
        tile, row, rows = PARAMS[name]
        return par[:, tile, row + i:row + i + n]

    def conv_f_w(j, c):
        r = j * 2 * NH2 + c
        if r < P:
            return par[:, 2, r:r + 1]
        return par[:, CONV_F_TAIL[0], CONV_F_TAIL[1] + r - P:CONV_F_TAIL[1] + r - P + 1]

    eps_c, eps2_c, _, one_c, lamn = (small[:, i:i + 1] for i in range(5))
    sub8 = small[:, 5:6]
    sp4 = small[:, 8:18]
    spw = small[:, 18:58]
    cposb = small[:, 58:60]
    b_f = small[0:16, 60:61]

    def out_count(g):
        return g // 2 + 3

    def x_ready(n, gi):
        if n == 0:
            return emptied[gi % 2], gi // 2 + 1
        if n == 6:
            return x_new, gi + 1
        g = st[{1: "a_out", 2: "a_dn", 3: "m_out", 4: "m_dn", 5: "r_out", 7: "f_dn"}[n]].g0 + gi
        return emptied[g % 2], out_count(g)

    PRE = {0: ("norm_mix", 0), 1: ("norm_mlp", 0), 2: ("norm_mix", 8), 3: ("norm_mlp", 8),
           4: None, 6: ("ffn_norm_pre_2", 0)}
    PRE_I = {n: i for i, n in enumerate(PRE)}

    def gain(n, c):
        return gain_f[:, c:c + 1] if n == 4 else col(PRE[n][0], PRE[n][1] + c)
    TOK = {0: 0, 2: 1, 4: 2}

    def att_units(p):
        units = []

        def full(q, k, bias, **kw):
            units.append(dict(q=q, k=[k[:, 0:P], k[:, 0:T]],
                              blocks=[(0, P), (P, T)], bias=bias,
                              tiles=[(0, P), (P, P), (2 * P, P)], init=3e38, cmp=False, **kw))

        if p == 0:
            for h in range(DIFF_H):
                for m in range(2):
                    lo = m * HD
                    v = [dv[:, tb, h * P:(h + 1) * P] for tb in range(TB)]
                    full(dqk[lo:lo + HD, h, :], dqk[lo:lo + HD, 4 + h, :],
                         [nb[:, NSA_H + h, P:T], nb[:, NSA_H + h, :]], diff=m, out=4 + h, rows=(0, P),
                         start=True, stop=True, last=True,
                         pv=None if m == 0 else [(v[0], P, (0, T), (0, T)), (v[1], P, (T, 384), (P, T))])
            for h in range(NSA_H):
                g, lo = h // 4, (h % 2) * HD
                q = aq[lo:lo + HD, h // 2, :]
                keys = kc[lo:lo + HD, g, :]
                end = CMP_BLOCK - 1
                vg = vc[:, g * HD:(g + 1) * HD]
                units.append(dict(
                    q=q, k=[keys[:, 0:NC0], keys], blocks=[(0, NC0), (P, NC)],
                    bias=[nb[:, h, P + end:P + end + (NC0 - 1) * CMP_STRIDE + 1:CMP_STRIDE],
                          nb[:, h, end:end + (NC - 1) * CMP_STRIDE + 1:CMP_STRIDE]],
                    tiles=[(0, NC0), (P, NC)], init=BIG / 10, cmp=True, gate=h, out=h // 2, rows=(lo, lo + HD),
                    start=True, stop=False, last=False,
                    pv=[(vg[0:NC0, :], NC0, (0, P), (0, P)), (vg[0:NC, :], NC, (P, T), (P, T))]))
                for b in range(2):
                    v = [sv[:, tb, b * P + g * HD:b * P + (g + 1) * HD] for tb in range(TB)]
                    full(q, skw[lo:lo + HD, b, g, :], [nb[:, h, P:T], nb[:, h, :]], gate=8 * (b + 1) + h,
                         out=h // 2, rows=(lo, lo + HD), start=False, stop=(b == 1), last=(b == 1 and h % 2 == 1),
                         pv=[(v[0], P, (0, T), (0, T)), (v[1], P, (T, 384), (P, T))])
        else:
            qk, vv = (mqk, mv) if p == 1 else (fqk, fv)
            for h in range(16):
                lo = (h % 2) * HD
                v = [vv[:, tb, h * HD:(h + 1) * HD] for tb in range(TB)]
                bias = [nb[:, h, P:T], nb[:, h, :]] if p == 1 else [nb2[:, h, 0:P], nb2[:, h, P:384]]
                full(qk[lo:lo + HD, h // 2, :], qk[lo:lo + HD, 8 + h // 2, :], bias, out=h // 2, rows=(lo, lo + HD),
                     start=True, stop=True, last=(h % 2 == 1),
                     pv=[(v[0], P, (0, T), (0, T)), (v[1], P, (T, 384), (P, T))])
        n = 0
        for i, u in enumerate(units):
            u["i"] = i
            u["n"] = n
            u["seq"] = u["out"] if p else (u["out"] + DIFF_H) % (2 * DIFF_H)
            if u["pv"] is not None:
                n += 1
            u["n_done"] = n
        return units

    UNITS = [att_units(p) for p in range(3)]

    def freed_by(units, i):
        u = units[i - PB]
        return u["n_done"] if u["pv"] is not None else None

    def raw_extra(slot, j):
        return 16 * sum(1 for s in (1, 4) if s % RING == slot and s <= j)

    def fcol(tap, i, ch):
        if isinstance(i, int):
            return fw[:, tap, 4 * i + ch:4 * i + ch + 1]
        return fw[:, tap, bass.ds(i * 4 + ch, 1)]

    def conv_cols(i, j, c):
        ch = (j % 2) * NH2 + 2 * (j // 2) + c
        return fcol(2, i, ch), fcol(3, i, ch)

    block = ctx.enter_context(nc.Block())

    @block.sync
    def _(sp):
        def slab(s, j, src, k=KS, n=NS):
            if not (isinstance(s, int) and s < RING):
                sp.wait_ge(w_ready, s - RING + 1)
            dst = raw[:, j % RING, 0:k, 0:n]
            if len(src.shape) == 4:
                dst = dst.rearrange("p k (a b) -> p k a b", a=2)
            sp.dma_start(dst, src).then_inc(raw_in[j % RING], 16)

        def rows(w):
            return w.rearrange("(k p) n -> p k n", p=P)

        w_a = rows(t["ev_w_in"][0])

        def a_slab(j):
            s = st["a_in"].s0 + j
            if j in (1, 4):
                c0 = 768 if j == 1 else 896
                for half in range(2):
                    if half == 0 and s >= RING:
                        sp.wait_ge(w_ready, s - RING + 1)
                    sp.dma_start(raw[:, s % RING, :, half * P:(half + 1) * P],
                                 w_a[:, :, c0 + half * 2 * P:c0 + half * 2 * P + P]).then_inc(raw_in[s % RING], 8 * 2)
                return
            c0 = {0: 512, 2: 0, 3: 256, 5: 1280, 6: 1304, 7: 1560, 8: 1816, 9: 2072, 10: 2328, 11: 2584}[j]
            n = GATES if j == 5 else NS
            slab(s, s, w_a[:, :, c0:c0 + n], n=n)

        for tb in range(TB):
            sp.dma_start(xin[:, tb, :], t["x"][0, tb * P:(tb + 1) * P, :]).then_inc(ld["x"], 16)
        for j in range(RING):
            a_slab(j)
        for name, (tile, row, n) in PARAMS.items():
            if name != "norm_mix":
                src, letters = t[name], " ".join("abcd"[:len(t[name].shape)])
                if len(src.shape) > 1:
                    src = src.rearrange(f"{letters} -> ({letters})")
                sp.dma_start(prow[row:row + n, tile, :], src[0:n * P].rearrange("(r c) -> r c", c=P)).then_inc(ld["par"], 16)
        tail = t["conv_f_w_2"].rearrange("a b c -> (a b c)")[P * P:144 * P].rearrange("(r c) -> r c", c=P)
        sp.dma_start(prow[CONV_F_TAIL[1]:CONV_F_TAIL[1] + 16, CONV_F_TAIL[0], :], tail).then_inc(ld["par"], 16)
        sp.dma_start(buck[:, :], t["bucket"]).then_inc(ld["bias"], 16)
        sp.dma_start(btab[:, :], t["bias_table"]).then_inc(ld["bias"], 16)
        for i, name in enumerate(("ev_lam_q1", "ev_lam_k1", "ev_lam_q2", "ev_lam_k2")):
            sp.dma_start(lamv[:, i, :], t[name].to_broadcast([P, HD])).then_inc(ld["lam"], 16)
        for j in range(RING, 6):
            a_slab(j)
        for i, name in enumerate(("k", "v")):
            sp.dma_start(cw1[:, i, :, :], t[f"ev_cmp_w1_{name}"][0].rearrange("(m p) j -> p m j", p=P)).then_inc(ld["cw"], 16)
            for half in range(2):
                sp.dma_start(cw2[:, i, half * HD:(half + 1) * HD], t[f"ev_cmp_w2_{name}"][0]).then_inc(ld["cw"], 16)
        for j in range(6, 8):
            a_slab(j)
        sp.wait_ge(brow_ok, 1)
        sp.dma_start(scr_b, brow[:, :]).then_inc(brow_out, 16)
        sp.wait_ge(brow_out, 16)
        sp.dma_start(scr_w, bass.AP(tensor=scr_b.tensor, offset=0, ap=[[0, 16], [1, 16 * REL]])).then_inc(brow_out, 16)
        sp.wait_ge(brow_out, 32)

        def load_bias():
            for a in range(P // 16):
                src = bass.AP(tensor=scr_w.tensor, offset=P - 1 - 16 * a, ap=[[16 * REL - 1, 16], [REL, 16], [1, T]])
                sp.dma_start(nb[16 * a:16 * a + 16, :, :], src).then_inc(nb_in, 16)

        load_bias()
        sp.dma_start(b_f, t["b_forget_2"].rearrange("a h -> h a"),).then_inc(ld["bf"], 16)
        for j in range(8, 12):
            a_slab(j)

        def cols(name, w, n, body):
            s0 = st[name].s0
            with sp.Fori(0, n // body) as i:
                for j in range(body):
                    slab(s0 + i * body + j, s0 + j, w[:, :, bass.ds(i * (body * NS) + j * NS, NS)])

        def groups(name, w, per, k, body):
            s0, n = st[name].s0, st[name].n
            with sp.Fori(0, n // body) as i:
                for j in range(body):
                    g, r = j // per, j % per
                    slab(s0 + i * body + j, s0 + j,
                         w[:, r * k:(r + 1) * k, bass.ds(i * (body // per * NS) + g * NS, NS)], k=k)

        for l, (pre, wi, wo) in enumerate((("a", None, "ev_w_out"), ("m", "od_w_in", "od_w_out"))):
            if wi:
                cols(pre + "_in", rows(t[wi][0]), 12, 4)
                sp.wait_ge(slab_done, st["m_in"].s0)
                load_bias()
            for j in range(4):
                s = st[pre + "_out"].s0 + j
                slab(s, s, rows(t[wo][0])[:, :, j * NS:(j + 1) * NS])
            cols(pre + "_up", rows(t["mlp_w1"][l]), 16, 4)
            groups(pre + "_dn", rows(t["mlp_w2"][l]), 4, KS, 8)
        w_r = rows(t["w_in_2"][0])
        for j in range(5):
            s = st["r_xa"].s0 + j
            slab(s, s, w_r[:, :, j * NS:(j + 1) * NS])

        def load_gates():
            sp.wait_ge(gz, 1)
            for i, name in enumerate(("w_rg_a_2", "w_rg_x_2")):
                for (c, r, n, b, r0) in pieces[:len(pieces) // 2]:
                    first = b * RNN_BLOCK - (c - 1) * P
                    sp.dma_start(gw[r:r + n, i, :, :, :].rearrange("p (h c) a b -> p h c (a b)", h=2)
                                 [:, :, c, first:first + RNN_BLOCK],
                                 t[name][0].rearrange("(h b) r c -> r h b c", h=2)[r0:r0 + n, :, b, :])\
                        .then_inc(ld["gw"], 16)

        QKV = 2 * D_RNN
        GA = QKV + 3 * D + ATT_H
        s = st["r_f"].s0
        slab(s, s, w_r[:, :, QKV + 3 * D:GA], n=ATT_H)
        for j in range(8):
            s = st["r_gate"].s0 + j
            c0 = GA + (j + 4) % 8 * NS
            slab(s, s, w_r[:, :, c0:c0 + NS])
            if j == 0:
                load_gates()
        for j in range(5):
            s = st["r_ga"].s0 + j
            slab(s, s, w_r[:, :, D_RNN + j * NS:D_RNN + (j + 1) * NS])
        for j in range(4):
            s = st["r_v"].s0 + j
            slab(s, s, w_r[:, :, QKV + 2 * D + j * NS:QKV + 2 * D + (j + 1) * NS])
        groups("r_pa", rows(t["w_proj_a_2"][0]), 2, NR // 2, 8)
        cols("r_qk", w_r[:, :, QKV:QKV + 2 * D], 8, 4)
        for name, w in (("r_pb", "w_proj_b_2"), ("r_out", "w_out_2")):
            for j in range(4):
                s = st[name].s0 + j
                slab(s, s, rows(t[w][0])[:, :, j * NS:(j + 1) * NS])
        w_u = rows(t["w_up_2"][0]).rearrange("p k (v n) -> p k v n", v=2)
        with sp.Fori(0, 6) as i:
            for j in range(4):
                slab(st["f_up"].s0 + i * 4 + j, st["f_up"].s0 + j,
                     w_u[:, :, j % 2, bass.ds(i * 2 * NS + j // 2 * NS, NS)])
        groups("f_dn", rows(t["w_down_2"][0]), 3, KS, 12)
        for gi in range(4):
            sp.wait_ge(oc, gi + 1)
            sp.dma_start(out[0].rearrange("(b p) n -> p b n", p=P)[:, :, gi * NS:(gi + 1) * NS],
                         xout[:, :, gi * NS:(gi + 1) * NS]).then_inc(o_out, 16)
        sp.wait_ge(o_out, 64)

    @block.gpsimd
    def _(pool):
        chain = [1]
        pool.memset(ident[:, :], 0.0).then_inc(pool_c, 1)
        pool.memset(eps_ones[:, :], EPS).then_inc(epso, 1)
        pool.memset(ones[:, :], 1.0).then_inc(idn, 1)
        pool.wait_ge(pool_c, 1)
        pool.affine_select(out=ident[:, :], in_=ident[:, :], compare_op=ALU.not_equal, fill=1.0, base=0,
                           pattern=[[-1, P]], channel_multiplier=1).then_inc(idn, 1)

        def link(ins):
            chain[0] += 1
            ins.then_inc(pool_c, 1)
            pool.wait_ge(pool_c, chain[0])

        def squares(n, src=x):
            if n:
                pool.wait_ge(stat_ok, n)
            for gi in range(4):
                pool.wait_ge(*x_ready(n, gi))
                dst = sq[:, 0, :, :] if gi else sq_sum[:, 0, :, :]
                v = src[:, 2 * gi:2 * gi + 2, :]
                ins = pool.tensor_tensor(dst, v, v, ALU.mult)
                if gi:
                    link(ins)
                    ins = pool.tensor_tensor(sq_sum[:, 0, :, :], sq_sum[:, 0, :, :], sq[:, 0, :, :], ALU.add)
                if n == 4:
                    link(ins)
                    pool.wait_ge(sqg, gi + 1)
                    if gi == 0:
                        ins = pool.tensor_copy(sq_sum[:, 1, :, :], sq[:, 1, :, :])
                    else:
                        ins = pool.tensor_tensor(sq_sum[:, 1, :, :], sq_sum[:, 1, :, :], sq[:, 1, :, :], ALU.add)
                if gi < 3 and n == 4:
                    ins.then_inc(sqg_used, 1)
                    pool.wait_ge(sqg_used, gi + 1)
                elif gi < 3:
                    link(ins)
                else:
                    ins.then_inc(sq_ok, 1)

        squares(0)
        pool.wait_ge(nb_in, 128)
        pool.affine_select(out=nb[:, :, P:T], in_=nb[:, :, P:T], compare_op=ALU.is_ge, fill=BIG, base=0,
                           pattern=[[0, 16], [-1, P]], channel_multiplier=1).then_inc(nb_ok, 1)
        squares(1)
        squares(2)
        pool.wait_ge(nb_in, 256)
        pool.affine_select(out=nb[:, :, P:T], in_=nb[:, :, P:T], compare_op=ALU.is_ge, fill=BIG, base=0,
                           pattern=[[0, 16], [-1, P]], channel_multiplier=1).then_inc(nb_ok, 1)
        squares(3)
        squares(4)
        pool.wait_ge(slab_done, st["m_dn"].s0 + st["m_dn"].n)
        pool.memset(xap[:, :, 0:CONV_A - 1], 0.0).then_inc(zero_pad, 1)
        for i in range(2):
            ins = pool.memset(gw[:, i, :, :, :], 0.0)
        ins.then_inc(gz, 1)
        for j in range(NR):
            pool.wait_ge(rg["sig"], j + 1)
            pool.tensor_tensor(rix[:, j, :], rix[:, j, :], xc[:, j, :], ALU.mult).then_inc(rg["ix"], 1)
        for h in range(2):
            pool.wait_ge(rg["sq"], h + 1)
            c = slice(h * NR // 2, (h + 1) * NR // 2)
            link(pool.tensor_tensor(rt[:, c, :], rt[:, c, :], rr[:, c, :], ALU.mult))
            pool.tensor_tensor(rt[:, c, :], rt[:, c, :], rix[:, c, :], ALU.mult).then_inc(rg["b2"], 1)
        pool.wait_ge(fin_, 32)
        pool.wait_ge(fcq_ok, 1)
        for c0, n, b in ((0, P, 0), (P, T, 1)):
            link(pool.tensor_tensor(nb2[:, :, c0:c0 + n], nb2[:, :, c0:c0 + n],
                                    fcq[:, b, :].unsqueeze(2).to_broadcast([P, 16, n]), ALU.subtract))
            pool.affine_select(out=nb2[:, :, 2 * c0:2 * c0 + P], in_=nb2[:, :, 2 * c0:2 * c0 + P],
                               compare_op=ALU.is_ge, fill=BIG, base=0, pattern=[[0, 16], [-1, P]],
                               channel_multiplier=1).then_inc(fnb, 1)
        squares(5, mo)
        pool.wait_ge(slab_done, st["r_out"].s0 + 4)
        pool.memset(upad[:, :, :, 0:CONV_F - 1], 0.0).then_inc(zero_pad, 1)
        squares(6)

        def product(q, b):
            pool.wait_ge(fug, q + 1)
            pool.wait_ge(fud, q * 8 + 8)
            pool.tensor_tensor(hp[:, b, :, :], ucv[:, 0, :, :], ucv[:, 1, :, :], ALU.mult).then_inc(fup, 1)

        for q in range(2):
            product(q, q)
        with pool.Fori(1, 6) as i:
            for b in range(2):
                pool.wait_ge(ful, i * 2 + b - 1)
                product(i * 2 + b, b)
        squares(7, fo)

    @block.scalar
    def _(act):
        def split_hi(s, j):
            if isinstance(s, int) and s >= n_slabs:
                return
            slot = j % RING
            extra = raw_extra(slot, j)
            act.wait_ge(raw_in[slot], (s - j + (j // RING + 1) * RING) * (16 // RING) + extra)
            if not (isinstance(s, int) and s < RING):
                act.wait_ge(slab_done, s - RING + 1)
            act.activation(w_hi[:, slot, :, :], raw[:, slot, :, :], ACT.Copy).then_inc(hi_done, 1)

        def split_x(n):
            for gi in range(4):
                act.wait_ge(*x_ready(n, gi))
                for c in (2 * gi, 2 * gi + 1):
                    ins = act.activation(act_hi[:, c, :], x[:, c, :], ACT.Copy, scale=gain(n, c))
                ins.then_inc(xh, 1)
                if n == 4:
                    if gi:
                        act.wait_ge(sqg_used, gi)
                    for c in (2 * gi, 2 * gi + 1):
                        ins = act.activation(sq[:, 1, c % 2, :], x[:, c, :], ACT.Square, scale=col("norm_final", c))
                    ins.then_inc(sqg, 1)

        def root(n):
            act.wait_ge(stat_ok, n + 1)
            act.activation(sd[:, :], ps_s[:, 0, 0:T], ACT.Sqrt, scale=1.0 / D, bias=eps2_c if n == 4 else eps_c)\
                .then_inc(sd_ok, 1)

        def tok(s, g, dst, func=ACT.Copy, n=NS):
            act.wait_ge(slab_done, s + 1)
            for tb in range(TB):
                ins = act.activation(dst[:, tb, :], ps_g[:, g % 2, tb * NS:tb * NS + n], func, scale=rs_tok[:, tb:tb + 1])
            ins.then_inc(emptied[g % 2], 1)

        def attention(p):
            a, units = att[p], UNITS[p]
            n_units = len(units)
            for i in range(n_units + LAG_HI):
                if i < n_units:
                    u = units[i]
                    act.wait_ge(a["logit"], i + 1)
                    for b, (c0, n) in enumerate(u["blocks"]):
                        v = prob[:, i % PB, c0:c0 + n]
                        ins = act.activation(v, v, ACT.Exp, scale=-1.0, bias=nmin[:, i, b:b + 1],
                                             accum_out=psum_[:, i, b:b + 1])
                    ins.then_inc(a["prob"], 1)
                if LAG_T <= i < n_units + LAG_T and units[i - LAG_T]["pv"] is not None:
                    u = units[i - LAG_T]
                    n = u["n"]
                    act.wait_ge(a["tr"], n + 1)
                    if n >= 2:
                        act.wait_ge(a["pv"], n - 1)
                    pt_ = prob_ts[p // 2]
                    if u["cmp"]:
                        act.activation(pt_[0:NC0, n % 2, 0:P], ps_t[0:NC0, n % 2, 0:P], ACT.Copy)
                        act.activation(pt_[0:NC, n % 2, P:T], ps_t[0:NC, n % 2, P:T], ACT.Copy).then_inc(a["trc"], 1)
                    else:
                        act.activation(pt_[:, n % 2, :], ps_t[:, n % 2, 0:384], ACT.Copy).then_inc(a["trc"], 1)
                if i >= LAG_HI and units[i - LAG_HI]["pv"] is not None and units[i - LAG_HI]["last"]:
                    u = units[i - LAG_HI]
                    act.wait_ge(a["pv"], u["n"] + 1)
                    o = u["out"]
                    dst = dob[:, o - 4, :] if "diff" in u else (mix_hi if p < 2 else act_hi)[:, o, :]
                    act.activation(dst, ps_o[:, u["seq"] % 2, 0:T], ACT.Copy).then_inc(a["oh"], 1)
                    if "diff" in u:
                        act.wait_ge(a["oh"], o - 3)
                        act.activation(dsq[:, o - 4, :], dob[:, o - 4, :], ACT.Square).then_inc(dn["sq"], 1)
                if p == 0 and i == DN_ROOT:
                    act.wait_ge(dn["ps"], DIFF_H)
                    act.activation(dsq[:, :, :].rearrange("p (a b) n -> p a (b n)", a=2), ps_g[:, :, :], ACT.Sqrt,
                                   scale=1.0 / P, bias=eps_c).then_inc(dn["sd"], 1)
                if p == 0 and i in DN_HI:
                    h = DN_HI.index(i)
                    act.wait_ge(dn["o2"], h + 1)
                    act.activation(mix_hi[:, 4 + h, :], dob[:, h, :], ACT.Copy).then_inc(dn["hi"], 1)

        n = PARAMS["norm_mix"][2]
        act.dma_start(prow[0:n, 0, :], t["norm_mix"].rearrange("a (r c) -> (a r) c", c=P)).then_inc(ld["g"], 16)
        split_hi(0, 0)
        act.wait_ge(par_ok, 1)
        split_x(0)
        for s in range(1, AHEAD):
            split_hi(s, s)
        root(0)
        for s in range(12):
            split_hi(s + AHEAD, s + AHEAD)
            g = st["a_in"].g0 + s
            if s in (4, 5, 10, 11):
                if s == 4:
                    act.wait_ge(rst_ok, 1)
                dst = {4: sv[:, :, :], 5: gates[:, :, :], 10: dv[:, :, 0:NS], 11: dv[:, :, NS:2 * NS]}[s]
                tok(s, g, dst, ACT.Sigmoid if s == 5 else ACT.Copy, GATES if s == 5 else NS)
            if s == CMP_STEP + 1:
                act.wait_ge(cmp_ps, 1)
                for i in range(2):
                    ins = act.activation(cposb[:, i:i + 1], ps_s[:, i, 2 * NC:2 * NC + 1], ACT.Copy)
                ins.then_inc(cmp_b, 1)
                act.wait_ge(cmp_b, 1)
                for i in range(2):
                    ins = act.activation(chid[:, i, :], ps_s[:, i, 0:2 * NC], ACT.Gelu_apprx_tanh, bias=cposb[:, i:i + 1])
                ins.then_inc(cmp_h, 1)
        act.wait_ge(lam_ok, 1)
        act.activation(small[:, 6:8], small[:, 6:8], ACT.Exp).then_inc(lam_e, 1)
        attention(0)
        def out_stage(name, n):
            for j in range(4):
                s = st[name].s0 + j
                split_hi(s + AHEAD, s + AHEAD)
            split_x(n)

        def mlp_up(name, n):
            root(n)
            s0, g0 = st[name].s0, st[name].g0
            with act.Fori(0, 4) as i:
                for j in range(4):
                    split_hi(s0 + i * 4 + j + AHEAD, s0 + j + AHEAD)
                    g = g0 + j
                    act.wait_ge(emptied[g % 2], out_count(g) + i * 2)
                    act.activation(hid_hi[:, bass.ds(i * 8 + j * 2, 2), :], up_r[:, j % 2, :, :], ACT.Square)\
                        .then_inc(hid_h, 1)

        def mlp_dn(name, n):
            s0 = st[name].s0
            with act.Fori(0, 2) as i:
                for j in range(8):
                    split_hi(s0 + i * 8 + j + AHEAD, s0 + j + AHEAD)
            if n in PRE:
                split_x(n)

        out_stage("a_out", 1)
        mlp_up("a_up", 1)
        mlp_dn("a_dn", 2)
        root(2)
        with act.Fori(0, 2) as i:
            for j in range(4):
                split_hi(st["m_in"].s0 + i * 4 + j + AHEAD, st["m_in"].s0 + j + AHEAD)
        act.wait_ge(rst_ok, 2)
        for j in range(4):
            s = st["m_in"].s0 + 8 + j
            split_hi(s + AHEAD, s + AHEAD)
            tok(s, st["m_in"].g0 + 8 + j, mv[:, :, j * NS:(j + 1) * NS])
        attention(1)
        out_stage("m_out", 3)
        mlp_up("m_up", 3)
        mlp_dn("m_dn", 4)
        act.wait_ge(sp_d, 1)
        act.activation(spw[:, 0:10], spw[:, 0:10], ACT.Exp).then_inc(sp_a, 1)
        root(4)
        act.wait_ge(rst_ok, 3)
        act.activation(rs_f[:, :], ps_s[:, 1, T:2 * T], ACT.Sqrt, scale=1.0 / D, bias=eps_c).then_inc(sdf, 1)
        for j in range(5):
            s = st["r_xa"].s0 + j
            split_hi(s + AHEAD, s + AHEAD)
            act.wait_ge(emptied[(st["r_xa"].g0 + j) % 2], out_count(st["r_xa"].g0 + j))
            for c in (2 * j, 2 * j + 1):
                ins = act.activation(xc[:, c, :], xap[:, c, CONV_A - 1:], ACT.Identity,
                                     scale=col("conv_a_w_2", (CONV_A - 1) * NR + c), bias=col("conv_a_b_2", c))
            ins.then_inc(cva, 1)
        split_hi(st["r_f"].s0 + AHEAD, st["r_f"].s0 + AHEAD)
        act.wait_ge(fz, 1)
        act.wait_ge(ld["bf"], 16)
        act.activation(fl[:, 1, :], fl[:, 0, :], ACT.Identity, bias=b_f).then_inc(fa, 1)
        act.wait_ge(fz, 2)
        act.activation(fl[:, 3, :], fl[:, 3, :], ACT.Exp).then_inc(fa, 1)
        act.wait_ge(fa, 2)
        act.activation(fl[:, 4, :], fl[:, 3, :], ACT.Ln, bias=one_c[0:16, :]).then_inc(fa, 1)
        act.wait_ge(fcum, 1)
        act.dma_start(scr_c, fl[:, 5, :]).then_inc(fout, 16)
        for j in range(8):
            s = st["r_gate"].s0 + j
            split_hi(s + AHEAD, s + AHEAD)
            g = st["r_gate"].g0 + j
            act.wait_ge(emptied[g % 2], out_count(g))
            for c in (2 * (j % 4), 2 * (j % 4) + 1):
                dst = (sga if j >= 4 else sgb)[:, c, :]
                ins = act.activation(dst, dst, ACT.Sigmoid, bias=col("b_merge_2", c + (0 if j >= 4 else NX)))
            ins.then_inc(gs2, 1)
            if j == RG_STEP:
                act.wait_ge(sp_d, 2)
                for j in range(NR):
                    act.wait_ge(rg["ps"], j + 1)
                    act.activation(rt[:, j, :], ps_s[:, j % 2, 0:T], ACT.Sigmoid, bias=col("b_rg_a_2", j)).then_inc(act_c, 1)
                    act.activation(rix[:, j, :], ps_s[:, j % 2, T:2 * T], ACT.Sigmoid, bias=col("b_rg_x_2", j)).then_inc(rg["sig"], 1)
                    act.wait_ge(act_c, j + 1)
                    act.activation(rt[:, j, :], rt[:, j, :], ACT.Tanh, scale=sp4[:, j:j + 1]).then_inc(rg["den"], 1)
            if j in (4, 7):
                h = (j - 4) // 3
                act.wait_ge(rg["a"], h + 1)
                v = rt[:, h * NR // 2:(h + 1) * NR // 2, :]
                act.activation(v, v, ACT.Sqrt, scale=4.0).then_inc(rg["sq"], 1)
        for j in range(5):
            s = st["r_ga"].s0 + j
            split_hi(s + AHEAD, s + AHEAD)
            g = st["r_ga"].g0 + j
            act.wait_ge(emptied[g % 2], out_count(g))
            act.activation(gt[:, j % 2, :, :], gt[:, j % 2, :, :], ACT.Gelu_apprx_tanh).then_inc(yg, 1)
            act.wait_ge(yy, j + 1)
            act.activation(ya_hi[:, 2 * j:2 * j + 2, :], gt[:, j % 2, :, :], ACT.Copy).then_inc(yh, 1)
        act.wait_ge(rg["h"], 2)
        for j in range(4):
            s = st["r_v"].s0 + j
            split_hi(s + AHEAD, s + AHEAD)
            tok(s, st["r_v"].g0 + j, fv[:, :, j * NS:(j + 1) * NS])
        for j in range(8):
            split_hi(st["r_pa"].s0 + j + AHEAD, st["r_pa"].s0 + j + AHEAD)
        act.wait_ge(fout, 16)
        act.wait_ge(slab_done, st["r_qk"].s0)
        for c0, n in ((0, P), (P, T)):
            act.dma_start(nb2[:, :, c0:c0 + n], bass.AP(tensor=scr_c.tensor, offset=0, ap=[[0, P], [T, 16], [1, n]]))\
                .then_inc(fin_, 16)
        with act.Fori(0, 2) as i:
            for j in range(4):
                split_hi(st["r_qk"].s0 + i * 4 + j + AHEAD, st["r_qk"].s0 + j + AHEAD)
        attention(2)
        for j in range(4):
            s = st["r_pb"].s0 + j
            split_hi(s + AHEAD, s + AHEAD)
            g = st["r_pb"].g0 + j
            act.wait_ge(emptied[g % 2], out_count(g))
            act.activation(m2_hi[:, 2 * j:2 * j + 2, :], mg[:, 2 * j:2 * j + 2, :], ACT.Copy).then_inc(pbh, 1)
        for j in range(4):
            s = st["r_out"].s0 + j
            split_hi(s + AHEAD, s + AHEAD)
        root(5)
        split_x(6)
        root(6)
        s0, g0 = st["f_up"].s0, st["f_up"].g0

        def hi_of(q, b):
            act.wait_ge(fup, q + 1)
            act.activation(h2_hi[:, bass.ds(q * 2, 2) if not isinstance(q, int) else slice(2 * q, 2 * q + 2), :],
                           hp[:, b, :, :], ACT.Copy).then_inc(fuh, 1)

        def up_step(i, j, first=False):
            split_hi(s0 + i * 4 + j + AHEAD, s0 + j + AHEAD)
            if j % 2:
                act.wait_ge(fud, i * 16 + j * 4)
                act.activation(ucv[:, 0, :, :], ucv[:, 0, :, :], ACT.Gelu_apprx_tanh).then_inc(fug, 1)
            elif not first:
                hi_of(i * 2 + j // 2 - 1, (j // 2 + 1) % 2)
            g = g0 + j
            act.wait_ge(emptied[g % 2], out_count(g) + i * 2)
            for c in range(2):
                wcol, bcol = conv_cols(i, j, c)
                ins = act.activation(ucv[:, j % 2, c, :], upad[:, j % 2, c, CONV_F - 1:], ACT.Identity,
                                     scale=wcol, bias=bcol)
            ins.then_inc(fuc, 1)

        for j in range(4):
            up_step(0, j, first=(j == 0))
        with act.Fori(1, 6) as i:
            for j in range(4):
                up_step(i, j)
        hi_of(11, 1)
        for j in range(12):
            split_hi(st["f_dn"].s0 + j + AHEAD, st["f_dn"].s0 + j + AHEAD)
        root(7)
        for gi in range(4):
            act.wait_ge(ot, gi + 1)
            act.activation(xout[:, :, gi * NS:(gi + 1) * NS], ps_g[:, gi % 2, :].rearrange("p (b n) -> p b n", b=TB),
                           ACT.Copy).then_inc(oc, 1)

    @block.vector
    def _(dve):
        chain = [0]

        def link(ins):
            chain[0] += 1
            ins.then_inc(dve_c, 1)
            dve.wait_ge(dve_c, chain[0])

        def split_lo(s, j):
            if isinstance(s, int) and s >= n_slabs:
                return
            slot = j % RING
            dve.wait_ge(hi_done, s + 1)
            dve.tensor_tensor(w_lo[:, slot, :, :], raw[:, slot, :, :], w_hi[:, slot, :, :].bitcast(F32), ALU.subtract)\
                .then_inc(w_ready, 1)

        def split_x(n):
            for gi in range(4):
                dve.wait_ge(xh, PRE_I[n] * 4 + gi + 1)
                for c in (2 * gi, 2 * gi + 1):
                    ins = dve.scalar_tensor_tensor(out=act_lo[:, c, :], in0=x[:, c, :], scalar=gain(n, c),
                                                   in1=act_hi[:, c, :].bitcast(F32), op0=ALU.mult, op1=ALU.subtract)
                ins.then_inc(xl, 1)

        def inv_rms(n):
            dve.wait_ge(sd_ok, n + 1)
            dve.reciprocal(rs[:, 1, :], sd[:, :]).then_inc(rs_ok, 1)
            dve.wait_ge(rs_ok, n + 1)
            if n in TOK:
                dve.tensor_scalar(rs[:, 0, :], rs[:, 1, :], -0.125, None, ALU.mult).then_inc(rsq_ok, 1)
                dve.wait_ge(rst_ps, TOK[n] + 1)
                dve.tensor_copy(rs_tok[:, :], ps_s[:, 1, 0:TB]).then_inc(rst_ok, 1)
                dve.wait_ge(rsq_ok, TOK[n] + 1)

        def bcast(ap, n=2):
            return ap.unsqueeze(1).to_broadcast([P, n, T])

        def pair(g):
            return ps_g[:, g % 2, :].rearrange("p (a n) -> p a n", a=2)

        def attention(p):
            a, units = att[p], UNITS[p]
            n_units = len(units)
            for i in range(n_units + LAG_LO):
                if i < n_units:
                    u = units[i]
                    dve.wait_ge(a["score"], i + 1)
                    if i >= PB and freed_by(units, i):
                        dve.wait_ge(a["tr"], freed_by(units, i))
                    for b, (c0, n) in enumerate(u["blocks"]):
                        ins = dve.tensor_tensor_reduce(
                            out=prob[:, i % PB, c0:c0 + n], in0=ps_s[:, i % 2, c0:c0 + n], in1=u["bias"][b],
                            scale=1.0, scalar=u["init"], op0=ALU.add, op1=ALU.min, accum_out=nmin[:, i, b:b + 1])
                    ins.then_inc(a["logit"], 1)
                if LAG_N <= i < n_units + LAG_N:
                    k = i - LAG_N
                    u = units[k]
                    dve.wait_ge(a["prob"], k + 1)
                    if u["cmp"]:
                        link(dve.tensor_scalar(psum_[:, k, :], psum_[:, k, :], 1e-30, None, ALU.max))
                    link(dve.reciprocal(fac[:, k, :], psum_[:, k, :]))
                    if "gate" in u:
                        link(dve.tensor_tensor(fac[:, k, :], fac[:, k, :], gates[:, :, u["gate"]], ALU.mult))
                    if u.get("diff") == 1:
                        link(dve.tensor_scalar(fac[:, k, :], fac[:, k, :], lamn, None, ALU.mult))
                    for b, (c0, n) in enumerate(u["blocks"]):
                        v = prob[:, k % PB, c0:c0 + n]
                        if u.get("diff") == 1:
                            ins = dve.scalar_tensor_tensor(out=v, in0=v, scalar=fac[:, k, b:b + 1],
                                                           in1=prob[:, (k - 1) % PB, c0:c0 + n], op0=ALU.mult, op1=ALU.add)
                        else:
                            ins = dve.tensor_scalar(v, v, fac[:, k, b:b + 1], None, ALU.mult)
                    if u.get("diff") == 0:
                        link(ins)
                    else:
                        ins.then_inc(a["norm"], 1)
                if i >= LAG_LO:
                    u = units[i - LAG_LO]
                    if u["pv"] is not None and u["last"] and "diff" not in u:
                        o, seq = u["out"], u["seq"]
                        hi, lo = (mix_hi, mix_lo) if p < 2 else (act_hi, act_lo)
                        dve.wait_ge(a["oh"], seq + 1)
                        dve.tensor_tensor(lo[:, o, :], ps_o[:, seq % 2, 0:T], hi[:, o, :].bitcast(F32), ALU.subtract)\
                            .then_inc(a["ol"], 1)
                if p == 0 and i in DN_R:
                    h = DN_R.index(i)
                    dve.wait_ge(dn["sd"], 1)
                    dve.reciprocal(dsq[:, h, :], dsq[:, h, :]).then_inc(dn["r"], 1)
                    dve.wait_ge(dn["r"], h + 1)
                    dve.scalar_tensor_tensor(out=dob[:, h, :], in0=dob[:, h, :], scalar=sub8, in1=dsq[:, h, :],
                                             op0=ALU.mult, op1=ALU.mult).then_inc(dn["o2"], 1)
                if p == 0 and i in DN_LO:
                    h = DN_LO.index(i)
                    dve.wait_ge(dn["hi"], h + 1)
                    dve.tensor_tensor(mix_lo[:, 4 + h, :], dob[:, h, :], mix_hi[:, 4 + h, :].bitcast(F32), ALU.subtract)\
                        .then_inc(dn["lo"], 1)

        dve.memset(eps_c, EPS)
        dve.memset(one_c, 1.0)
        link(dve.memset(eps2_c, EPS * EPS))
        dve.wait_ge(par_t, 1)
        n_gain = PARAMS["norm_mix"][2]
        dve.tensor_copy(par[:, 0, 0:n_gain], ps_t[:, 1, 0:n_gain]).then_inc(par_ok, 1)
        dve.wait_ge(par_ok, 1)
        for gi in range(4):
            dve.wait_ge(xt, gi + 1)
            dve.tensor_copy(x[:, 2 * gi:2 * gi + 2, :], pair(gi)).then_inc(emptied[gi % 2], 1)
        split_lo(0, 0)
        split_x(0)
        split_lo(1, 1)
        dve.wait_ge(ld["lam"], 64)
        for i in range(2):
            ins = dve.tensor_tensor_reduce(out=lamv[:, 2 * i, :], in0=lamv[:, 2 * i, :], in1=lamv[:, 2 * i + 1, :],
                                           scale=1.0, scalar=0.0, op0=ALU.mult, op1=ALU.add,
                                           accum_out=small[:, 6 + i:7 + i])
        ins.then_inc(lam_ok, 1)
        inv_rms(0)
        dve.wait_ge(par_t, 2)
        for k in range(4):
            c0 = n_gain if k == 0 else 0
            ins = dve.tensor_copy(par[:, k, c0:TILE_ROWS[k]], ps_t[:, 0, k * P + c0:k * P + TILE_ROWS[k]])
        ins.then_inc(par_ok, 1)
        dve.wait_ge(brow_ps, 1)
        dve.tensor_copy(brow[:, :], ps_o[0:16, 0, 0:REL]).then_inc(brow_ok, 1)
        dve.wait_ge(par_ok, 2)
        dve.tensor_scalar(sub8, col("ev_subln"), 1.0 - 0.2, None, ALU.mult)
        link(dve.memset(cmp2[:, :, 2, :], 0.0))
        dve.tensor_copy(cmp2[:, :, 2, 0:CMP_BLOCK:2], par[:, 3, 0:32].rearrange("p (i m) -> p i m", i=2))
        for j in range(CONV_F):
            for c0, c1 in ((0, 2 * NH2),):
                r = j * 2 * NH2
                if r + 2 * NH2 <= P:
                    dve.tensor_copy(fw[:, j, :], par[:, 2, r:r + 2 * NH2])
                else:
                    n = P - r
                    dve.tensor_copy(fw[:, j, 0:n], par[:, 2, r:P])
                    dve.tensor_copy(fw[:, j, n:], par[:, CONV_F_TAIL[0], CONV_F_TAIL[1]:CONV_F_TAIL[1] + 16])
        link(dve.tensor_copy(fw[:, 3, :], col("conv_f_b_2", 0, 2 * NH2)))
        dve.tensor_tensor(gain_f[:, :], col("norm_final", 0, NX), col("mix_norm_pre_2", 0, NX), ALU.mult).then_inc(gain_ok, 1)
        q_pair = bcast(rs[:, 0, :])
        k_pair = bcast(rs[:, 1, :])
        for s in range(12):
            split_lo(s + AHEAD - 1, s + AHEAD - 1)
            g = st["a_in"].g0 + s
            if s in (4, 5, 10, 11):
                continue
            dve.wait_ge(slab_done, s + 1)
            if s == 0:
                for i in range(2):
                    for gg in range(2):
                        rws = slice(gg * HD, (gg + 1) * HD)
                        dve.tensor_tensor(cmp2[0:HD, i, gg, :], ps_g[rws, g % 2, i * T:(i + 1) * T], rs[rws, 1, :], ALU.mult)
                        ins = dve.tensor_tensor(cmp2[HD:P, i, gg, 0:T - 1], ps_g[rws, g % 2, i * T + 1:(i + 1) * T],
                                                rs[rws, 1, 1:T], ALU.mult)
            elif s == 1:
                for i in range(2):
                    for gg in range(2):
                        rws = slice(gg * HD, (gg + 1) * HD)
                        for half in range(2):
                            ins = dve.tensor_tensor(skw[half * HD:(half + 1) * HD, i, gg, :],
                                                    ps_g[rws, g % 2, i * T:(i + 1) * T], rs[rws, 1, :], ALU.mult)
            elif s in (2, 3):
                ins = dve.tensor_tensor(aq[:, 2 * (s - 2):2 * (s - 2) + 2, :], pair(g), q_pair, ALU.mult)
            else:
                ins = dve.tensor_tensor(dqk[:, 2 * (s - 6):2 * (s - 6) + 2, :], pair(g), q_pair if s < 8 else k_pair, ALU.mult)
            ins.then_inc(emptied[g % 2], 1)
        dve.wait_ge(lam_e, 1)
        link(dve.tensor_tensor(lamn, small[:, 7:8], small[:, 6:7], ALU.subtract))
        link(dve.tensor_scalar(lamn, lamn, 0.2, None, ALU.subtract))
        dve.wait_ge(cmp_ps2, 1)
        dve.tensor_copy(kc[:, :, :], ps_s[:, 0, 128:128 + 2 * NC].rearrange("p (g c) -> p g c", g=2))
        dve.tensor_copy(vc[0:NC, :], ps_s[0:NC, 0, 256:384]).then_inc(cmp_ok, 1)
        dve.wait_ge(nb_ok, 1)
        attention(0)
        def add_x(g, gi):
            dve.tensor_tensor(x[:, 2 * gi:2 * gi + 2, :], pair(g), x[:, 2 * gi:2 * gi + 2, :], ALU.add)\
                .then_inc(emptied[g % 2], 1)

        def out_stage(name, n):
            for j in range(4):
                s, g = st[name].s0 + j, st[name].g0 + j
                split_lo(s + AHEAD - 1, s + AHEAD - 1)
                dve.wait_ge(slab_done, s + 1)
                add_x(g, j)
            split_x(n)

        def mlp_up(name, n, l):
            inv_rms(n)
            s0, g0 = st[name].s0, st[name].g0
            with dve.Fori(0, 4) as i:
                for j in range(4):
                    split_lo(s0 + i * 4 + j + AHEAD - 1, s0 + j + AHEAD - 1)
                    g = g0 + j
                    dve.wait_ge(slab_done, s0 + i * 4 + j + 1)
                    dve.scalar_tensor_tensor(out=up_r[:, j % 2, :, :], in0=pair(g), scalar=0.0, in1=k_pair, op0=ALU.max,
                                             op1=ALU.mult).then_inc(emptied[g % 2], 1)
                    dve.wait_ge(emptied[g % 2], out_count(g) + i * 2)
                    dve.tensor_tensor(up_q[:, j % 2, :, :], up_r[:, j % 2, :, :], up_r[:, j % 2, :, :], ALU.mult)\
                        .then_inc(upr, 1)
                    dve.wait_ge(upr, l * 16 + i * 4 + j + 1)
                    dve.wait_ge(hid_h, l * 16 + i * 4 + j + 1)
                    c = bass.ds(i * 8 + j * 2, 2)
                    dve.tensor_tensor(hid_lo[:, c, :], up_q[:, j % 2, :, :], hid_hi[:, c, :].bitcast(F32), ALU.subtract)\
                        .then_inc(hid_l, 1)

        def mlp_dn(name, n):
            s0, g0 = st[name].s0, st[name].g0
            with dve.Fori(0, 2) as i:
                for j in range(8):
                    split_lo(s0 + i * 8 + j + AHEAD - 1, s0 + j + AHEAD - 1)
                    if j % 4 == 3:
                        g = g0 + j // 4
                        dve.wait_ge(slab_done, s0 + i * 8 + j + 1)
                        c = bass.ds(i * 4 + j // 4 * 2, 2)
                        dve.tensor_tensor(x[:, c, :], pair(g), x[:, c, :], ALU.add).then_inc(emptied[g % 2], 1)
            if n in PRE:
                split_x(n)

        def qk_stage(name, dst):
            s0, g0 = st[name].s0, st[name].g0
            with dve.Fori(0, 2) as i:
                for j in range(4):
                    split_lo(s0 + i * 4 + j + AHEAD - 1, s0 + j + AHEAD - 1)
                    g = g0 + j
                    dve.wait_ge(slab_done, s0 + i * 4 + j + 1)
                    dve.tensor_tensor(dst[:, bass.ds(i * 8 + 2 * j, 2), :], pair(g),
                                      rs[:, bass.ds(i, 1), :].to_broadcast([P, 2, T]), ALU.mult).then_inc(emptied[g % 2], 1)

        out_stage("a_out", 1)
        mlp_up("a_up", 1, 0)
        mlp_dn("a_dn", 2)
        inv_rms(2)
        qk_stage("m_in", mqk)
        for j in range(4):
            s = st["m_in"].s0 + 8 + j
            split_lo(s + AHEAD - 1, s + AHEAD - 1)
        dve.wait_ge(nb_ok, 2)
        attention(1)
        out_stage("m_out", 3)
        mlp_up("m_up", 3, 1)
        mlp_dn("m_dn", 4)
        lam = col("lru_lambda_2", 0, 10)
        z, zz, s2, acc = (spw[:, 10 * k:10 * k + 10] for k in range(4))
        link(dve.tensor_scalar(zz, lam, -1.0, None, ALU.mult))
        dve.tensor_tensor(z, zz, lam, ALU.min).then_inc(sp_d, 1)
        dve.wait_ge(sp_a, 1)
        link(dve.tensor_scalar(zz, z, 2.0, None, ALU.add))
        link(dve.reciprocal(zz, zz))
        link(dve.tensor_tensor(z, z, zz, ALU.mult))
        link(dve.tensor_tensor(s2, z, z, ALU.mult))
        link(dve.tensor_scalar(acc, s2, 1.0 / 17, 1.0 / 15, ALU.mult, ALU.add))
        for k in (13, 11, 9, 7, 5, 3, 1):
            link(dve.tensor_tensor(acc, acc, s2, ALU.mult))
            link(dve.tensor_scalar(acc, acc, 1.0 / k, None, ALU.add))
        link(dve.tensor_tensor(acc, acc, z, ALU.mult))
        link(dve.tensor_scalar(zz, lam, -1.0, 0.0, ALU.mult, ALU.max))
        link(dve.scalar_tensor_tensor(out=acc, in0=acc, scalar=2.0, in1=zz, op0=ALU.mult, op1=ALU.add))
        dve.tensor_scalar(sp4, acc, 4.0, None, ALU.mult).then_inc(sp_d, 1)
        inv_rms(4)
        dve.wait_ge(zero_pad, 1)
        k = 0
        for j in range(5):
            s, g = st["r_xa"].s0 + j, st["r_xa"].g0 + j
            split_lo(s + AHEAD - 1, s + AHEAD - 1)
            dve.wait_ge(slab_done, s + 1)
            dve.tensor_tensor(xap[:, 2 * j:2 * j + 2, CONV_A - 1:], pair(g), k_pair, ALU.mult).then_inc(emptied[g % 2], 1)
            dve.wait_ge(cva, j + 1)
            dve.wait_ge(emptied[g % 2], out_count(g))
            for tap in range(CONV_A - 1):
                for c in (2 * j, 2 * j + 1):
                    if tap:
                        dve.wait_ge(cvd, k - 1)
                    dve.scalar_tensor_tensor(out=xc[:, c, :], in0=xap[:, c, tap:tap + T],
                                             scalar=col("conv_a_w_2", tap * NR + c), in1=xc[:, c, :], op0=ALU.mult,
                                             op1=ALU.add).then_inc(cvd, 1)
                    k += 1
        s, g = st["r_f"].s0, st["r_f"].g0
        split_lo(s + AHEAD - 1, s + AHEAD - 1)
        dve.wait_ge(slab_done, s + 1)
        dve.tensor_tensor(fl[:, 0, :], ps_g[0:16, g % 2, 0:T], rs[0:16, 1, :], ALU.mult).then_inc(fz, 1)
        dve.wait_ge(fa, 1)
        link(dve.tensor_scalar(fl[:, 2, :], fl[:, 1, :], 0.0, None, ALU.min))
        dve.scalar_tensor_tensor(out=fl[:, 3, :], in0=fl[:, 2, :], scalar=2.0, in1=fl[:, 1, :], op0=ALU.mult,
                                 op1=ALU.subtract).then_inc(fz, 1)
        dve.memset(fl[:, 0, :], 1.0).then_inc(emptied[g % 2], 1)
        dve.wait_ge(emptied[g % 2], out_count(g))
        dve.wait_ge(fa, 3)
        link(dve.tensor_tensor(fl[:, 2, :], fl[:, 2, :], fl[:, 4, :], ALU.subtract))
        dve.tensor_tensor_scan(fl[:, 5, :], fl[:, 0, :], fl[:, 2, :], 0.0, ALU.mult, ALU.add).then_inc(fcum, 1)
        dve.wait_ge(sdf, 1)
        dve.reciprocal(rs_f[:, :], rs_f[:, :]).then_inc(rsf, 1)
        dve.wait_ge(rsf, 1)
        for c in range(NX):
            ins = dve.scalar_tensor_tensor(out=x[:, c, :], in0=x[:, c, :], scalar=col("norm_final", c), in1=rs_f[:, :],
                                           op0=ALU.mult, op1=ALU.mult)
        ins.then_inc(x_mat, 1)

        def decay(j):
            dve.wait_ge(rg["den"], j + 1)
            dve.wait_ge(rg["ps"], min(j + 2, NR))
            dve.wait_ge(rg["ix"], j + 1)
            link(dve.tensor_scalar(rr[:, j, :], rt[:, j, :], 1.0, None, ALU.add))
            dve.reciprocal(rr[:, j, :], rr[:, j, :]).then_inc(rcp, 1)

        def decay_a(h):
            dve.wait_ge(rcp, (h + 1) * NR // 2)
            dve.wait_ge(rg["ps"], NR)
            c = slice(h * NR // 2, (h + 1) * NR // 2)
            dve.tensor_scalar(ra[:, c, :], rr[:, c, :], 2.0, -1.0, ALU.mult, ALU.add).then_inc(rg["a"], 1)

        def scan(h):
            dve.wait_ge(rg["b2"], h + 1)
            dve.wait_ge(rg["a"], h + 1)
            if h == 0:
                dve.wait_ge(rg["b2"], 1)
            for j in range(h * NR // 2, (h + 1) * NR // 2):
                ins = dve.tensor_tensor_scan(hr[:, j, :], ra[:, j, :], rt[:, j, :], 0.0, ALU.mult, ALU.add)
            ins.then_inc(rg["h"], 1)

        for j in range(8):
            s, g = st["r_gate"].s0 + j, st["r_gate"].g0 + j
            split_lo(s + AHEAD - 1, s + AHEAD - 1)
            dve.wait_ge(slab_done, s + 1)
            if j == 4:
                dve.wait_ge(fcq_ps, 1)
                dve.tensor_copy(fcq[:, :, :], ps_s[:, 0, 0:32].rearrange("p (b h) -> p b h", b=TB)).then_inc(fcq_ok, 1)
                dve.wait_ge(fout, 16)
            dst = (sga if j >= 4 else sgb)[:, 2 * (j % 4):2 * (j % 4) + 2, :]
            dve.tensor_tensor(dst, pair(g), k_pair, ALU.mult).then_inc(emptied[g % 2], 1)
            for k in {2: (0, 1, 2), 3: (3, 4), 4: (5, 6), 5: (7,), 6: (8,), 7: (9,)}.get(j, ()):
                decay(k)
            if j == 3:
                decay_a(0)
        decay_a(1)
        scan(0)
        for j in range(5):
            s, g = st["r_ga"].s0 + j, st["r_ga"].g0 + j
            split_lo(s + AHEAD - 1, s + AHEAD - 1)
            dve.wait_ge(slab_done, s + 1)
            if j == 0:
                scan(1)
                dve.wait_ge(rg["h"], 2)
            if j >= 2:
                dve.wait_ge(yl, j - 1)
            dve.tensor_tensor(gt[:, j % 2, :, :], pair(g), k_pair, ALU.mult).then_inc(emptied[g % 2], 1)
            dve.wait_ge(yg, j + 1)
            dve.tensor_tensor(gt[:, j % 2, :, :], gt[:, j % 2, :, :], hr[:, 2 * j:2 * j + 2, :], ALU.mult).then_inc(yy, 1)
            dve.wait_ge(yy, j + 1)
            dve.wait_ge(yh, j + 1)
            dve.tensor_tensor(ya_lo[:, 2 * j:2 * j + 2, :], gt[:, j % 2, :, :],
                              ya_hi[:, 2 * j:2 * j + 2, :].bitcast(F32), ALU.subtract).then_inc(yl, 1)
        for j in range(4):
            s = st["r_v"].s0 + j
            split_lo(s + AHEAD - 1, s + AHEAD - 1)
        dve.wait_ge(gs2, 8)
        for j in range(8):
            s, g = st["r_pa"].s0 + j, st["r_pa"].g0 + j // 2
            split_lo(s + AHEAD - 1, s + AHEAD - 1)
            if j % 2:
                dve.wait_ge(slab_done, s + 1)
                dve.tensor_tensor(mg[:, j - 1:j + 1, :], pair(g), sga[:, j - 1:j + 1, :], ALU.mult).then_inc(emptied[g % 2], 1)
        qk_stage("r_qk", fqk)
        dve.wait_ge(fnb, 2)
        attention(2)
        for j in range(4):
            s, g = st["r_pb"].s0 + j, st["r_pb"].g0 + j
            split_lo(s + AHEAD - 1, s + AHEAD - 1)
            dve.wait_ge(slab_done, s + 1)
            c = slice(2 * j, 2 * j + 2)
            dve.tensor_tensor(sgb[:, c, :], pair(g), sgb[:, c, :], ALU.mult).then_inc(pbm, 1)
            dve.wait_ge(pbm, j + 1)
            dve.tensor_tensor(mg[:, c, :], sgb[:, c, :], mg[:, c, :], ALU.add).then_inc(emptied[g % 2], 1)
            dve.wait_ge(emptied[g % 2], out_count(g))
            dve.wait_ge(pbh, j + 1)
            dve.tensor_tensor(m2_lo[:, c, :], mg[:, c, :], m2_hi[:, c, :].bitcast(F32), ALU.subtract).then_inc(pbl, 1)

        def post(n, name, src, tmp):
            inv_rms(n)
            for gi in range(4):
                b = gi % 2
                if gi >= 2:
                    dve.wait_ge(x_new, (n - 5) // 2 * 4 + gi - 1)
                link(dve.tensor_tensor(tmp[:, b, :, :], src[:, 2 * gi:2 * gi + 2, :], k_pair, ALU.mult))
                for c in (0, 1):
                    cc = 2 * gi + c
                    ins = dve.scalar_tensor_tensor(out=x[:, cc, :], in0=tmp[:, b, c, :], scalar=col(name, cc),
                                                   in1=x[:, cc, :], op0=ALU.mult, op1=ALU.add)
                ins.then_inc(x_new, 1)

        for j in range(4):
            s, g = st["r_out"].s0 + j, st["r_out"].g0 + j
            split_lo(s + AHEAD - 1, s + AHEAD - 1)
            dve.wait_ge(slab_done, s + 1)
            dve.tensor_copy(mo[:, 2 * j:2 * j + 2, :], pair(g)).then_inc(emptied[g % 2], 1)
        post(5, "mix_norm_post_2", mo, pt2)
        split_x(6)
        inv_rms(6)
        dve.wait_ge(zero_pad, 2)
        s0, g0 = st["f_up"].s0, st["f_up"].g0

        def lo_of(q, b):
            dve.wait_ge(fuh, q + 1)
            c = slice(2 * q, 2 * q + 2) if isinstance(q, int) else bass.ds(q * 2, 2)
            dve.tensor_tensor(h2_lo[:, c, :], hp[:, b, :, :], h2_hi[:, c, :].bitcast(F32), ALU.subtract).then_inc(ful, 1)

        def up_step(i, j, first=False):
            g = g0 + j
            dve.wait_ge(slab_done, s0 + i * 4 + j + 1)
            if not (isinstance(i, int) and i * 4 + j < 2):
                dve.wait_ge(fud, i * 16 + j * 4 - 4)
            dve.tensor_tensor(upad[:, j % 2, :, CONV_F - 1:], pair(g), k_pair, ALU.mult).then_inc(emptied[g % 2], 1)
            if j % 2 == 0 and not first:
                lo_of(i * 2 + j // 2 - 1, (j // 2 + 1) % 2)
            split_lo(s0 + i * 4 + j + AHEAD - 1, s0 + j + AHEAD - 1)
            dve.wait_ge(emptied[g % 2], out_count(g) + i * 2)
            dve.wait_ge(fuc, i * 4 + j + 1)
            for tap in range(CONV_F - 1):
                for c in range(2):
                    if tap:
                        dve.wait_ge(fud, i * 16 + j * 4 + c + 1)
                    ch = (j % 2) * NH2 + 2 * (j // 2) + c
                    dve.scalar_tensor_tensor(out=ucv[:, j % 2, c, :], in0=upad[:, j % 2, c, tap:tap + T],
                                             scalar=fcol(tap, i, ch), in1=ucv[:, j % 2, c, :],
                                             op0=ALU.mult, op1=ALU.add).then_inc(fud, 1)

        for j in range(4):
            up_step(0, j, first=(j == 0))
        with dve.Fori(1, 6) as i:
            for j in range(4):
                up_step(i, j)
        lo_of(11, 1)
        for j in range(12):
            s, g = st["f_dn"].s0 + j, st["f_dn"].g0 + j // 3
            split_lo(s + AHEAD - 1, s + AHEAD - 1)
            if j % 3 == 2:
                dve.wait_ge(slab_done, s + 1)
                c = 2 * (j // 3)
                dve.tensor_copy(fo[:, c:c + 2, :], pair(g)).then_inc(emptied[g % 2], 1)
        post(7, "ffn_norm_post_2", fo, pt3)

    @block.tensor
    def _(pe):
        def gemm(s, sj, g, gj, x_hi, x_lo, kc0=0, n_k=KS, first=True, last=True, tok_major=False, n=NS, m=None,
                 before_pair=None):
            slot, b = sj % RING, gj % 2
            pe.wait_ge(w_ready, s + 1)
            if first:
                pe.wait_ge(emptied[b], g)
            for k in range(n_k):
                if before_pair is not None and k % 2 == 0:
                    before_pair(k // 2)
                passes = ((w_hi, x_hi), (w_hi, x_lo), (w_lo, x_hi))
                for half in range(2):
                    if m is not None and half:
                        break
                    for q, (w, xx) in enumerate(passes):
                        if tok_major:
                            lhs = xx[:, kc0 + k, half * P:(half + 1) * P]
                            rhs = w[:, slot, k, 0:n]
                            dst = ps_g[:, b, half * NS:half * NS + n]
                        else:
                            mm = m or P
                            lhs = w[:, slot, k, half * P:half * P + mm]
                            rhs = xx[:, kc0 + k, :]
                            dst = ps_g[0:mm, b, half * T:(half + 1) * T]
                        ins = pe.matmul(dst, lhs, rhs, start=(first and k == 0 and half == 0 and q == 0),
                                        stop=(last and k == n_k - 1 and q == 2), skip_group_check=True)
            ins.then_inc(slab_done, 1)

        def gwait(g):
            return out_count(g) - 1

        def x_in(n):
            def wait(pair):
                pe.wait_ge(xl, PRE_I[n] * 4 + pair + 1)
            return wait

        def stat(n):
            if n:
                pe.wait_ge(sd_ok, n)
            pe.wait_ge(sq_ok, n + 1)
            terms = [(ones, 0)] if n != 4 else [(ones, 1), (eps_ones, 0)]
            k = 0
            for w, i in terms:
                for c in range(2):
                    ins = pe.matmul(ps_s[:, 0, 0:T], w[:, :], sq_sum[:, i, c, :], start=(k == 0), stop=(k == 2 * len(terms) - 1))
                    k += 1
            if n == 4:
                for c in range(2):
                    ins = pe.matmul(ps_s[:, 1, T:2 * T], ones[:, :], sq_sum[:, 0, c, :], start=(c == 0), stop=(c == 1))
            ins.then_inc(stat_ok, 1)

        def stat_tok(n):
            pe.wait_ge(rs_ok, n + 1)
            if TOK[n]:
                pe.wait_ge(rst_ok, TOK[n])
            for tb in range(TB):
                ins = pe.matmul(ps_s[:, 1, tb:tb + 1], rs[0:1, 1, tb * P:(tb + 1) * P], ones[0:1, 0:1], start=True,
                                stop=True)
            ins.then_inc(rst_ps, 1)

        def attention(p):
            a, units = att[p], UNITS[p]
            n_units = len(units)

            def scores(i):
                u = units[i]
                if i >= 2:
                    pe.wait_ge(a["logit"], i - 1)
                for b, (c0, n) in enumerate(u["blocks"]):
                    ins = pe.matmul(ps_s[:, i % 2, c0:c0 + n], u["q"][:, b * P:(b + 1) * P], u["k"][b], start=True, stop=True)
                ins.then_inc(a["score"], 1)

            def normed(i):
                return units[i]["n_done"]

            def transposes(i):
                u = units[i]
                if u["pv"] is None:
                    return
                n = u["n"]
                pe.wait_ge(a["norm"], normed(i))
                if n >= 2:
                    pe.wait_ge(a["trc"], n - 1)
                for q, (c0, k) in enumerate(u["tiles"]):
                    ins = pe.transpose(ps_t[0:k, n % 2, q * P:(q + 1) * P], prob[:, i % PB, c0:c0 + k], ident[:, :])
                ins.then_inc(a["tr"], 1)

            def values(i):
                u = units[i]
                if u["pv"] is None:
                    return
                n, o = u["n"], u["seq"]
                pe.wait_ge(a["trc"], n + 1)
                if u["start"] and u["rows"][0] == 0 and o >= 2:
                    if p == 0 and o - 2 < DIFF_H:
                        pe.wait_ge(a["oh"], o - 1)
                    else:
                        pe.wait_ge(a["ol"], o - 1 - (DIFF_H if p == 0 else 0))
                r0, r1 = u["rows"]
                for q, (v, k, (c0, c1), (o0, o1)) in enumerate(u["pv"]):
                    ins = pe.matmul(ps_o[r0:r1, o % 2, o0:o1], v, prob_ts[p // 2][0:k, n % 2, c0:c1],
                                    start=(u["start"] and q == 0), stop=(u["stop"] and q == 1), skip_group_check=True)
                ins.then_inc(a["pv"], 1)

            for i in range(n_units + LAG_V):
                if i < n_units:
                    scores(i)
                if LAG_T <= i < n_units + LAG_T:
                    transposes(i - LAG_T)
                if i >= LAG_V:
                    values(i - LAG_V)
                if p == 0 and i in DN_PS:
                    h = DN_PS.index(i)
                    pe.wait_ge(dn["sq"], h + 1)
                    pe.matmul(ps_g[:, h // 2, (h % 2) * T:(h % 2 + 1) * T], ones[:, :], dsq[:, h, :], start=True, stop=True)\
                        .then_inc(dn["ps"], 1)

        pe.wait_ge(idn, 2)
        pe.wait_ge(ld["g"], 16)
        n_gain = PARAMS["norm_mix"][2]
        pe.transpose(ps_t[:, 1, 0:n_gain], prow[0:n_gain, 0, :], ident[0:n_gain, 0:n_gain]).then_inc(par_t, 1)
        pe.wait_ge(ld["x"], 32)
        for gi in range(4):
            if gi >= 2:
                pe.wait_ge(emptied[gi % 2], gi // 2)
            for c in range(2):
                for tb in range(TB):
                    ins = pe.transpose(ps_g[:, gi % 2, c * T + tb * P:c * T + (tb + 1) * P],
                                       xin[:, tb, (2 * gi + c) * P:(2 * gi + c + 1) * P], ident[:, :])
            ins.then_inc(xt, 1)
        g0 = st["a_in"].g0
        for j in range(12):
            s, g = st["a_in"].s0 + j, g0 + j
            gemm(s, s, gwait(g), g, act_hi, act_lo, before_pair=x_in(0) if j == 0 else None, tok_major=j in (4, 5, 10, 11),
                 n=GATES if j == 5 else NS)
            if j == 0:
                stat(0)
                stat_tok(0)
                pe.wait_ge(ld["par"], 16 * len(PARAMS))
                for k in range(4):
                    ins = pe.transpose(ps_t[:, 0, k * P:k * P + TILE_ROWS[k]], prow[0:TILE_ROWS[k], k, :],
                                       ident[0:TILE_ROWS[k], 0:TILE_ROWS[k]])
                ins.then_inc(par_t, 1)
                pe.wait_ge(ld["bias"], 32)
                pe.matmul(ps_o[0:16, 0, 0:REL], btab[:, :], buck[:, :], start=True, stop=True).then_inc(brow_ps, 1)
            if j == CMP_STEP:
                pe.wait_ge(ld["cw"], 16 * 6)
                pe.wait_ge(emptied[g0 % 2], out_count(g0))
                pe.wait_ge(rst_ok, 1)
                for i in range(2):
                    for m in range(16):
                        ins = pe.matmul(ps_s[:, i, 0:3 * NC].rearrange("p (g c) -> p g c", g=3), cw1[:, i, m, :],
                                        cmp2[:, i, :, 2 * m:2 * m + (NC - 1) * CMP_STRIDE + 1:CMP_STRIDE],
                                        start=(m == 0), stop=(m == 15))
                ins.then_inc(cmp_ps, 1)
            if j == CMP_STEP + 2:
                pe.wait_ge(cmp_h, 1)
                pe.matmul(ps_s[:, 0, 128:128 + 2 * NC], cw2[:, 0, :], chid[:, 0, :], start=True, stop=True)
                for gg in range(2):
                    ins = pe.matmul(ps_s[0:NC, 0, 256 + gg * HD:256 + (gg + 1) * HD], chid[:, 1, gg * NC:(gg + 1) * NC],
                                    cw2[:, 1, 0:HD], start=True, stop=True)
                ins.then_inc(cmp_ps2, 1)
        pe.wait_ge(cmp_ok, 1)
        for b in range(2):
            g = g0 + 10 + b
            pe.wait_ge(emptied[g % 2], out_count(g))
        attention(0)
        def out_stage(name, n, h, l, ready):
            for j in range(4):
                s, g = st[name].s0 + j, st[name].g0 + j
                gemm(s, s, gwait(g), g, h, l, before_pair=ready if j == 0 else None)

        def mlp(up, dn_, n, l):
            s0, g0 = st[up].s0, st[up].g0
            for j in range(4):
                gemm(s0 + j, s0 + j, gwait(g0 + j), g0 + j, act_hi, act_lo, before_pair=x_in(n) if j == 0 else None)
                if j == 0:
                    stat(n)
            with pe.Fori(1, 4) as i:
                for j in range(4):
                    gemm(s0 + i * 4 + j, s0 + j, gwait(g0 + j) + i * 2, g0 + j, act_hi, act_lo)
            s0, g0 = st[dn_].s0, st[dn_].g0
            with pe.Fori(0, 2) as i:
                for j in range(8):
                    def ready(pair, r=j % 4):
                        pe.wait_ge(hid_l, l * 16 + r * 4 + pair + 1)
                    gemm(s0 + i * 8 + j, s0 + j, gwait(g0 + j // 4) + i, g0 + j // 4, hid_hi, hid_lo, kc0=(j % 4) * 8,
                         first=j % 4 == 0, last=j % 4 == 3, before_pair=ready if j < 4 else None)

        def mix_in(p):
            def wait(pair):
                if p == 0 and pair >= 2:
                    pe.wait_ge(dn["lo"], 2 * pair - 2)
                else:
                    pe.wait_ge(att[p]["ol"], 2 * pair + 2)
            return wait

        pe.wait_ge(dn["sd"], 1)
        out_stage("a_out", 1, mix_hi, mix_lo, mix_in(0))
        mlp("a_up", "a_dn", 1, 0)
        s0, g0 = st["m_in"].s0, st["m_in"].g0
        for j in range(4):
            gemm(s0 + j, s0 + j, gwait(g0 + j), g0 + j, act_hi, act_lo, before_pair=x_in(2) if j == 0 else None)
            if j == 0:
                stat(2)
                stat_tok(2)
        for j in range(4, 8):
            gemm(s0 + j, s0 + j, gwait(g0 + j), g0 + j, act_hi, act_lo)
        for j in range(8, 12):
            gemm(s0 + j, s0 + j, gwait(g0 + j), g0 + j, act_hi, act_lo, tok_major=True)
        for b in range(2):
            pe.wait_ge(emptied[(g0 + 10 + b) % 2], out_count(g0 + 10 + b))
        attention(1)
        out_stage("m_out", 3, mix_hi, mix_lo, mix_in(1))
        mlp("m_up", "m_dn", 3, 1)
        s0, g0 = st["r_xa"].s0, st["r_xa"].g0
        for j in range(5):
            gemm(s0 + j, s0 + j, gwait(g0 + j), g0 + j, act_hi, act_lo, before_pair=x_in(4) if j == 0 else None)
            if j == 0:
                pe.wait_ge(epso, 1)
                stat(4)
                stat_tok(4)
        s0, g0 = st["r_f"].s0, st["r_f"].g0
        gemm(s0, s0, gwait(g0), g0, act_hi, act_lo, m=ATT_H)
        s0, g0 = st["r_gate"].s0, st["r_gate"].g0
        for j in range(8):
            gemm(s0 + j, s0 + j, gwait(g0 + j), g0 + j, act_hi, act_lo)
            if j == RG_STEP:
                pe.wait_ge(ld["gw"], 16 * len(pieces))
                pe.wait_ge(rst_ok, 3)
                pe.wait_ge(sdf, 1)
                for j in range(NR):
                    srcs = rg_inputs(j)
                    pe.wait_ge(cvd, 6 * (srcs[-1] // 2) + 6)
                    if j >= 2:
                        pe.wait_ge(rg["sig"], j - 1)
                    for i in range(2):
                        for q, c in enumerate(srcs):
                            ins = pe.matmul(ps_s[:, j % 2, i * T:(i + 1) * T], gw[:, i, c, j - c + 1, :], xc[:, c, :],
                                            start=(q == 0), stop=(q == len(srcs) - 1))
                    ins.then_inc(rg["ps"], 1)
            if j == RG_STEP + 1:
                pe.wait_ge(fcum, 1)
                pe.wait_ge(rg["sig"], NR)
                for tb in range(TB):
                    ins = pe.transpose(ps_s[:, 0, tb * 16:(tb + 1) * 16], fl[:, 5, tb * P:(tb + 1) * P], ident[0:16, 0:16])
                ins.then_inc(fcq_ps, 1)
        s0, g0 = st["r_ga"].s0, st["r_ga"].g0
        for j in range(5):
            gemm(s0 + j, s0 + j, gwait(g0 + j), g0 + j, act_hi, act_lo)
        s0, g0 = st["r_v"].s0, st["r_v"].g0
        for j in range(4):
            gemm(s0 + j, s0 + j, gwait(g0 + j), g0 + j, act_hi, act_lo, tok_major=True)
        s0, g0 = st["r_pa"].s0, st["r_pa"].g0

        def ya_in(r):
            def wait(pair):
                pe.wait_ge(yl, (r * (NR // 2) + 2 * pair + 1) // 2 + 1 if r * (NR // 2) + 2 * pair + 1 < NR else 5)
            return wait

        for j in range(8):
            gemm(s0 + j, s0 + j, gwait(g0 + j // 2), g0 + j // 2, ya_hi, ya_lo, kc0=(j % 2) * (NR // 2), n_k=NR // 2,
                 first=j % 2 == 0, last=j % 2 == 1, before_pair=ya_in(j) if j < 2 else None)
        s0, g0 = st["r_qk"].s0, st["r_qk"].g0
        with pe.Fori(0, 2) as i:
            for j in range(4):
                gemm(s0 + i * 4 + j, s0 + j, gwait(g0 + j) + i * 2, g0 + j, act_hi, act_lo)
        for b in range(2):
            pe.wait_ge(emptied[(g0 + 6 + b) % 2], out_count(g0 + 6 + b))
        pe.wait_ge(fcq_ok, 1)
        attention(2)
        out_stage("r_pb", 6, act_hi, act_lo, mix_in(2))

        def m2_in(pair):
            pe.wait_ge(pbl, pair + 1)

        out_stage("r_out", 6, m2_hi, m2_lo, m2_in)
        stat(5)
        s0, g0 = st["f_up"].s0, st["f_up"].g0
        for j in range(4):
            gemm(s0 + j, s0 + j, gwait(g0 + j), g0 + j, act_hi, act_lo, before_pair=x_in(6) if j == 0 else None)
            if j == 0:
                stat(6)
        with pe.Fori(1, 6) as i:
            for j in range(4):
                gemm(s0 + i * 4 + j, s0 + j, gwait(g0 + j) + i * 2, g0 + j, act_hi, act_lo)
        s0, g0 = st["f_dn"].s0, st["f_dn"].g0
        for j in range(12):
            def ready(pair, r=j % 3):
                pe.wait_ge(ful, r * 4 + pair + 1)
            gemm(s0 + j, s0 + j, gwait(g0 + j // 3), g0 + j // 3, h2_hi, h2_lo, kc0=(j % 3) * 8, first=j % 3 == 0,
                 last=j % 3 == 2, before_pair=ready if j < 3 else None)
        stat(7)
        for gi in range(4):
            pe.wait_ge(x_new, 4 + gi + 1)
            if gi >= 2:
                pe.wait_ge(oc, gi - 1)
            for tb in range(TB):
                for c in range(2):
                    ins = pe.transpose(ps_g[:, gi % 2, tb * NS + c * P:tb * NS + (c + 1) * P],
                                       x[:, 2 * gi + c, tb * P:(tb + 1) * P], ident[:, :])
            ins.then_inc(ot, 1)


_NAMES = [
    "x", "bias_table", "norm_mix", "norm_mlp", "norm_final", "mlp_w1", "mlp_w2", "ev_w_in", "ev_w_out",
    "ev_cmp_pos_k", "ev_cmp_w1_k", "ev_cmp_w2_k", "ev_cmp_pos_v", "ev_cmp_w1_v", "ev_cmp_w2_v", "ev_lam_q1",
    "ev_lam_k1", "ev_lam_q2", "ev_lam_k2", "ev_subln", "od_w_in", "od_w_out", "mix_norm_pre_2",
    "mix_norm_post_2", "w_in_2", "conv_a_w_2", "conv_a_b_2", "w_rg_a_2", "b_rg_a_2", "w_rg_x_2", "b_rg_x_2",
    "lru_lambda_2", "b_forget_2", "b_merge_2", "w_proj_a_2", "w_proj_b_2", "w_out_2", "ffn_norm_pre_2",
    "ffn_norm_post_2", "w_up_2", "conv_f_w_2", "conv_f_b_2", "w_down_2",
]


def kernel(**inputs):
    import concourse.bacc as bacc
    from concourse.bass_utils import run_bass_kernel_spmd

    nc = bacc.Bacc("TRN2", target_bir_lowering=False, num_devices=1)
    arrays, t = {}, {}
    for name in _NAMES:
        a = np.ascontiguousarray(inputs[name])
        arrays[f"in_{name}"] = a
        t[name] = nc.dram_tensor(f"in_{name}", a.shape, mybir.dt.from_np(a.dtype), kind="ExternalInput").ap()
    rows = bucket_rows()
    arrays["bucket_rows"] = rows
    t["bucket"] = nc.dram_tensor("bucket_rows", rows.shape, F32, kind="ExternalInput").ap()
    out = nc.dram_tensor("out", (1, T, D), F32, kind="ExternalOutput").ap()
    with ExitStack() as ctx:
        build(nc, ctx, t, out)
    return run_bass_kernel_spmd(nc, [arrays], core_ids=[0]).results[0]["out"]
```

```python
import math
from contextlib import ExitStack

import concourse.bass as bass
from concourse import mybir
import numpy as np

F32 = mybir.dt.float32
F32R = mybir.dt.float32r
ALU = mybir.AluOpType
ACT = mybir.ActivationFunctionType

P = 128
T = 256
TB = T // P
D = 1024
NX = D // P
KS = 8
NS = 256
HD = 64
BIG = 1e30
EPS = 1e-6
NSA_H, DIFF_H, MOBA_H, ATT_H = 8, 4, 16, 16
GATES = 3 * NSA_H
CMP_BLOCK, CMP_STRIDE = 32, 16
NC = (T - CMP_BLOCK) // CMP_STRIDE + 1
NC0 = (P - CMP_BLOCK) // CMP_STRIDE + 1
D_RNN, RNN_BLOCK = 1280, 80
NR = D_RNN // P
CONV_A, CONV_F = 4, 3
D_FF = 4096
NH1 = D_FF // P
D_FF2 = 3072
NH2 = D_FF2 // P
NUM_BUCKETS, MAX_DISTANCE = 32, 128
PB = 5
LAG_N, LAG_T, LAG_V, LAG_HI, LAG_LO = 2, 3, 5, 6, 7
DN_PS = [2 * h + 9 for h in range(DIFF_H)]
DN_ROOT = DN_PS[-1] + 1
DN_R = [DN_ROOT + 2 + 4 * h for h in range(DIFF_H)]
DN_HI = [i + 1 for i in DN_R]
DN_LO = [i + 2 for i in DN_R]
RG_STEP = 1
A_SLABS = [((1304,), 256), ((1816,), 256), ((2328,), 256), ((1560,), 256), ((1280,), 24), ((512,), 256),
           ((2072,), 256), ((2584,), 256), ((768, 1024), 128), ((0,), 256), ((256,), 256), ((896, 1152), 128)]
DQ0, DK0, DV0, DQ1, GATE, KV_CMP, DK1, DV1, SKW, Q0, Q1, SV = range(12)
TWO_LOADS = (SKW, SV)
CMP1_STEP, CMP2_STEP = 3, 5
A_GROUPS = [j + (j > DV1) + (j > Q0) for j in range(12)]
CMP1_GROUP, CMP2_GROUP = DV1 + 1, Q0 + 2
IN_STEPS = ({1: 5, 2: 6, 3: 7, 4: 8, 5: 9, 6: 10, 7: 11}, {1: 3, 2: 4, 3: 5, 5: 6, 6: 7, 7: 8, 9: 9, 10: 10, 11: 11}, {})
RING = 4
AHEAD = 3
REL = 384


class Stage:
    s, g = 0, 0

    def __init__(self, slabs, per_group=1):
        self.s0, self.g0, self.n, self.per = Stage.s, Stage.g, slabs, per_group
        Stage.s += slabs
        Stage.g += slabs // per_group


def stages():
    Stage.s = Stage.g = 0
    st = {}
    for name, n, per in (("a_in", 12, 1), ("a_out", 4, 1), ("a_up", 16, 1), ("a_dn", 16, 4),
                         ("m_in", 12, 1), ("m_out", 4, 1), ("m_up", 16, 1), ("m_dn", 16, 4),
                         ("r_xa", 5, 1), ("r_f", 1, 1), ("r_gate", 8, 1), ("r_ga", 5, 1), ("r_v", 4, 1),
                         ("r_pa", 8, 2), ("r_qk", 8, 1), ("r_pb", 4, 1), ("r_out", 4, 1),
                         ("f_up", 24, 1), ("f_dn", 12, 3)):
        st[name] = Stage(n, per)
        if name == "a_in":
            Stage.g += 2
    return st, Stage.s


PARAMS = {
    "norm_mix": (0, 0, 16), "norm_mlp": (0, 16, 16), "norm_final": (0, 32, 8), "mix_norm_pre_2": (0, 40, 8),
    "mix_norm_post_2": (0, 48, 8), "ffn_norm_pre_2": (0, 56, 8), "ffn_norm_post_2": (0, 64, 8),
    "conv_a_b_2": (0, 72, 10), "b_rg_a_2": (0, 82, 10), "b_rg_x_2": (0, 92, 10), "lru_lambda_2": (0, 102, 10),
    "b_merge_2": (0, 112, 16),
    "conv_a_w_2": (1, 0, 40), "ev_subln": (1, 40, 1), "conv_f_b_2": (1, 41, 48),
    "conv_f_w_2": (2, 0, 128),
    "ev_cmp_pos_k": (3, 0, 16), "ev_cmp_pos_v": (3, 16, 16),
}
CONV_F_TAIL = (3, 32, 16)
TILE_ROWS = (128, 89, 128, 48)


def bucket_rows():
    rel = 255 - np.arange(REL)
    n = np.maximum(rel, 0)
    half = NUM_BUCKETS // 2
    large = half + (np.log(np.maximum(n, 1).astype(np.float32) / np.float32(half))
                    / np.float32(math.log(MAX_DISTANCE / half)) * np.float32(NUM_BUCKETS - half)).astype(np.int32)
    bucket = np.where(n < half, n, np.minimum(large, NUM_BUCKETS - 1))
    return -(bucket[None, :] == np.arange(NUM_BUCKETS)[:, None]).astype(np.float32)


def rg_pieces():
    out = []
    for b in range(D_RNN // RNN_BLOCK):
        row = b * RNN_BLOCK
        end = row + RNN_BLOCK
        while row < end:
            n = min(end, (row // P + 1) * P) - row
            out.append((row // P, row % P, n, b, row - b * RNN_BLOCK))
            row += n
    return out


def rg_inputs(j):
    lo = (j * P) // RNN_BLOCK * RNN_BLOCK
    hi = -(-((j + 1) * P) // RNN_BLOCK) * RNN_BLOCK
    return list(range(lo // P, (hi - 1) // P + 1))


def build(nc, ctx, t, out):
    st, n_slabs = stages()
    pieces = rg_pieces()

    base = 16512
    top = [base]

    def place(name, shape, dt=F32, at=None):
        size = int(np.prod(shape[1:])) * 4
        if at is None:
            at = top[0]
            top[0] = -(-(at + size) // 32) * 32
        return nc.alloc_sbuf_tensor_at(name, shape, dt, offset=at)

    K = 1024
    raw = place("raw", [P, RING, KS, NS])
    w_hi = place("w_hi", [P, RING, KS, NS], F32R)
    w_lo = place("w_lo", [P, RING, KS, NS], F32R)
    x = place("x", [P, NX, T])
    ident = place("ident", [P, P])
    ones = place("ones", [P, P])
    par = place("par", [P, 4, P])
    rs = place("rs", [P, 2, T])
    sd = place("sd", [P, T])
    rs_f = place("rs_f", [P, T])
    gain_f = place("gain_f", [P, NX])
    eps_ones = place("eps_ones", [P, P])
    rs_tok = place("rs_tok", [P, TB])
    nmin = place("nmin", [P, 24 + 2 * DIFF_H, 2])
    psum_ = place("sums", [P, 24 + 2 * DIFF_H, 2])
    fac = place("fac", [P, 24 + 2 * DIFF_H, 2])
    small = place("small", [P, 64])
    ssq = place("ffn_sums", [P, TB, 4])
    rs_o = place("ffn_rs", [P, TB])
    fcq = place("f_cum_q", [P, TB, 16])
    fw = place("conv_f", [P, 4, 2 * NH2])
    act_hi = place("act_hi", [P, NX, T], F32R)
    act_lo = place("act_lo", [P, NX, T], F32R)
    tmp0 = top[0]
    arena = tmp0 + 8 * K
    assert arena + 70 * K <= 229344, arena + 70 * K

    def tm(name, shape, at, dt=F32):
        assert at + int(np.prod(shape[1:])) * 4 <= 8 * K
        return place(name, shape, dt, tmp0 + at)

    def ar(name, shape, at, dt=F32):
        assert arena + at + int(np.prod(shape[1:])) * 4 <= 229344, name
        return place(name, shape, dt, arena + int(at))

    sq = tm("sq", [P, 2, 2, T], 0)
    sq_sum = tm("sq_sum", [P, 2, 2, T], 4 * K)
    sq4 = tm("sq_pairs", [P, 4, 2, T], 0)
    up_r = tm("up_r", [P, 2, 2, T], 0)
    up_q = tm("up_q", [P, 2, 2, T], 4 * K)
    prob = tm("prob", [P, PB, 384], 0)
    hid_hi = ar("hid_hi", [P, NH1, T], 0, F32R)
    hid_lo = ar("hid_lo", [P, NH1, T], 32 * K, F32R)
    mix_hi = ar("mix_hi", [P, NX, T], 0, F32R)
    mix_lo = ar("mix_lo", [P, NX, T], 8 * K, F32R)
    cw1 = ar("cmp_w1", [P, 2, 16, P], 0)
    nb = ar("bias", [P, 16, T], 16 * K)
    aq = ar("a_q", [P, 4, T], 32 * K)
    cmp2 = ar("cmp_in", [P, 2, 3, T], 58 * K)
    skw = ar("a_skw", [P, 2, 2, T], 40 * K)
    sv = ar("a_sv", [P, TB, NS], 44 * K)
    dqk = ar("d_qk", [P, 8, T], 46 * K)
    dv = ar("d_v", [P, TB, 4 * P], 54 * K)
    gates = ar("gates", [P, TB, GATES], 36 * K)
    cw2 = ar("cmp_w2", [P, 2, P], 37 * K + 256)
    chid = ar("cmp_hid", [P, 2, 2 * NC], 36 * K + 256)
    kc = ar("kc", [P, 2, NC], 36 * K + 512)
    vc = ar("vc", [P, P], 36 * K + 768)
    dob = ar("d_ob", [P, DIFF_H, T], 61 * K)
    lamv = ar("lam_v", [P, 4, HD], 65 * K)
    xin = ar("x_in", [P, TB, D], 32 * K)
    prow = ar("par_rows", [P, 4, P], 40 * K)
    buck = ar("bucket", [NUM_BUCKETS, REL], 42 * K)
    btab = ar("bias_table", [NUM_BUCKETS, 16], 44 * K)
    brow = ar("bias_row", [16, REL], 66.5 * K)
    dsq = ar("d_sq", [P, DIFF_H, T], 46 * K)
    mqk = ar("m_qk", [P, 16, T], 32 * K)
    mv = ar("m_v", [P, TB, D], 48 * K)
    xap = ar("xa_pad", [P, NR, T + CONV_A - 1], 0)
    rt = ar("rg_t", [P, NR, T], 0)
    xc = ar("xc", [P, NR, T], 10.25 * K)
    rr = ar("rg_r1", [P, NR, T], 10.25 * K)
    gw = ar("rg_w", [P, 2, NR, 3, P], 20.5 * K)
    ra = ar("rg_decay", [P, NR, T], 20.5 * K)
    rix = ar("rg_ix", [P, NR, T], 50.5 * K)
    hr = ar("h_rnn", [P, NR, T], 50.5 * K)
    ya_hi = ar("ya_hi", [P, NR, T], 30.5 * K, F32R)
    ya_lo = ar("ya_lo", [P, NR, T], 40.5 * K, F32R)
    gt = ar("gelu_tmp", [P, 2, 2, T], 0)
    sga = tm("sig_a", [P, NX, T], 0)
    sgb = ar("sig_b", [P, NX, T], 60.5 * K)
    fl = tm("f_logsig", [16, 6, T], 0)
    fqk = ar("f_qk", [P, 16, T], 0)
    fv = ar("f_v", [P, TB, D], 16 * K)
    nb2 = ar("f_bias", [P, 16, 384], 27 * K)
    mg = ar("merge", [P, NX, T], 51 * K)
    prob_ts = [ar("prob_t", [P, 2, 384], 66.5 * K), ar("prob_t_f", [P, 2, 384], 24 * K)]
    m2_hi = ar("m2_hi", [P, NX, T], 0, F32R)
    m2_lo = ar("m2_lo", [P, NX, T], 8 * K, F32R)
    mo = ar("mix_out", [P, NX, T], 27 * K)
    h2_hi = ar("h2_hi", [P, NH2, T], 0, F32R)
    h2_lo = ar("h2_lo", [P, NH2, T], 24 * K, F32R)
    upad = ar("up_pad", [P, 2, 2, T + CONV_F - 1], 48 * K)
    ucv = ar("up_conv", [P, 2, 2, T], 52.25 * K)
    hp = ar("up_prod", [P, 2, 2, T], 56.25 * K)
    fo = ar("ffn_out", [P, TB, D], 48 * K)
    fsq = ar("ffn_sq", [P, TB, NS], 56 * K)
    gain_row = ar("gain_row", [P, D], 62 * K)

    ps_g = ctx.enter_context(nc.psum_tensor("ps_gemm", [P, 2, 512], F32))
    ps_s = ctx.enter_context(nc.psum_tensor("ps_score", [P, 2, 512], F32))
    ps_t = ctx.enter_context(nc.psum_tensor("ps_trans", [P, 2, 512], F32))
    ps_o = ctx.enter_context(nc.psum_tensor("ps_out", [P, 2, 512], F32))

    def sem(name):
        return ctx.enter_context(nc.semaphore(name))

    raw_in = [sem(f"raw_in{i}") for i in range(RING)]
    hi_done = sem("hi_done")
    w_ready = sem("w_ready")
    slab_done = sem("slab_done")
    emptied = [sem(f"emptied{b}") for b in range(2)]
    ld = {n: sem(f"ld_{n}") for n in ("x", "g", "par", "bias", "cw", "gw", "lam", "bf", "gain")}
    idn = sem("idn")
    par_t, par_ok = sem("par_t"), sem("par_ok")
    xt = sem("x_transposed")
    brow_ps, brow_ok, brow_out, nb_in, nb_ok = (sem(n) for n in ("brow_ps", "brow_ok", "brow_out", "nb_in", "nb_ok"))
    xh, xl = sem("act_hi_done"), sem("act_lo_done")
    sq_ok, stat_ok, sd_ok, rs_ok = sem("sq_ok"), sem("stat_ok"), sem("sd_ok"), sem("rs_ok")
    rsq_ok, rst_ps, rst_ok = sem("rsq_ok"), sem("rst_ps"), sem("rst_ok")
    x_new = sem("x_new")
    upr, hid_h, hid_l = sem("up_relu2"), sem("hid_hi_done"), sem("hid_lo_done")
    dve_c, act_c = sem("dve_chain"), sem("act_chain")
    att = [{n: sem(f"at{p}_{n}") for n in ("in", "score", "logit", "prob", "sum", "norm", "tr", "trc", "pv", "oh", "ol")}
           for p in range(3)]
    cmp_ps, cmp_b, cmp_ps2 = (sem(n) for n in ("cmp_ps", "cmp_b", "cmp_ps2"))
    dn = {n: sem(f"dn_{n}") for n in ("o", "sq", "ps", "sd", "r", "o2", "hi", "lo")}
    lam_ok, lam_e = sem("lam_ok"), sem("lam_e")
    gz = sem("gw_zero")
    cva, cvd = sem("conv_a_act"), sem("conv_a_dve")
    rg = {n: sem(f"rg_{n}") for n in ("ps", "sig", "ix", "den", "sq", "a", "b1", "b2", "h")}
    rcp = sem("rg_recip")
    sp_a, sp_d = sem("sp_act"), sem("sp_dve")
    yg, yy, yh, yl = (sem(n) for n in ("ya_gelu", "ya_y", "ya_hi_done", "ya_lo_done"))
    gs2 = sem("gate_sig")
    sqg, sdf, rsf, x_mat, gain_ok = (sem(n) for n in ("sq_gain", "sd_f", "rs_f_ok", "x_mat", "gain_ok"))
    epso, sqg_used = sem("eps_ones_ok"), sem("sq_gain_used")
    fz, fa, fcum = sem("f_z"), sem("f_act"), sem("f_cum")
    fout, fin_, fcq_ps, fcq_ok, fnb = (sem(n) for n in ("f_cum_out", "f_bias_in", "f_cq_ps", "f_cq_ok", "f_nb"))
    pbm, pbh, pbl = sem("pb_m"), sem("pb_hi"), sem("pb_lo")
    fuz, fuc, fud, fug, fup, fuh, ful = (sem(n) for n in ("fu_z", "fu_conv1", "fu_conv", "fu_gelu", "fu_prod", "fu_hi", "fu_lo"))
    zero_pad = sem("zero_pad")
    sq5, sq6, x_new_p = sem("sq5_pairs"), sem("sq6_pairs"), sem("x_new_pool")
    x_tok, fsq_ok, fsum, fsd, frs, o_done, o_out = (sem(n) for n in (
        "x_by_token", "ffn_sq_ok", "ffn_sum", "ffn_sd", "ffn_rs_ok", "out_done", "out_dma"))
    pool_c = sem("pool_chain")

    scr_b = nc.dram_tensor("bias_rows_scr", [16, REL], F32, kind="Internal").ap()
    scr_w = nc.dram_tensor("bias_wide_scr", [16, 16 * REL], F32, kind="Internal").ap()
    scr_c = nc.dram_tensor("cum_scr", [16, T], F32, kind="Internal").ap()

    def col(name, i=0, n=1):
        tile, row, rows = PARAMS[name]
        return par[:, tile, row + i:row + i + n]

    def conv_f_w(j, c):
        r = j * 2 * NH2 + c
        if r < P:
            return par[:, 2, r:r + 1]
        return par[:, CONV_F_TAIL[0], CONV_F_TAIL[1] + r - P:CONV_F_TAIL[1] + r - P + 1]

    eps_c, eps2_c, _, one_c, lamn = (small[:, i:i + 1] for i in range(5))
    sub8 = small[:, 5:6]
    sp4 = small[:, 8:18]
    spw = small[:, 18:58]
    cposb = small[:, 58:60]
    b_f = small[0:16, 60:61]

    def out_count(g):
        return g // 2 + 3

    def x_ready(n, gi):
        if n == 0:
            return emptied[gi % 2], gi // 2 + 1
        if n == 6:
            return (x_new, gi + 1) if gi < 2 else (x_new_p, gi - 1)
        g = st[{1: "a_out", 2: "a_dn", 3: "m_out", 4: "m_dn"}[n]].g0 + gi
        return emptied[g % 2], out_count(g)

    PRE = {0: ("norm_mix", 0), 1: ("norm_mlp", 0), 2: ("norm_mix", 8), 3: ("norm_mlp", 8),
           4: None, 6: ("ffn_norm_pre_2", 0)}
    PRE_I = {n: i for i, n in enumerate(PRE)}

    def gain(n, c):
        return gain_f[:, c:c + 1] if n == 4 else col(PRE[n][0], PRE[n][1] + c)
    DIRECT = (4,)
    TOK = {0: 0, 2: 1, 4: 2}

    def att_units(p):
        units = []

        def full(q, k, bias, **kw):
            units.append(dict(q=q, k=[k[:, 0:P], k[:, 0:T]],
                              blocks=[(0, P), (P, T)], bias=bias,
                              tiles=[(0, P), (P, P), (2 * P, P)], init=3e38, cmp=False, **kw))

        if p == 0:
            for h in range(DIFF_H):
                for m in range(2):
                    lo = m * HD
                    v = [dv[:, tb, h * P:(h + 1) * P] for tb in range(TB)]
                    full(dqk[lo:lo + HD, h, :], dqk[lo:lo + HD, 4 + h, :],
                         [nb[:, NSA_H + h, P:T], nb[:, NSA_H + h, :]], diff=m, out=4 + h, rows=(0, P),
                         start=True, stop=True, last=True,
                         pv=None if m == 0 else [(v[0], P, (0, T), (0, T)), (v[1], P, (T, 384), (P, T))])
            for h in range(NSA_H):
                g, lo = h // 4, (h % 2) * HD
                q = aq[lo:lo + HD, h // 2, :]
                keys = kc[lo:lo + HD, g, :]
                end = CMP_BLOCK - 1
                vg = vc[:, g * HD:(g + 1) * HD]
                units.append(dict(
                    q=q, k=[keys[:, 0:NC0], keys], blocks=[(0, NC0), (P, NC)],
                    bias=[nb[:, h, P + end:P + end + (NC0 - 1) * CMP_STRIDE + 1:CMP_STRIDE],
                          nb[:, h, end:end + (NC - 1) * CMP_STRIDE + 1:CMP_STRIDE]],
                    tiles=[(0, NC0), (P, NC)], init=BIG / 10, cmp=True, gate=h, out=h // 2, rows=(lo, lo + HD),
                    start=True, stop=False, last=False,
                    pv=[(vg[0:NC0, :], NC0, (0, P), (0, P)), (vg[0:NC, :], NC, (P, T), (P, T))]))
                for b in range(2):
                    v = [sv[:, tb, b * P + g * HD:b * P + (g + 1) * HD] for tb in range(TB)]
                    full(q, skw[lo:lo + HD, b, g, :], [nb[:, h, P:T], nb[:, h, :]], gate=8 * (b + 1) + h,
                         out=h // 2, rows=(lo, lo + HD), start=False, stop=(b == 1), last=(b == 1 and h % 2 == 1),
                         pv=[(v[0], P, (0, T), (0, T)), (v[1], P, (T, 384), (P, T))])
        else:
            qk, vv = (mqk, mv) if p == 1 else (fqk, fv)
            for h in range(16):
                lo = (h % 2) * HD
                v = [vv[:, tb, h * HD:(h + 1) * HD] for tb in range(TB)]
                bias = [nb[:, h, P:T], nb[:, h, :]] if p == 1 else [nb2[:, h, 0:P], nb2[:, h, P:384]]
                full(qk[lo:lo + HD, h // 2, :], qk[lo:lo + HD, 8 + h // 2, :], bias, out=h // 2, rows=(lo, lo + HD),
                     start=True, stop=True, last=(h % 2 == 1),
                     pv=[(v[0], P, (0, T), (0, T)), (v[1], P, (T, 384), (P, T))])
        n = 0
        for i, u in enumerate(units):
            if p == 0:
                g0 = st["a_in"].g0
                u["qk_groups"] = [g0 + g for g in {
                    0: (A_GROUPS[DQ0], A_GROUPS[DK0]), 4: (A_GROUPS[DQ1], A_GROUPS[DK1]), 8: (A_GROUPS[Q0], CMP2_GROUP),
                    9: (A_GROUPS[SKW],), 20: (A_GROUPS[Q1],)}.get(i, ())]
                u["v_groups"] = [g0 + A_GROUPS[j] for j in {1: (DV0,), 5: (DV1,), 9: (SV,)}.get(i, ())]
            if p == 1 and i % 4 == 0:
                g = st["m_in"].g0 + 3 * (i // 4)
                u["qk_groups"], u["v_groups"] = (g, g + 1), (g + 2,)
            u["n"] = n
            u["seq"] = u["out"] if p else (u["out"] + DIFF_H) % (2 * DIFF_H)
            if u["pv"] is not None:
                n += 1
            u["n_done"] = n
        return units

    UNITS = [att_units(p) for p in range(3)]

    def freed_by(units, i):
        u = units[i - PB]
        return u["n_done"] if u["pv"] is not None else None

    def raw_extra(slot, j):
        return 16 * sum(1 for s in TWO_LOADS if s % RING == slot and s <= j)

    def fcol(tap, i, ch):
        if isinstance(i, int):
            return fw[:, tap, 4 * i + ch:4 * i + ch + 1]
        return fw[:, tap, bass.ds(i * 4 + ch, 1)]

    def conv_cols(i, j, c):
        ch = (j % 2) * NH2 + 2 * (j // 2) + c
        return fcol(2, i, ch), fcol(3, i, ch)

    block = ctx.enter_context(nc.Block())

    @block.sync
    def _(sp):
        def slab(s, j, src, k=KS, n=NS):
            if not (isinstance(s, int) and s < RING):
                sp.wait_ge(w_ready, s - RING + 1)
            dst = raw[:, j % RING, 0:k, 0:n]
            if len(src.shape) == 4:
                dst = dst.rearrange("p k (a b) -> p k a b", a=2)
            sp.dma_start(dst, src).then_inc(raw_in[j % RING], 16)

        def rows(w):
            return w.rearrange("(k p) n -> p k n", p=P)

        w_a = rows(t["ev_w_in"][0])

        def a_slab(j):
            s = st["a_in"].s0 + j
            starts, n = A_SLABS[j]
            if j in TWO_LOADS:
                sp.wait_ge(w_ready, s - RING + 1)
                for half, c0 in enumerate(starts):
                    sp.dma_start(raw[:, s % RING, :, half * P:(half + 1) * P], w_a[:, :, c0:c0 + n]).then_inc(raw_in[s % RING], 16)
            else:
                slab(s, s, w_a[:, :, starts[0]:starts[0] + n], n=n)

        for tb in range(TB):
            sp.dma_start(xin[:, tb, :], t["x"][0, tb * P:(tb + 1) * P, :]).then_inc(ld["x"], 16)
        for j in range(RING):
            a_slab(j)
        for name, (tile, row, n) in PARAMS.items():
            if name != "norm_mix":
                src, letters = t[name], " ".join("abcd"[:len(t[name].shape)])
                if len(src.shape) > 1:
                    src = src.rearrange(f"{letters} -> ({letters})")
                sp.dma_start(prow[row:row + n, tile, :], src[0:n * P].rearrange("(r c) -> r c", c=P)).then_inc(ld["par"], 16)
        tail = t["conv_f_w_2"].rearrange("a b c -> (a b c)")[P * P:144 * P].rearrange("(r c) -> r c", c=P)
        sp.dma_start(prow[CONV_F_TAIL[1]:CONV_F_TAIL[1] + 16, CONV_F_TAIL[0], :], tail).then_inc(ld["par"], 16)
        sp.dma_start(buck[:, :], t["bucket"]).then_inc(ld["bias"], 16)
        sp.dma_start(btab[:, :], t["bias_table"]).then_inc(ld["bias"], 16)
        for i, name in enumerate(("ev_lam_q1", "ev_lam_k1", "ev_lam_q2", "ev_lam_k2")):
            sp.dma_start(lamv[:, i, :], t[name].to_broadcast([P, HD])).then_inc(ld["lam"], 16)
        a_slab(RING)
        sp.wait_ge(brow_ok, 1)
        sp.dma_start(scr_b, brow[:, :]).then_inc(brow_out, 16)
        a_slab(RING + 1)
        sp.wait_ge(brow_out, 16)
        sp.dma_start(scr_w, bass.AP(tensor=scr_b.tensor, offset=0, ap=[[0, 16], [1, 16 * REL]])).then_inc(brow_out, 16)
        sp.wait_ge(brow_out, 32)

        def load_bias():
            for a in range(P // 16):
                src = bass.AP(tensor=scr_w.tensor, offset=P - 1 - 16 * a, ap=[[16 * REL - 1, 16], [REL, 16], [1, T]])
                sp.dma_start(nb[16 * a:16 * a + 16, :, :], src).then_inc(nb_in, 16)

        load_bias()
        a_slab(RING + 2)
        for i, name in enumerate(("k", "v")):
            sp.dma_start(cw1[:, i, :, :], t[f"ev_cmp_w1_{name}"][0].rearrange("(m p) j -> p m j", p=P)).then_inc(ld["cw"], 16)
            for half in range(2):
                sp.dma_start(cw2[:, i, half * HD:(half + 1) * HD], t[f"ev_cmp_w2_{name}"][0]).then_inc(ld["cw"], 16)
        sp.dma_start(b_f, t["b_forget_2"].rearrange("a h -> h a"),).then_inc(ld["bf"], 16)
        for j in range(RING + 3, 12):
            a_slab(j)

        def cols(name, w, n, body):
            s0 = st[name].s0
            with sp.Fori(0, n // body) as i:
                for j in range(body):
                    slab(s0 + i * body + j, s0 + j, w[:, :, bass.ds(i * (body * NS) + j * NS, NS)])

        def groups(name, w, per, k, body):
            s0, n = st[name].s0, st[name].n
            with sp.Fori(0, n // body) as i:
                for j in range(body):
                    g, r = j // per, j % per
                    slab(s0 + i * body + j, s0 + j,
                         w[:, r * k:(r + 1) * k, bass.ds(i * (body // per * NS) + g * NS, NS)], k=k)

        for l, (pre, wi, wo) in enumerate((("a", None, "ev_w_out"), ("m", "od_w_in", "od_w_out"))):
            if wi:
                for j in range(12):
                    s, c0 = st["m_in"].s0 + j, j % 3 * D + j // 3 * NS
                    slab(s, s, rows(t[wi][0])[:, :, c0:c0 + NS])
                    if j == 2:
                        sp.wait_ge(slab_done, st["m_in"].s0)
                        load_bias()
            for j in range(4):
                s = st[pre + "_out"].s0 + j
                slab(s, s, rows(t[wo][0])[:, :, j * NS:(j + 1) * NS])
            cols(pre + "_up", rows(t["mlp_w1"][l]), 16, 4)
            groups(pre + "_dn", rows(t["mlp_w2"][l]), 4, KS, 8)
        w_r = rows(t["w_in_2"][0])
        for j in range(5):
            s = st["r_xa"].s0 + j
            slab(s, s, w_r[:, :, j * NS:(j + 1) * NS])

        def load_gates():
            sp.wait_ge(gz, 1)
            for i, name in enumerate(("w_rg_a_2", "w_rg_x_2")):
                for (c, r, n, b, r0) in pieces[:len(pieces) // 2]:
                    first = b * RNN_BLOCK - (c - 1) * P
                    sp.dma_start(gw[r:r + n, i, :, :, :].rearrange("p (h c) a b -> p h c (a b)", h=2)
                                 [:, :, c, first:first + RNN_BLOCK],
                                 t[name][0].rearrange("(h b) r c -> r h b c", h=2)[r0:r0 + n, :, b, :])\
                        .then_inc(ld["gw"], 16)

        QKV = 2 * D_RNN
        GA = QKV + 3 * D + ATT_H
        s = st["r_f"].s0
        slab(s, s, w_r[:, :, QKV + 3 * D:GA], n=ATT_H)
        for j in range(8):
            s = st["r_gate"].s0 + j
            c0 = GA + (j + 4) % 8 * NS
            slab(s, s, w_r[:, :, c0:c0 + NS])
            if j == 0:
                load_gates()
        for j in range(5):
            s = st["r_ga"].s0 + j
            slab(s, s, w_r[:, :, D_RNN + j * NS:D_RNN + (j + 1) * NS])
        for j in range(4):
            s = st["r_v"].s0 + j
            slab(s, s, w_r[:, :, QKV + 2 * D + j * NS:QKV + 2 * D + (j + 1) * NS])
        groups("r_pa", rows(t["w_proj_a_2"][0]), 2, NR // 2, 8)
        cols("r_qk", w_r[:, :, QKV:QKV + 2 * D], 8, 4)
        for name, w in (("r_pb", "w_proj_b_2"), ("r_out", "w_out_2")):
            for j in range(4):
                s = st[name].s0 + j
                slab(s, s, rows(t[w][0])[:, :, j * NS:(j + 1) * NS])
        w_u = rows(t["w_up_2"][0]).rearrange("p k (v n) -> p k v n", v=2)
        with sp.Fori(0, 6) as i:
            for j in range(4):
                slab(st["f_up"].s0 + i * 4 + j, st["f_up"].s0 + j,
                     w_u[:, :, j % 2, bass.ds(i * 2 * NS + j // 2 * NS, NS)])
        sp.dma_start(gain_row[:, :], t["ffn_norm_post_2"].to_broadcast([P, D])).then_inc(ld["gain"], 16)
        groups("f_dn", rows(t["w_down_2"][0]), 3, KS, 12)
        for k in range(4):
            tb, c = k // 2, slice(k % 2 * (D // 2), (k % 2 + 1) * (D // 2))
            sp.wait_ge(o_done, k + 1)
            sp.dma_start(out[0, tb * P:(tb + 1) * P, c], fo[:, tb, c]).then_inc(o_out, 16)
        sp.wait_ge(o_out, 64)

    @block.gpsimd
    def _(pool):
        chain = [1]
        pool.memset(ident[:, :], 0.0).then_inc(pool_c, 1)
        pool.memset(eps_ones[:, :], EPS).then_inc(epso, 1)
        pool.memset(ones[:, :], 1.0).then_inc(idn, 1)
        pool.wait_ge(pool_c, 1)
        pool.affine_select(out=ident[:, :], in_=ident[:, :], compare_op=ALU.not_equal, fill=1.0, base=0,
                           pattern=[[-1, P]], channel_multiplier=1).then_inc(idn, 1)

        def link(ins):
            chain[0] += 1
            ins.then_inc(pool_c, 1)
            pool.wait_ge(pool_c, chain[0])

        def squares(n, src=x):
            if n:
                pool.wait_ge(stat_ok, n)
            for gi in range(4):
                pool.wait_ge(*x_ready(n, gi))
                dst = sq[:, 0, :, :] if gi else sq_sum[:, 0, :, :]
                v = src[:, 2 * gi:2 * gi + 2, :]
                ins = pool.tensor_tensor(dst, v, v, ALU.mult)
                if gi and not (n in DIRECT and gi == 3):
                    link(ins)
                    ins = pool.tensor_tensor(sq_sum[:, 0, :, :], sq_sum[:, 0, :, :], sq[:, 0, :, :], ALU.add)
                if n == 4 and gi < 3:
                    link(ins)
                    pool.wait_ge(sqg, gi + 1)
                    if gi == 0:
                        ins = pool.tensor_copy(sq_sum[:, 1, :, :], sq[:, 1, :, :])
                    else:
                        ins = pool.tensor_tensor(sq_sum[:, 1, :, :], sq_sum[:, 1, :, :], sq[:, 1, :, :], ALU.add)
                if gi < 3 and n == 4:
                    ins.then_inc(sqg_used, 1)
                    pool.wait_ge(sqg_used, gi + 1)
                elif gi < 3:
                    link(ins)
                else:
                    ins.then_inc(sq_ok, 1)

        squares(0)
        pool.wait_ge(nb_in, 128)
        pool.affine_select(out=nb[:, :, P:T], in_=nb[:, :, P:T], compare_op=ALU.is_ge, fill=BIG, base=0,
                           pattern=[[0, 16], [-1, P]], channel_multiplier=1).then_inc(nb_ok, 1)
        squares(1)
        squares(2)
        pool.wait_ge(nb_in, 256)
        pool.affine_select(out=nb[:, :, P:T], in_=nb[:, :, P:T], compare_op=ALU.is_ge, fill=BIG, base=0,
                           pattern=[[0, 16], [-1, P]], channel_multiplier=1).then_inc(nb_ok, 1)
        squares(3)
        squares(4)
        pool.wait_ge(slab_done, st["m_dn"].s0 + st["m_dn"].n)
        pool.memset(xap[:, :, 0:CONV_A - 1], 0.0).then_inc(zero_pad, 1)
        for i in range(2):
            ins = pool.memset(gw[:, i, :, :, :], 0.0)
        ins.then_inc(gz, 1)
        for j in range(NR):
            pool.wait_ge(rg["sig"], j + 1)
            pool.tensor_tensor(rix[:, j, :], rix[:, j, :], xc[:, j, :], ALU.mult).then_inc(rg["ix"], 1)
        for h in range(2):
            pool.wait_ge(rg["sq"], h + 1)
            c = slice(h * NR // 2, (h + 1) * NR // 2)
            link(pool.tensor_tensor(rt[:, c, :], rt[:, c, :], rr[:, c, :], ALU.mult))
            pool.tensor_tensor(rt[:, c, :], rt[:, c, :], rix[:, c, :], ALU.mult).then_inc(rg["b2"], 1)
        pool.wait_ge(fin_, 32)
        pool.wait_ge(fcq_ok, 1)
        for c0, n, b in ((0, P, 0), (P, T, 1)):
            link(pool.tensor_tensor(nb2[:, :, c0:c0 + n], nb2[:, :, c0:c0 + n],
                                    fcq[:, b, :].unsqueeze(2).to_broadcast([P, 16, n]), ALU.subtract))
            pool.affine_select(out=nb2[:, :, 2 * c0:2 * c0 + P], in_=nb2[:, :, 2 * c0:2 * c0 + P],
                               compare_op=ALU.is_ge, fill=BIG, base=0, pattern=[[0, 16], [-1, P]],
                               channel_multiplier=1).then_inc(fnb, 1)
        pool.wait_ge(sq5, 2)
        link(pool.tensor_tensor(sq4[:, 0, :, :], sq4[:, 0, :, :], sq4[:, 1, :, :], ALU.add))
        pool.wait_ge(sq5, 3)
        pool.tensor_tensor(sq4[:, 0, :, :], sq4[:, 0, :, :], sq4[:, 2, :, :], ALU.add).then_inc(sq_ok, 1)
        pool.wait_ge(slab_done, st["r_out"].s0 + 4)
        pool.memset(upad[:, :, :, 0:CONV_F - 1], 0.0).then_inc(zero_pad, 1)
        pool.wait_ge(rs_ok, 6)
        for gi in (2, 3):
            c = slice(2 * gi, 2 * gi + 2)
            link(pool.tensor_tensor(mo[:, c, :], mo[:, c, :], rs[:, 1, :].unsqueeze(1).to_broadcast([P, 2, T]), ALU.mult))
            pool.tensor_tensor(x[:, c, :], x[:, c, :], mo[:, c, :], ALU.add).then_inc(x_new_p, 1)

        def product(q, b):
            pool.wait_ge(fug, q + 1)
            pool.wait_ge(fud, q * 8 + 8)
            pool.tensor_tensor(hp[:, b, :, :], ucv[:, 0, :, :], ucv[:, 1, :, :], ALU.mult).then_inc(fup, 1)

        for q in range(2):
            product(q, q)
        with pool.Fori(1, 6) as i:
            for b in range(2):
                pool.wait_ge(ful, i * 2 + b - 1)
                product(i * 2 + b, b)

    @block.scalar
    def _(act):
        def split_hi(s, j):
            if isinstance(s, int) and s >= n_slabs:
                return
            slot = j % RING
            extra = raw_extra(slot, j)
            act.wait_ge(raw_in[slot], (s - j + (j // RING + 1) * RING) * (16 // RING) + extra)
            if not (isinstance(s, int) and s < RING):
                act.wait_ge(slab_done, s - RING + 1)
            act.activation(w_hi[:, slot, :, :], raw[:, slot, :, :], ACT.Copy).then_inc(hi_done, 1)

        def split_x(n):
            for gi in range(4):
                act.wait_ge(*x_ready(n, gi))
                for c in (2 * gi, 2 * gi + 1):
                    act.activation(act_hi[:, c, :], x[:, c, :], ACT.Copy, scale=gain(n, c)).then_inc(xh, 1)
                if n == 4:
                    if gi:
                        act.wait_ge(sqg_used, gi)
                    for c in (2 * gi, 2 * gi + 1):
                        ins = act.activation(sq[:, 1, c % 2, :], x[:, c, :], ACT.Square, scale=col("norm_final", c))
                    ins.then_inc(sqg, 1)

        def root(n):
            act.wait_ge(stat_ok, n + 1)
            act.activation(sd[:, :], ps_s[:, 0, 0:T], ACT.Sqrt, scale=1.0 / D, bias=eps2_c if n == 4 else eps_c)\
                .then_inc(sd_ok, 1)

        def tok(s, g, dst, func=ACT.Copy, n=NS):
            act.wait_ge(slab_done, s + 1)
            for tb in range(TB):
                ins = act.activation(dst[:, tb, :], ps_g[:, g % 2, tb * NS:tb * NS + n], func, scale=rs_tok[:, tb:tb + 1])
            ins.then_inc(emptied[g % 2], 1)

        def attention(p, slab_step=None, compress=None):
            a, units = att[p], UNITS[p]
            n_units = len(units)
            for i in range(n_units + LAG_HI):
                if i in IN_STEPS[p]:
                    slab_step(IN_STEPS[p][i])
                if p == 0 and i == CMP1_STEP + 1:
                    compress()
                if i < n_units:
                    u = units[i]
                    act.wait_ge(a["logit"], i + 1)
                    for b, (c0, n) in enumerate(u["blocks"]):
                        v = prob[:, i % PB, c0:c0 + n]
                        ins = act.activation(v, v, ACT.Exp, scale=-1.0, bias=nmin[:, i, b:b + 1],
                                             accum_out=psum_[:, i, b:b + 1])
                    ins.then_inc(a["prob"], 1)
                if LAG_T <= i < n_units + LAG_T and units[i - LAG_T]["pv"] is not None:
                    u = units[i - LAG_T]
                    n = u["n"]
                    act.wait_ge(a["tr"], n + 1)
                    if n >= 2:
                        act.wait_ge(a["pv"], n - 1)
                    pt_ = prob_ts[p // 2]
                    if u["cmp"]:
                        act.activation(pt_[0:NC0, n % 2, 0:P], ps_t[0:NC0, n % 2, 0:P], ACT.Copy)
                        act.activation(pt_[0:NC, n % 2, P:T], ps_t[0:NC, n % 2, P:T], ACT.Copy).then_inc(a["trc"], 1)
                    else:
                        act.activation(pt_[:, n % 2, :], ps_t[:, n % 2, 0:384], ACT.Copy).then_inc(a["trc"], 1)
                if i >= LAG_HI and units[i - LAG_HI]["pv"] is not None and units[i - LAG_HI]["last"]:
                    u = units[i - LAG_HI]
                    act.wait_ge(a["pv"], u["n"] + 1)
                    o = u["out"]
                    dst = dob[:, o - 4, :] if "diff" in u else (mix_hi if p < 2 else act_hi)[:, o, :]
                    act.activation(dst, ps_o[:, u["seq"] % 2, 0:T], ACT.Copy).then_inc(a["oh"], 1)
                    if "diff" in u:
                        act.wait_ge(a["oh"], o - 3)
                        act.activation(dsq[:, o - 4, :], dob[:, o - 4, :], ACT.Square).then_inc(dn["sq"], 1)
                if p == 0 and i == DN_ROOT:
                    act.wait_ge(dn["ps"], DIFF_H)
                    act.activation(dsq[:, :, :].rearrange("p (a b) n -> p a (b n)", a=2), ps_g[:, :, :], ACT.Sqrt,
                                   scale=1.0 / P, bias=eps_c).then_inc(dn["sd"], 1)
                if p == 0 and i in DN_HI:
                    h = DN_HI.index(i)
                    act.wait_ge(dn["o2"], h + 1)
                    act.activation(mix_hi[:, 4 + h, :], dob[:, h, :], ACT.Copy).then_inc(dn["hi"], 1)

        n = PARAMS["norm_mix"][2]
        act.dma_start(prow[0:n, 0, :], t["norm_mix"].rearrange("a (r c) -> (a r) c", c=P)).then_inc(ld["g"], 16)
        split_hi(0, 0)
        act.wait_ge(par_ok, 1)
        split_x(0)
        for s in range(1, AHEAD):
            split_hi(s, s)
        root(0)

        def a_slab(j):
            s = st["a_in"].s0 + j
            split_hi(s + AHEAD, s + AHEAD)
            if j == DV0:
                act.wait_ge(rst_ok, 1)
            dst = {SV: sv[:, :, :], GATE: gates[:, :, :], DV0: dv[:, :, 0:NS], DV1: dv[:, :, NS:2 * NS]}
            if j in dst:
                tok(s, st["a_in"].g0 + A_GROUPS[j], dst[j], ACT.Sigmoid if j == GATE else ACT.Copy, A_SLABS[j][1]
                    if j == GATE else NS)

        def compress():
            b = (st["a_in"].g0 + CMP1_GROUP) % 2
            act.wait_ge(cmp_ps, 1)
            for i in range(2):
                ins = act.activation(cposb[:, i:i + 1], ps_g[:, b, i * T + 2 * NC:i * T + 2 * NC + 1], ACT.Copy)
            ins.then_inc(cmp_b, 1)
            act.wait_ge(cmp_b, 1)
            for i in range(2):
                ins = act.activation(chid[:, i, :], ps_g[:, b, i * T:i * T + 2 * NC], ACT.Gelu_apprx_tanh, bias=cposb[:, i:i + 1])
            ins.then_inc(emptied[b], 1)

        for j in range(5):
            a_slab(j)
        act.wait_ge(lam_ok, 1)
        act.activation(small[:, 6:8], small[:, 6:8], ACT.Exp).then_inc(lam_e, 1)
        attention(0, a_slab, compress)

        def out_stage(name, n):
            for j in range(4):
                s = st[name].s0 + j
                split_hi(s + AHEAD, s + AHEAD)
            split_x(n)

        def mlp_up(name, n):
            root(n)
            s0, g0 = st[name].s0, st[name].g0
            with act.Fori(0, 4) as i:
                for j in range(4):
                    split_hi(s0 + i * 4 + j + AHEAD, s0 + j + AHEAD)
                    g = g0 + j
                    act.wait_ge(emptied[g % 2], out_count(g) + i * 2)
                    act.activation(hid_hi[:, bass.ds(i * 8 + j * 2, 2), :], up_r[:, j % 2, :, :], ACT.Square)\
                        .then_inc(hid_h, 1)

        def mlp_dn(name, n):
            s0 = st[name].s0
            with act.Fori(0, 2) as i:
                for j in range(8):
                    split_hi(s0 + i * 8 + j + AHEAD, s0 + j + AHEAD)
            if n in PRE:
                split_x(n)

        out_stage("a_out", 1)
        mlp_up("a_up", 1)
        mlp_dn("a_dn", 2)
        root(2)

        def m_slab(j):
            s = st["m_in"].s0 + j
            split_hi(s + AHEAD, s + AHEAD)
            if j == 2:
                act.wait_ge(rst_ok, 2)
            if j % 3 == 2:
                tok(s, st["m_in"].g0 + j, mv[:, :, j // 3 * NS:(j // 3 + 1) * NS])

        for j in range(3):
            m_slab(j)
        attention(1, m_slab)
        out_stage("m_out", 3)
        mlp_up("m_up", 3)
        mlp_dn("m_dn", 4)
        act.wait_ge(sp_d, 1)
        act.activation(spw[:, 0:10], spw[:, 0:10], ACT.Exp).then_inc(sp_a, 1)
        root(4)
        for j in range(5):
            s = st["r_xa"].s0 + j
            split_hi(s + AHEAD, s + AHEAD)
            act.wait_ge(emptied[(st["r_xa"].g0 + j) % 2], out_count(st["r_xa"].g0 + j))
            for c in (2 * j, 2 * j + 1):
                ins = act.activation(xc[:, c, :], xap[:, c, CONV_A - 1:], ACT.Identity,
                                     scale=col("conv_a_w_2", (CONV_A - 1) * NR + c), bias=col("conv_a_b_2", c))
            ins.then_inc(cva, 1)
        act.wait_ge(rst_ok, 3)
        act.activation(rs_f[:, :], ps_s[:, 1, T:2 * T], ACT.Sqrt, scale=1.0 / D, bias=eps_c).then_inc(sdf, 1)
        split_hi(st["r_f"].s0 + AHEAD, st["r_f"].s0 + AHEAD)
        act.wait_ge(fz, 1)
        act.wait_ge(ld["bf"], 16)
        act.activation(fl[:, 1, :], fl[:, 0, :], ACT.Identity, bias=b_f).then_inc(fa, 1)
        act.wait_ge(fz, 2)
        act.activation(fl[:, 3, :], fl[:, 3, :], ACT.Exp).then_inc(fa, 1)
        act.wait_ge(fa, 2)
        act.activation(fl[:, 4, :], fl[:, 3, :], ACT.Ln, bias=one_c[0:16, :]).then_inc(fa, 1)
        act.wait_ge(fcum, 1)
        act.dma_start(scr_c, fl[:, 5, :]).then_inc(fout, 16)
        for j in range(8):
            s = st["r_gate"].s0 + j
            split_hi(s + AHEAD, s + AHEAD)
            g = st["r_gate"].g0 + j
            act.wait_ge(emptied[g % 2], out_count(g))
            for c in (2 * (j % 4), 2 * (j % 4) + 1):
                dst = (sga if j >= 4 else sgb)[:, c, :]
                ins = act.activation(dst, dst, ACT.Sigmoid, bias=col("b_merge_2", c + (0 if j >= 4 else NX)))
            ins.then_inc(gs2, 1)
            if j == RG_STEP:
                act.wait_ge(sp_d, 2)
                for j in range(NR):
                    act.wait_ge(rg["ps"], j + 1)
                    act.activation(rt[:, j, :], ps_s[:, j % 2, 0:T], ACT.Sigmoid, bias=col("b_rg_a_2", j)).then_inc(act_c, 1)
                    act.activation(rix[:, j, :], ps_s[:, j % 2, T:2 * T], ACT.Sigmoid, bias=col("b_rg_x_2", j)).then_inc(rg["sig"], 1)
                    act.wait_ge(act_c, j + 1)
                    act.activation(rt[:, j, :], rt[:, j, :], ACT.Tanh, scale=sp4[:, j:j + 1]).then_inc(rg["den"], 1)
            if j in (4, 7):
                h = (j - 4) // 3
                act.wait_ge(rg["a"], h + 1)
                v = rt[:, h * NR // 2:(h + 1) * NR // 2, :]
                act.activation(v, v, ACT.Sqrt, scale=4.0).then_inc(rg["sq"], 1)
        for j in range(5):
            s = st["r_ga"].s0 + j
            split_hi(s + AHEAD, s + AHEAD)
            g = st["r_ga"].g0 + j
            act.wait_ge(emptied[g % 2], out_count(g))
            act.activation(gt[:, j % 2, :, :], gt[:, j % 2, :, :], ACT.Gelu_apprx_tanh).then_inc(yg, 1)
            act.wait_ge(yy, j + 1)
            act.activation(ya_hi[:, 2 * j:2 * j + 2, :], gt[:, j % 2, :, :], ACT.Copy).then_inc(yh, 1)
        act.wait_ge(rg["h"], 2)
        for j in range(4):
            s = st["r_v"].s0 + j
            split_hi(s + AHEAD, s + AHEAD)
            tok(s, st["r_v"].g0 + j, fv[:, :, j * NS:(j + 1) * NS])
        for j in range(8):
            split_hi(st["r_pa"].s0 + j + AHEAD, st["r_pa"].s0 + j + AHEAD)
        act.wait_ge(fout, 16)
        act.wait_ge(slab_done, st["r_qk"].s0)
        for c0, n in ((0, P), (P, T)):
            act.dma_start(nb2[:, :, c0:c0 + n], bass.AP(tensor=scr_c.tensor, offset=0, ap=[[0, P], [T, 16], [1, n]]))\
                .then_inc(fin_, 16)
        with act.Fori(0, 2) as i:
            for j in range(4):
                split_hi(st["r_qk"].s0 + i * 4 + j + AHEAD, st["r_qk"].s0 + j + AHEAD)
        attention(2)
        for j in range(4):
            s = st["r_pb"].s0 + j
            split_hi(s + AHEAD, s + AHEAD)
            g = st["r_pb"].g0 + j
            act.wait_ge(emptied[g % 2], out_count(g))
            act.activation(m2_hi[:, 2 * j:2 * j + 2, :], mg[:, 2 * j:2 * j + 2, :], ACT.Copy).then_inc(pbh, 1)
        for j in range(4):
            s = st["r_out"].s0 + j
            split_hi(s + AHEAD, s + AHEAD)
            act.wait_ge(slab_done, s + 1)
            act.activation(sq4[:, j, :, :], ps_g[:, (st["r_out"].g0 + j) % 2, :].rearrange("p (a n) -> p a n", a=2),
                           ACT.Square).then_inc(sq5, 1)
        root(5)

        def square6(gi):
            act.activation(sq4[:, gi, :, :], x[:, 2 * gi:2 * gi + 2, :], ACT.Square).then_inc(sq6, 1)

        for gi in range(4):
            act.wait_ge(*x_ready(6, gi))
            for c in (2 * gi, 2 * gi + 1):
                act.activation(act_hi[:, c, :], x[:, c, :], ACT.Copy, scale=gain(6, c)).then_inc(xh, 1)
            if gi == 2:
                square6(0)
                square6(1)
        square6(2)
        square6(3)
        root(6)
        s0, g0 = st["f_up"].s0, st["f_up"].g0

        def hi_of(q, b):
            act.wait_ge(fup, q + 1)
            act.activation(h2_hi[:, bass.ds(q * 2, 2) if not isinstance(q, int) else slice(2 * q, 2 * q + 2), :],
                           hp[:, b, :, :], ACT.Copy).then_inc(fuh, 1)

        def up_step(i, j, first=False):
            split_hi(s0 + i * 4 + j + AHEAD, s0 + j + AHEAD)
            if j % 2:
                act.wait_ge(fud, i * 16 + j * 4)
                act.activation(ucv[:, 0, :, :], ucv[:, 0, :, :], ACT.Gelu_apprx_tanh).then_inc(fug, 1)
            elif not first:
                hi_of(i * 2 + j // 2 - 1, (j // 2 + 1) % 2)
            g = g0 + j
            act.wait_ge(emptied[g % 2], out_count(g) + i * 2)
            for c in range(2):
                wcol, bcol = conv_cols(i, j, c)
                ins = act.activation(ucv[:, j % 2, c, :], upad[:, j % 2, c, CONV_F - 1:], ACT.Identity,
                                     scale=wcol, bias=bcol)
            ins.then_inc(fuc, 1)

        for j in range(4):
            up_step(0, j, first=(j == 0))
        with act.Fori(1, 6) as i:
            for j in range(4):
                up_step(i, j)
        hi_of(11, 1)
        for j in range(12):
            s = st["f_dn"].s0 + j
            split_hi(s + AHEAD, s + AHEAD)
            if j % 3 == 2:
                act.wait_ge(slab_done, s + 1)
                gi = j // 3
                for tb in range(TB):
                    ins = act.activation(fsq[:, tb, :], ps_g[:, (st["f_dn"].g0 + gi) % 2, tb * NS:(tb + 1) * NS],
                                         ACT.Square, accum_out=ssq[:, tb, gi:gi + 1])
                ins.then_inc(fsq_ok, 1)
        act.wait_ge(fsum, 3)
        act.activation(rs_o[:, :], ssq[:, :, 0], ACT.Sqrt, scale=1.0 / D, bias=eps_c).then_inc(fsd, 1)

    @block.vector
    def _(dve):
        chain = [0]

        def link(ins):
            chain[0] += 1
            ins.then_inc(dve_c, 1)
            dve.wait_ge(dve_c, chain[0])

        def split_lo(s, j):
            if isinstance(s, int) and s >= n_slabs:
                return
            slot = j % RING
            dve.wait_ge(hi_done, s + 1)
            dve.tensor_tensor(w_lo[:, slot, :, :], raw[:, slot, :, :], w_hi[:, slot, :, :].bitcast(F32), ALU.subtract)\
                .then_inc(w_ready, 1)

        def split_x(n):
            for c in range(NX):
                dve.wait_ge(xh, PRE_I[n] * NX + c + 1)
                dve.scalar_tensor_tensor(out=act_lo[:, c, :], in0=x[:, c, :], scalar=gain(n, c),
                                         in1=act_hi[:, c, :].bitcast(F32), op0=ALU.mult, op1=ALU.subtract).then_inc(xl, 1)

        def inv_rms(n):
            dve.wait_ge(sd_ok, n + 1)
            dve.reciprocal(rs[:, 1, :], sd[:, :]).then_inc(rs_ok, 1)
            dve.wait_ge(rs_ok, n + 1)
            if n in TOK:
                dve.tensor_scalar(rs[:, 0, :], rs[:, 1, :], -0.125, None, ALU.mult).then_inc(rsq_ok, 1)
                dve.wait_ge(rsq_ok, TOK[n] + 1)

        def rms_tok(n):
            dve.wait_ge(rst_ps, TOK[n] + 1)
            dve.tensor_copy(rs_tok[:, :], ps_s[:, 1, 0:TB]).then_inc(rst_ok, 1)

        def bcast(ap, n=2):
            return ap.unsqueeze(1).to_broadcast([P, n, T])

        def pair(g):
            return ps_g[:, g % 2, :].rearrange("p (a n) -> p a n", a=2)

        def attention(p, slab_step=None, compress=None):
            a, units = att[p], UNITS[p]
            n_units = len(units)
            for i in range(n_units + LAG_LO):
                if i in IN_STEPS[p]:
                    slab_step(IN_STEPS[p][i])
                if p == 0 and i == CMP2_STEP + 1:
                    compress()
                if p == 0 and i == 8 + LAG_N:
                    g = st["a_in"].g0 + A_GROUPS[GATE]
                    dve.wait_ge(emptied[g % 2], out_count(g))
                if i < n_units:
                    u = units[i]
                    dve.wait_ge(a["score"], i + 1)
                    if i >= PB and freed_by(units, i):
                        dve.wait_ge(a["tr"], freed_by(units, i))
                    for b, (c0, n) in enumerate(u["blocks"]):
                        ins = dve.tensor_tensor_reduce(
                            out=prob[:, i % PB, c0:c0 + n], in0=ps_s[:, i % 2, c0:c0 + n], in1=u["bias"][b],
                            scale=1.0, scalar=u["init"], op0=ALU.add, op1=ALU.min, accum_out=nmin[:, i, b:b + 1])
                    ins.then_inc(a["logit"], 1)
                if LAG_N <= i < n_units + LAG_N:
                    k = i - LAG_N
                    u = units[k]
                    dve.wait_ge(a["prob"], k + 1)
                    if u["cmp"]:
                        link(dve.tensor_scalar(psum_[:, k, :], psum_[:, k, :], 1e-30, None, ALU.max))
                    link(dve.reciprocal(fac[:, k, :], psum_[:, k, :]))
                    if "gate" in u:
                        link(dve.tensor_tensor(fac[:, k, :], fac[:, k, :], gates[:, :, u["gate"]], ALU.mult))
                    if u.get("diff") == 1:
                        link(dve.tensor_scalar(fac[:, k, :], fac[:, k, :], lamn, None, ALU.mult))
                    for b, (c0, n) in enumerate(u["blocks"]):
                        v = prob[:, k % PB, c0:c0 + n]
                        if u.get("diff") == 1:
                            ins = dve.scalar_tensor_tensor(out=v, in0=v, scalar=fac[:, k, b:b + 1],
                                                           in1=prob[:, (k - 1) % PB, c0:c0 + n], op0=ALU.mult, op1=ALU.add)
                        else:
                            ins = dve.tensor_scalar(v, v, fac[:, k, b:b + 1], None, ALU.mult)
                    if u.get("diff") == 0:
                        link(ins)
                    else:
                        ins.then_inc(a["norm"], 1)
                if i >= LAG_LO:
                    u = units[i - LAG_LO]
                    if u["pv"] is not None and u["last"] and "diff" not in u:
                        o, seq = u["out"], u["seq"]
                        hi, lo = (mix_hi, mix_lo) if p < 2 else (act_hi, act_lo)
                        dve.wait_ge(a["oh"], seq + 1)
                        dve.tensor_tensor(lo[:, o, :], ps_o[:, seq % 2, 0:T], hi[:, o, :].bitcast(F32), ALU.subtract)\
                            .then_inc(a["ol"], 1)
                if p == 0 and i in DN_R:
                    h = DN_R.index(i)
                    dve.wait_ge(dn["sd"], 1)
                    dve.reciprocal(dsq[:, h, :], dsq[:, h, :]).then_inc(dn["r"], 1)
                    dve.wait_ge(dn["r"], h + 1)
                    dve.scalar_tensor_tensor(out=dob[:, h, :], in0=dob[:, h, :], scalar=sub8, in1=dsq[:, h, :],
                                             op0=ALU.mult, op1=ALU.mult).then_inc(dn["o2"], 1)
                if p == 0 and i in DN_LO:
                    h = DN_LO.index(i)
                    dve.wait_ge(dn["hi"], h + 1)
                    dve.tensor_tensor(mix_lo[:, 4 + h, :], dob[:, h, :], mix_hi[:, 4 + h, :].bitcast(F32), ALU.subtract)\
                        .then_inc(dn["lo"], 1)

        dve.memset(eps_c, EPS)
        dve.memset(one_c, 1.0)
        link(dve.memset(eps2_c, EPS * EPS))
        dve.wait_ge(par_t, 1)
        n_gain = PARAMS["norm_mix"][2]
        dve.tensor_copy(par[:, 0, 0:n_gain], ps_t[:, 1, 0:n_gain]).then_inc(par_ok, 1)
        dve.wait_ge(par_ok, 1)
        for gi in range(4):
            dve.wait_ge(xt, gi + 1)
            dve.tensor_copy(x[:, 2 * gi:2 * gi + 2, :], pair(gi)).then_inc(emptied[gi % 2], 1)
        split_lo(0, 0)
        split_x(0)
        split_lo(1, 1)
        dve.wait_ge(ld["lam"], 64)
        for i in range(2):
            ins = dve.tensor_tensor_reduce(out=lamv[:, 2 * i, :], in0=lamv[:, 2 * i, :], in1=lamv[:, 2 * i + 1, :],
                                           scale=1.0, scalar=0.0, op0=ALU.mult, op1=ALU.add,
                                           accum_out=small[:, 6 + i:7 + i])
        ins.then_inc(lam_ok, 1)
        inv_rms(0)
        q_pair = bcast(rs[:, 0, :])
        k_pair = bcast(rs[:, 1, :])

        def a_slab(j):
            s = st["a_in"].s0 + j
            split_lo(s + AHEAD - 1, s + AHEAD - 1)
            g = st["a_in"].g0 + A_GROUPS[j]
            if j == DV0:
                rms_tok(0)
            if j in (DV0, DV1, SV, GATE):
                return
            dve.wait_ge(slab_done, s + 1)
            if j == KV_CMP:
                for i in range(2):
                    for gg in range(2):
                        rws = slice(gg * HD, (gg + 1) * HD)
                        dve.tensor_tensor(cmp2[0:HD, i, gg, :], ps_g[rws, g % 2, i * T:(i + 1) * T], rs[rws, 1, :], ALU.mult)
                        ins = dve.tensor_tensor(cmp2[HD:P, i, gg, 0:T - 1], ps_g[rws, g % 2, i * T + 1:(i + 1) * T],
                                                rs[rws, 1, 1:T], ALU.mult)
            elif j == SKW:
                for i in range(2):
                    for gg in range(2):
                        rws = slice(gg * HD, (gg + 1) * HD)
                        for half in range(2):
                            ins = dve.tensor_tensor(skw[half * HD:(half + 1) * HD, i, gg, :],
                                                    ps_g[rws, g % 2, i * T:(i + 1) * T], rs[rws, 1, :], ALU.mult)
            else:
                dst = {Q0: aq[:, 0:2, :], Q1: aq[:, 2:4, :], DQ0: dqk[:, 0:2, :], DQ1: dqk[:, 2:4, :],
                       DK0: dqk[:, 4:6, :], DK1: dqk[:, 6:8, :]}[j]
                ins = dve.tensor_tensor(dst, pair(g), k_pair if j in (DK0, DK1) else q_pair, ALU.mult)
            ins.then_inc(emptied[g % 2], 1)

        def compress():
            b = (st["a_in"].g0 + CMP2_GROUP) % 2
            dve.wait_ge(cmp_ps2, 1)
            dve.tensor_copy(kc[:, :, :], ps_g[:, b, 0:2 * NC].rearrange("p (g c) -> p g c", g=2))
            dve.tensor_copy(vc[0:NC, :], ps_g[0:NC, b, T:T + P]).then_inc(emptied[b], 1)

        a_slab(0)
        dve.wait_ge(par_t, 2)
        for k in range(4):
            c0 = n_gain if k == 0 else 0
            ins = dve.tensor_copy(par[:, k, c0:TILE_ROWS[k]], ps_t[:, 0, k * P + c0:k * P + TILE_ROWS[k]])
        ins.then_inc(par_ok, 1)
        dve.wait_ge(brow_ps, 1)
        dve.tensor_copy(brow[:, :], ps_o[0:16, 0, 0:REL]).then_inc(brow_ok, 1)
        dve.wait_ge(par_ok, 2)
        dve.tensor_scalar(sub8, col("ev_subln"), 1.0 - 0.2, None, ALU.mult)
        link(dve.memset(cmp2[:, :, 2, :], 0.0))
        dve.tensor_copy(cmp2[:, :, 2, 0:CMP_BLOCK:2], par[:, 3, 0:32].rearrange("p (i m) -> p i m", i=2))
        for j in range(CONV_F):
            for c0, c1 in ((0, 2 * NH2),):
                r = j * 2 * NH2
                if r + 2 * NH2 <= P:
                    dve.tensor_copy(fw[:, j, :], par[:, 2, r:r + 2 * NH2])
                else:
                    n = P - r
                    dve.tensor_copy(fw[:, j, 0:n], par[:, 2, r:P])
                    dve.tensor_copy(fw[:, j, n:], par[:, CONV_F_TAIL[0], CONV_F_TAIL[1]:CONV_F_TAIL[1] + 16])
        link(dve.tensor_copy(fw[:, 3, :], col("conv_f_b_2", 0, 2 * NH2)))
        dve.tensor_tensor(gain_f[:, :], col("norm_final", 0, NX), col("mix_norm_pre_2", 0, NX), ALU.mult).then_inc(gain_ok, 1)
        for j in range(1, 5):
            a_slab(j)
        dve.wait_ge(lam_e, 1)
        link(dve.tensor_tensor(lamn, small[:, 7:8], small[:, 6:7], ALU.subtract))
        link(dve.tensor_scalar(lamn, lamn, 0.2, None, ALU.subtract))
        dve.wait_ge(nb_ok, 1)
        attention(0, a_slab, compress)

        def add_x(g, gi):
            dve.tensor_tensor(x[:, 2 * gi:2 * gi + 2, :], pair(g), x[:, 2 * gi:2 * gi + 2, :], ALU.add)\
                .then_inc(emptied[g % 2], 1)

        def out_stage(name, n):
            for j in range(4):
                s, g = st[name].s0 + j, st[name].g0 + j
                split_lo(s + AHEAD - 1, s + AHEAD - 1)
                dve.wait_ge(slab_done, s + 1)
                add_x(g, j)
            split_x(n)

        def mlp_up(name, n, l):
            inv_rms(n)
            s0, g0 = st[name].s0, st[name].g0
            with dve.Fori(0, 4) as i:
                for j in range(4):
                    split_lo(s0 + i * 4 + j + AHEAD - 1, s0 + j + AHEAD - 1)
                    g = g0 + j
                    dve.wait_ge(slab_done, s0 + i * 4 + j + 1)
                    dve.scalar_tensor_tensor(out=up_r[:, j % 2, :, :], in0=pair(g), scalar=0.0, in1=k_pair, op0=ALU.max,
                                             op1=ALU.mult).then_inc(emptied[g % 2], 1)
                    dve.wait_ge(emptied[g % 2], out_count(g) + i * 2)
                    dve.tensor_tensor(up_q[:, j % 2, :, :], up_r[:, j % 2, :, :], up_r[:, j % 2, :, :], ALU.mult)\
                        .then_inc(upr, 1)
                    dve.wait_ge(upr, l * 16 + i * 4 + j + 1)
                    dve.wait_ge(hid_h, l * 16 + i * 4 + j + 1)
                    c = bass.ds(i * 8 + j * 2, 2)
                    dve.tensor_tensor(hid_lo[:, c, :], up_q[:, j % 2, :, :], hid_hi[:, c, :].bitcast(F32), ALU.subtract)\
                        .then_inc(hid_l, 1)

        def mlp_dn(name, n):
            s0, g0 = st[name].s0, st[name].g0
            with dve.Fori(0, 2) as i:
                for j in range(8):
                    split_lo(s0 + i * 8 + j + AHEAD - 1, s0 + j + AHEAD - 1)
                    if j % 4 == 3:
                        g = g0 + j // 4
                        dve.wait_ge(slab_done, s0 + i * 8 + j + 1)
                        c = bass.ds(i * 4 + j // 4 * 2, 2)
                        dve.tensor_tensor(x[:, c, :], pair(g), x[:, c, :], ALU.add).then_inc(emptied[g % 2], 1)
            if n in PRE:
                split_x(n)

        def qk_stage(name, dst):
            s0, g0 = st[name].s0, st[name].g0
            with dve.Fori(0, 2) as i:
                for j in range(4):
                    split_lo(s0 + i * 4 + j + AHEAD - 1, s0 + j + AHEAD - 1)
                    g = g0 + j
                    dve.wait_ge(slab_done, s0 + i * 4 + j + 1)
                    dve.tensor_tensor(dst[:, bass.ds(i * 8 + 2 * j, 2), :], pair(g),
                                      rs[:, bass.ds(i, 1), :].to_broadcast([P, 2, T]), ALU.mult).then_inc(emptied[g % 2], 1)

        out_stage("a_out", 1)
        mlp_up("a_up", 1, 0)
        mlp_dn("a_dn", 2)
        inv_rms(2)

        def m_slab(j):
            s, g = st["m_in"].s0 + j, st["m_in"].g0 + j
            split_lo(s + AHEAD - 1, s + AHEAD - 1)
            if j == 2:
                rms_tok(2)
            if j % 3 < 2:
                dve.wait_ge(slab_done, s + 1)
                c = j % 3 * 8 + j // 3 * 2
                dve.tensor_tensor(mqk[:, c:c + 2, :], pair(g), (q_pair, k_pair)[j % 3], ALU.mult)\
                    .then_inc(emptied[g % 2], 1)

        for j in range(3):
            m_slab(j)
        dve.wait_ge(nb_ok, 2)
        attention(1, m_slab)
        out_stage("m_out", 3)
        mlp_up("m_up", 3, 1)
        mlp_dn("m_dn", 4)
        lam = col("lru_lambda_2", 0, 10)
        z, zz, s2, acc = (spw[:, 10 * k:10 * k + 10] for k in range(4))
        link(dve.tensor_scalar(zz, lam, -1.0, None, ALU.mult))
        dve.tensor_tensor(z, zz, lam, ALU.min).then_inc(sp_d, 1)
        dve.wait_ge(sp_a, 1)
        link(dve.tensor_scalar(zz, z, 2.0, None, ALU.add))
        link(dve.reciprocal(zz, zz))
        link(dve.tensor_tensor(z, z, zz, ALU.mult))
        link(dve.tensor_tensor(s2, z, z, ALU.mult))
        link(dve.tensor_scalar(acc, s2, 1.0 / 17, 1.0 / 15, ALU.mult, ALU.add))
        for k in (13, 11, 9, 7, 5, 3, 1):
            link(dve.tensor_tensor(acc, acc, s2, ALU.mult))
            link(dve.tensor_scalar(acc, acc, 1.0 / k, None, ALU.add))
        link(dve.tensor_tensor(acc, acc, z, ALU.mult))
        link(dve.tensor_scalar(zz, lam, -1.0, 0.0, ALU.mult, ALU.max))
        link(dve.scalar_tensor_tensor(out=acc, in0=acc, scalar=2.0, in1=zz, op0=ALU.mult, op1=ALU.add))
        dve.tensor_scalar(sp4, acc, 4.0, None, ALU.mult).then_inc(sp_d, 1)
        inv_rms(4)
        dve.wait_ge(zero_pad, 1)
        k = 0
        for j in range(5):
            s, g = st["r_xa"].s0 + j, st["r_xa"].g0 + j
            if j == 0:
                split_lo(s + AHEAD - 1, s + AHEAD - 1)
            dve.wait_ge(slab_done, s + 1)
            dve.tensor_tensor(xap[:, 2 * j:2 * j + 2, CONV_A - 1:], pair(g), k_pair, ALU.mult).then_inc(emptied[g % 2], 1)
            if j == 2:
                rms_tok(4)
            split_lo(s + AHEAD, s + AHEAD)
            dve.wait_ge(cva, j + 1)
            dve.wait_ge(emptied[g % 2], out_count(g))
            for tap in range(CONV_A - 1):
                for c in (2 * j, 2 * j + 1):
                    if tap:
                        dve.wait_ge(cvd, k - 1)
                    dve.scalar_tensor_tensor(out=xc[:, c, :], in0=xap[:, c, tap:tap + T],
                                             scalar=col("conv_a_w_2", tap * NR + c), in1=xc[:, c, :], op0=ALU.mult,
                                             op1=ALU.add).then_inc(cvd, 1)
                    k += 1
        s, g = st["r_f"].s0, st["r_f"].g0
        dve.wait_ge(slab_done, s + 1)
        dve.tensor_tensor(fl[:, 0, :], ps_g[0:16, g % 2, 0:T], rs[0:16, 1, :], ALU.mult).then_inc(fz, 1)
        dve.wait_ge(fa, 1)
        link(dve.tensor_scalar(fl[:, 2, :], fl[:, 1, :], 0.0, None, ALU.min))
        dve.scalar_tensor_tensor(out=fl[:, 3, :], in0=fl[:, 2, :], scalar=2.0, in1=fl[:, 1, :], op0=ALU.mult,
                                 op1=ALU.subtract).then_inc(fz, 1)
        dve.memset(fl[:, 0, :], 1.0).then_inc(emptied[g % 2], 1)
        dve.wait_ge(emptied[g % 2], out_count(g))
        dve.wait_ge(fa, 3)
        link(dve.tensor_tensor(fl[:, 2, :], fl[:, 2, :], fl[:, 4, :], ALU.subtract))
        dve.tensor_tensor_scan(fl[:, 5, :], fl[:, 0, :], fl[:, 2, :], 0.0, ALU.mult, ALU.add).then_inc(fcum, 1)
        def decay(j):
            dve.wait_ge(rg["den"], j + 1)
            dve.wait_ge(rg["ps"], min(j + 2, NR))
            dve.wait_ge(rg["ix"], j + 1)
            link(dve.tensor_scalar(rr[:, j, :], rt[:, j, :], 1.0, None, ALU.add))
            dve.reciprocal(rr[:, j, :], rr[:, j, :]).then_inc(rcp, 1)

        def decay_a(h):
            dve.wait_ge(rcp, (h + 1) * NR // 2)
            dve.wait_ge(rg["ps"], NR)
            c = slice(h * NR // 2, (h + 1) * NR // 2)
            dve.tensor_scalar(ra[:, c, :], rr[:, c, :], 2.0, -1.0, ALU.mult, ALU.add).then_inc(rg["a"], 1)

        def scan(h):
            dve.wait_ge(rg["b2"], h + 1)
            dve.wait_ge(rg["a"], h + 1)
            if h == 0:
                dve.wait_ge(rg["b2"], 1)
            for j in range(h * NR // 2, (h + 1) * NR // 2):
                ins = dve.tensor_tensor_scan(hr[:, j, :], ra[:, j, :], rt[:, j, :], 0.0, ALU.mult, ALU.add)
            ins.then_inc(rg["h"], 1)

        for j in range(8):
            s, g = st["r_gate"].s0 + j, st["r_gate"].g0 + j
            split_lo(s + AHEAD - 1, s + AHEAD - 1)
            dve.wait_ge(slab_done, s + 1)
            if j == 4:
                dve.wait_ge(fcq_ps, 1)
                dve.tensor_copy(fcq[:, :, :], ps_s[:, 0, 0:32].rearrange("p (b h) -> p b h", b=TB)).then_inc(fcq_ok, 1)
                dve.wait_ge(fout, 16)
            dst = (sga if j >= 4 else sgb)[:, 2 * (j % 4):2 * (j % 4) + 2, :]
            dve.tensor_tensor(dst, pair(g), k_pair, ALU.mult).then_inc(emptied[g % 2], 1)
            for k in {RG_STEP: range(0, 9), RG_STEP + 1: (9,)}.get(j, ()):
                decay(k)
            if j == 3:
                decay_a(0)
        decay_a(1)
        scan(0)
        for j in range(5):
            s, g = st["r_ga"].s0 + j, st["r_ga"].g0 + j
            split_lo(s + AHEAD - 1, s + AHEAD - 1)
            dve.wait_ge(slab_done, s + 1)
            if j == 0:
                scan(1)
                dve.wait_ge(rg["h"], 2)
            if j >= 2:
                dve.wait_ge(yl, j - 1)
            dve.tensor_tensor(gt[:, j % 2, :, :], pair(g), k_pair, ALU.mult).then_inc(emptied[g % 2], 1)
            dve.wait_ge(yg, j + 1)
            dve.tensor_tensor(gt[:, j % 2, :, :], gt[:, j % 2, :, :], hr[:, 2 * j:2 * j + 2, :], ALU.mult).then_inc(yy, 1)
            dve.wait_ge(yy, j + 1)
            dve.wait_ge(yh, j + 1)
            dve.tensor_tensor(ya_lo[:, 2 * j:2 * j + 2, :], gt[:, j % 2, :, :],
                              ya_hi[:, 2 * j:2 * j + 2, :].bitcast(F32), ALU.subtract).then_inc(yl, 1)
        for j in range(4):
            s = st["r_v"].s0 + j
            split_lo(s + AHEAD - 1, s + AHEAD - 1)
        dve.wait_ge(sdf, 1)
        dve.reciprocal(rs_f[:, :], rs_f[:, :]).then_inc(rsf, 1)
        dve.wait_ge(rsf, 1)
        for c in range(NX):
            ins = dve.scalar_tensor_tensor(out=x[:, c, :], in0=x[:, c, :], scalar=col("norm_final", c), in1=rs_f[:, :],
                                           op0=ALU.mult, op1=ALU.mult)
        ins.then_inc(x_mat, 1)
        dve.wait_ge(gs2, 8)
        for j in range(8):
            s, g = st["r_pa"].s0 + j, st["r_pa"].g0 + j // 2
            split_lo(s + AHEAD - 1, s + AHEAD - 1)
            if j % 2:
                dve.wait_ge(slab_done, s + 1)
                dve.tensor_tensor(mg[:, j - 1:j + 1, :], pair(g), sga[:, j - 1:j + 1, :], ALU.mult).then_inc(emptied[g % 2], 1)
        qk_stage("r_qk", fqk)
        dve.wait_ge(fnb, 2)
        attention(2)
        for j in range(4):
            s, g = st["r_pb"].s0 + j, st["r_pb"].g0 + j
            split_lo(s + AHEAD - 1, s + AHEAD - 1)
            dve.wait_ge(slab_done, s + 1)
            c = slice(2 * j, 2 * j + 2)
            dve.tensor_tensor(sgb[:, c, :], pair(g), sgb[:, c, :], ALU.mult).then_inc(pbm, 1)
            dve.wait_ge(pbm, j + 1)
            dve.tensor_tensor(mg[:, c, :], sgb[:, c, :], mg[:, c, :], ALU.add).then_inc(emptied[g % 2], 1)
            dve.wait_ge(emptied[g % 2], out_count(g))
            dve.wait_ge(pbh, j + 1)
            dve.tensor_tensor(m2_lo[:, c, :], mg[:, c, :], m2_hi[:, c, :].bitcast(F32), ALU.subtract).then_inc(pbl, 1)

        for j in range(4):
            s, g = st["r_out"].s0 + j, st["r_out"].g0 + j
            split_lo(s + AHEAD - 1, s + AHEAD - 1)
            dve.wait_ge(sq5, j + 1)
            for c in range(2):
                ins = dve.tensor_scalar(mo[:, 2 * j + c, :], ps_g[:, g % 2, c * T:(c + 1) * T],
                                        col("mix_norm_post_2", 2 * j + c), None, ALU.mult)
            ins.then_inc(emptied[g % 2], 1)
        inv_rms(5)
        for gi in range(2):
            c = slice(2 * gi, 2 * gi + 2)
            link(dve.tensor_tensor(mo[:, c, :], mo[:, c, :], k_pair, ALU.mult))
            dve.tensor_tensor(x[:, c, :], x[:, c, :], mo[:, c, :], ALU.add).then_inc(x_new, 1)
        dve.wait_ge(x_new, 2)
        split_x(6)
        dve.wait_ge(sq6, 4)
        for k in (0, 2):
            ins = dve.tensor_tensor(sq4[:, k, :, :], sq4[:, k, :, :], sq4[:, k + 1, :, :], ALU.add)
        ins.then_inc(sq_ok, 1)
        inv_rms(6)
        dve.wait_ge(zero_pad, 2)
        s0, g0 = st["f_up"].s0, st["f_up"].g0

        def lo_of(q, b):
            dve.wait_ge(fuh, q + 1)
            c = slice(2 * q, 2 * q + 2) if isinstance(q, int) else bass.ds(q * 2, 2)
            dve.tensor_tensor(h2_lo[:, c, :], hp[:, b, :, :], h2_hi[:, c, :].bitcast(F32), ALU.subtract).then_inc(ful, 1)

        def up_step(i, j, first=False):
            g = g0 + j
            dve.wait_ge(slab_done, s0 + i * 4 + j + 1)
            if not (isinstance(i, int) and i * 4 + j < 2):
                dve.wait_ge(fud, i * 16 + j * 4 - 4)
            dve.tensor_tensor(upad[:, j % 2, :, CONV_F - 1:], pair(g), k_pair, ALU.mult).then_inc(emptied[g % 2], 1)
            split_lo(s0 + i * 4 + j + AHEAD - 1, s0 + j + AHEAD - 1)
            if j % 2 == 0 and not first:
                lo_of(i * 2 + j // 2 - 1, (j // 2 + 1) % 2)
            dve.wait_ge(emptied[g % 2], out_count(g) + i * 2)
            dve.wait_ge(fuc, i * 4 + j + 1)
            for tap in range(CONV_F - 1):
                for c in range(2):
                    if tap:
                        dve.wait_ge(fud, i * 16 + j * 4 + c + 1)
                    ch = (j % 2) * NH2 + 2 * (j // 2) + c
                    dve.scalar_tensor_tensor(out=ucv[:, j % 2, c, :], in0=upad[:, j % 2, c, tap:tap + T],
                                             scalar=fcol(tap, i, ch), in1=ucv[:, j % 2, c, :],
                                             op0=ALU.mult, op1=ALU.add).then_inc(fud, 1)

        for j in range(4):
            up_step(0, j, first=(j == 0))
        with dve.Fori(1, 6) as i:
            for j in range(4):
                up_step(i, j)
        lo_of(11, 1)
        dve.wait_ge(ld["gain"], 16)
        for j in range(12):
            s, g = st["f_dn"].s0 + j, st["f_dn"].g0 + j // 3
            split_lo(s + AHEAD - 1, s + AHEAD - 1)
            if j % 3 == 2:
                gi = j // 3
                dve.wait_ge(fsq_ok, gi + 1)
                dve.tensor_tensor(fo[:, :, gi * NS:(gi + 1) * NS], ps_g[:, g % 2, :].rearrange("p (b n) -> p b n", b=TB),
                                  gain_row[:, gi * NS:(gi + 1) * NS].unsqueeze(1).to_broadcast([P, TB, NS]), ALU.mult)\
                    .then_inc(emptied[g % 2], 1)
                if gi:
                    dve.tensor_tensor(ssq[:, :, 0], ssq[:, :, 0], ssq[:, :, gi], ALU.add).then_inc(fsum, 1)
                    dve.wait_ge(fsum, gi)
        dve.wait_ge(fsd, 1)
        dve.reciprocal(rs_o[:, :], rs_o[:, :]).then_inc(frs, 1)
        dve.wait_ge(frs, 1)
        dve.wait_ge(x_tok, 1)
        for k in range(4):
            tb, c = k // 2, slice(k % 2 * (D // 2), (k % 2 + 1) * (D // 2))
            dve.scalar_tensor_tensor(out=fo[:, tb, c], in0=fo[:, tb, c], scalar=rs_o[:, tb:tb + 1],
                                     in1=(ps_s, ps_o)[tb][:, k % 2, :], op0=ALU.mult, op1=ALU.add).then_inc(o_done, 1)

    @block.tensor
    def _(pe):
        def gemm(s, sj, g, gj, x_hi, x_lo, kc0=0, n_k=KS, first=True, last=True, tok_major=False, n=NS, m=None,
                 before_pair=None, before_chunk=None):
            slot, b = sj % RING, gj % 2
            pe.wait_ge(w_ready, s + 1)
            if first:
                pe.wait_ge(emptied[b], g)
            for k in range(n_k):
                if before_chunk is not None:
                    before_chunk(k)
                if before_pair is not None and k % 2 == 0:
                    before_pair(k // 2)
                passes = ((w_hi, x_hi), (w_hi, x_lo), (w_lo, x_hi))
                for half in range(2):
                    if m is not None and half:
                        break
                    for q, (w, xx) in enumerate(passes):
                        if tok_major:
                            lhs = xx[:, kc0 + k, half * P:(half + 1) * P]
                            rhs = w[:, slot, k, 0:n]
                            dst = ps_g[:, b, half * NS:half * NS + n]
                        else:
                            mm = m or P
                            lhs = w[:, slot, k, half * P:half * P + mm]
                            rhs = xx[:, kc0 + k, :]
                            dst = ps_g[0:mm, b, half * T:(half + 1) * T]
                        ins = pe.matmul(dst, lhs, rhs, start=(first and k == 0 and half == 0 and q == 0),
                                        stop=(last and k == n_k - 1 and q == 2), skip_group_check=True)
            ins.then_inc(slab_done, 1)

        def gwait(g):
            return out_count(g) - 1

        def x_in(n):
            def wait(c):
                pe.wait_ge(xl, PRE_I[n] * NX + c + 1)
            return wait

        def stat(n):
            if n:
                pe.wait_ge(sd_ok, n)
            pe.wait_ge(sq_ok, n + 1)
            if n == 4:
                pe.wait_ge(sqg, 4)
            if n in (5, 6):
                for k, c in enumerate(((0, 0), (0, 1), (3 if n == 5 else 2, 0), (3 if n == 5 else 2, 1))):
                    if n == 5 and k == 2:
                        pe.wait_ge(sq5, 4)
                    ins = pe.matmul(ps_s[:, 0, 0:T], ones[:, :], sq4[:, c[0], c[1], :], start=(k == 0), stop=(k == 3))
                ins.then_inc(stat_ok, 1)
                return
            terms = [(w, src[:, i, c, :]) for w, i in ([(ones, 0)] if n != 4 else [(ones, 1), (eps_ones, 0)])
                     for src in ((sq_sum, sq) if n in DIRECT else (sq_sum,)) for c in range(2)]
            for k, (w, v) in enumerate(terms):
                ins = pe.matmul(ps_s[:, 0, 0:T], w[:, :], v, start=(k == 0), stop=(k == len(terms) - 1))
            if n == 4:
                for k, (w, v) in enumerate(terms[4:]):
                    ins = pe.matmul(ps_s[:, 1, T:2 * T], ones[:, :], v, start=(k == 0), stop=(k == 3))
            ins.then_inc(stat_ok, 1)

        def stat_tok(n):
            pe.wait_ge(rs_ok, n + 1)
            if TOK[n]:
                pe.wait_ge(rst_ok, TOK[n])
            for tb in range(TB):
                ins = pe.matmul(ps_s[:, 1, tb:tb + 1], rs[0:1, 1, tb * P:(tb + 1) * P], ones[0:1, 0:1], start=True,
                                stop=True)
            ins.then_inc(rst_ps, 1)

        def attention(p, slab_step=None, compress=None):
            a, units = att[p], UNITS[p]
            n_units = len(units)

            def scores(i):
                u = units[i]
                if i >= 2:
                    pe.wait_ge(a["logit"], i - 1)
                for b, (c0, n) in enumerate(u["blocks"]):
                    ins = pe.matmul(ps_s[:, i % 2, c0:c0 + n], u["q"][:, b * P:(b + 1) * P], u["k"][b], start=True, stop=True)
                ins.then_inc(a["score"], 1)

            def normed(i):
                return units[i]["n_done"]

            def transposes(i):
                u = units[i]
                if u["pv"] is None:
                    return
                n = u["n"]
                pe.wait_ge(a["norm"], normed(i))
                if n >= 2:
                    pe.wait_ge(a["trc"], n - 1)
                for q, (c0, k) in enumerate(u["tiles"]):
                    ins = pe.transpose(ps_t[0:k, n % 2, q * P:(q + 1) * P], prob[:, i % PB, c0:c0 + k], ident[:, :])
                ins.then_inc(a["tr"], 1)

            def values(i):
                u = units[i]
                if u["pv"] is None:
                    return
                n, o = u["n"], u["seq"]
                for g in u.get("v_groups", ()):
                    pe.wait_ge(emptied[g % 2], out_count(g))
                pe.wait_ge(a["trc"], n + 1)
                if u["start"] and u["rows"][0] == 0 and o >= 2:
                    if p == 0 and o - 2 < DIFF_H:
                        pe.wait_ge(a["oh"], o - 1)
                    else:
                        pe.wait_ge(a["ol"], o - 1 - (DIFF_H if p == 0 else 0))
                r0, r1 = u["rows"]
                for q, (v, k, (c0, c1), (o0, o1)) in enumerate(u["pv"]):
                    ins = pe.matmul(ps_o[r0:r1, o % 2, o0:o1], v, prob_ts[p // 2][0:k, n % 2, c0:c1],
                                    start=(u["start"] and q == 0), stop=(u["stop"] and q == 1), skip_group_check=True)
                ins.then_inc(a["pv"], 1)

            for i in range(n_units + LAG_V):
                if i in IN_STEPS[p]:
                    slab_step(IN_STEPS[p][i])
                if p == 0 and i in (CMP1_STEP, CMP2_STEP):
                    compress(i == CMP2_STEP)
                if i < n_units:
                    for g in units[i].get("qk_groups", ()):
                        pe.wait_ge(emptied[g % 2], out_count(g))
                    scores(i)
                if LAG_T <= i < n_units + LAG_T:
                    transposes(i - LAG_T)
                if i >= LAG_V:
                    values(i - LAG_V)
                if p == 0 and i in DN_PS:
                    h = DN_PS.index(i)
                    if h == 0:
                        for g in (g0 + A_GROUPS[Q1], g0 + A_GROUPS[SV]):
                            pe.wait_ge(emptied[g % 2], out_count(g))
                    pe.wait_ge(dn["sq"], h + 1)
                    pe.matmul(ps_g[:, h // 2, (h % 2) * T:(h % 2 + 1) * T], ones[:, :], dsq[:, h, :], start=True, stop=True)\
                        .then_inc(dn["ps"], 1)

        pe.wait_ge(idn, 2)
        pe.wait_ge(ld["g"], 16)
        n_gain = PARAMS["norm_mix"][2]
        pe.transpose(ps_t[:, 1, 0:n_gain], prow[0:n_gain, 0, :], ident[0:n_gain, 0:n_gain]).then_inc(par_t, 1)
        pe.wait_ge(ld["x"], 32)
        for gi in range(4):
            if gi >= 2:
                pe.wait_ge(emptied[gi % 2], gi // 2)
            for c in range(2):
                for tb in range(TB):
                    ins = pe.transpose(ps_g[:, gi % 2, c * T + tb * P:c * T + (tb + 1) * P],
                                       xin[:, tb, (2 * gi + c) * P:(2 * gi + c + 1) * P], ident[:, :])
            ins.then_inc(xt, 1)
        g0 = st["a_in"].g0

        def a_slab(j):
            s, g = st["a_in"].s0 + j, g0 + A_GROUPS[j]
            gemm(s, s, gwait(g), g, act_hi, act_lo, before_chunk=x_in(0) if j == 0 else None,
                 tok_major=j in (DV0, DV1, SV, GATE), n=GATES if j == GATE else NS)

        def compress(second):
            g = g0 + (CMP2_GROUP if second else CMP1_GROUP)
            b = g % 2
            pe.wait_ge(emptied[b], gwait(g))
            if not second:
                pe.wait_ge(ld["cw"], 16 * 6)
                gi = g0 + A_GROUPS[KV_CMP]
                pe.wait_ge(emptied[gi % 2], out_count(gi))
                for i in range(2):
                    for m in range(16):
                        ins = pe.matmul(ps_g[:, b, i * T:i * T + 3 * NC].rearrange("p (g c) -> p g c", g=3), cw1[:, i, m, :],
                                        cmp2[:, i, :, 2 * m:2 * m + (NC - 1) * CMP_STRIDE + 1:CMP_STRIDE],
                                        start=(m == 0), stop=(m == 15))
                ins.then_inc(cmp_ps, 1)
                return
            gh = g0 + CMP1_GROUP
            pe.wait_ge(emptied[gh % 2], out_count(gh))
            pe.matmul(ps_g[:, b, 0:2 * NC], cw2[:, 0, :], chid[:, 0, :], start=True, stop=True)
            for gg in range(2):
                ins = pe.matmul(ps_g[0:NC, b, T + gg * HD:T + (gg + 1) * HD], chid[:, 1, gg * NC:(gg + 1) * NC],
                                cw2[:, 1, 0:HD], start=True, stop=True)
            ins.then_inc(cmp_ps2, 1)

        a_slab(0)
        stat(0)
        pe.wait_ge(ld["par"], 16 * len(PARAMS))
        for k in range(4):
            ins = pe.transpose(ps_t[:, 0, k * P:k * P + TILE_ROWS[k]], prow[0:TILE_ROWS[k], k, :],
                               ident[0:TILE_ROWS[k], 0:TILE_ROWS[k]])
        ins.then_inc(par_t, 1)
        pe.wait_ge(ld["bias"], 32)
        pe.matmul(ps_o[0:16, 0, 0:REL], btab[:, :], buck[:, :], start=True, stop=True).then_inc(brow_ps, 1)
        a_slab(1)
        stat_tok(0)
        for j in range(2, 5):
            a_slab(j)
        pe.wait_ge(rst_ok, 1)
        attention(0, a_slab, compress)

        def out_stage(name, n, h, l, ready):
            for j in range(4):
                s, g = st[name].s0 + j, st[name].g0 + j
                gemm(s, s, gwait(g), g, h, l, before_pair=ready if j == 0 else None)

        def mlp(up, dn_, n, l):
            s0, g0 = st[up].s0, st[up].g0
            for j in range(4):
                gemm(s0 + j, s0 + j, gwait(g0 + j), g0 + j, act_hi, act_lo, before_chunk=x_in(n) if j == 0 else None)
                if j == 0:
                    stat(n)
            with pe.Fori(1, 4) as i:
                for j in range(4):
                    gemm(s0 + i * 4 + j, s0 + j, gwait(g0 + j) + i * 2, g0 + j, act_hi, act_lo)
            s0, g0 = st[dn_].s0, st[dn_].g0
            with pe.Fori(0, 2) as i:
                for j in range(8):
                    def ready(pair, r=j % 4):
                        pe.wait_ge(hid_l, l * 16 + r * 4 + pair + 1)
                    gemm(s0 + i * 8 + j, s0 + j, gwait(g0 + j // 4) + i, g0 + j // 4, hid_hi, hid_lo, kc0=(j % 4) * 8,
                         first=j % 4 == 0, last=j % 4 == 3, before_pair=ready if j < 4 else None)

        def mix_in(p):
            def wait(pair):
                if p == 0 and pair >= 2:
                    pe.wait_ge(dn["lo"], 2 * pair - 2)
                else:
                    pe.wait_ge(att[p]["ol"], 2 * pair + 2)
            return wait

        pe.wait_ge(dn["sd"], 1)
        out_stage("a_out", 1, mix_hi, mix_lo, mix_in(0))
        mlp("a_up", "a_dn", 1, 0)

        def m_slab(j):
            s, g = st["m_in"].s0 + j, st["m_in"].g0 + j
            gemm(s, s, gwait(g), g, act_hi, act_lo, before_chunk=x_in(2) if j == 0 else None, tok_major=j % 3 == 2)
            if j == 0:
                stat(2)
            if j == 1:
                stat_tok(2)

        for j in range(3):
            m_slab(j)
        pe.wait_ge(rst_ok, 2)
        attention(1, m_slab)
        out_stage("m_out", 3, mix_hi, mix_lo, mix_in(1))
        mlp("m_up", "m_dn", 3, 1)
        s0, g0 = st["r_xa"].s0, st["r_xa"].g0
        for j in range(5):
            gemm(s0 + j, s0 + j, gwait(g0 + j), g0 + j, act_hi, act_lo, before_chunk=x_in(4) if j == 0 else None)
            if j == 0:
                pe.wait_ge(epso, 1)
                stat(4)
            if j == 1:
                stat_tok(4)
        s0, g0 = st["r_f"].s0, st["r_f"].g0
        gemm(s0, s0, gwait(g0), g0, act_hi, act_lo, m=ATT_H)
        s0, g0 = st["r_gate"].s0, st["r_gate"].g0
        for j in range(8):
            gemm(s0 + j, s0 + j, gwait(g0 + j), g0 + j, act_hi, act_lo)
            if j == RG_STEP:
                pe.wait_ge(ld["gw"], 16 * len(pieces))
                pe.wait_ge(rst_ok, 3)
                pe.wait_ge(sdf, 1)
                for j in range(NR):
                    srcs = rg_inputs(j)
                    pe.wait_ge(cvd, 6 * (srcs[-1] // 2) + 6)
                    if j >= 2:
                        pe.wait_ge(rg["sig"], j - 1)
                    for i in range(2):
                        for q, c in enumerate(srcs):
                            ins = pe.matmul(ps_s[:, j % 2, i * T:(i + 1) * T], gw[:, i, c, j - c + 1, :], xc[:, c, :],
                                            start=(q == 0), stop=(q == len(srcs) - 1))
                    ins.then_inc(rg["ps"], 1)
            if j == RG_STEP + 1:
                pe.wait_ge(fcum, 1)
                pe.wait_ge(rg["sig"], NR)
                for tb in range(TB):
                    ins = pe.transpose(ps_s[:, 0, tb * 16:(tb + 1) * 16], fl[:, 5, tb * P:(tb + 1) * P], ident[0:16, 0:16])
                ins.then_inc(fcq_ps, 1)
        s0, g0 = st["r_ga"].s0, st["r_ga"].g0
        for j in range(5):
            gemm(s0 + j, s0 + j, gwait(g0 + j), g0 + j, act_hi, act_lo)
        s0, g0 = st["r_v"].s0, st["r_v"].g0
        for j in range(4):
            gemm(s0 + j, s0 + j, gwait(g0 + j), g0 + j, act_hi, act_lo, tok_major=True)
        s0, g0 = st["r_pa"].s0, st["r_pa"].g0

        def ya_in(r):
            def wait(pair):
                pe.wait_ge(yl, (r * (NR // 2) + 2 * pair + 1) // 2 + 1 if r * (NR // 2) + 2 * pair + 1 < NR else 5)
            return wait

        for j in range(8):
            gemm(s0 + j, s0 + j, gwait(g0 + j // 2), g0 + j // 2, ya_hi, ya_lo, kc0=(j % 2) * (NR // 2), n_k=NR // 2,
                 first=j % 2 == 0, last=j % 2 == 1, before_pair=ya_in(j) if j < 2 else None)
        s0, g0 = st["r_qk"].s0, st["r_qk"].g0
        with pe.Fori(0, 2) as i:
            for j in range(4):
                gemm(s0 + i * 4 + j, s0 + j, gwait(g0 + j) + i * 2, g0 + j, act_hi, act_lo)
        for b in range(2):
            pe.wait_ge(emptied[(g0 + 6 + b) % 2], out_count(g0 + 6 + b))
        pe.wait_ge(fcq_ok, 1)
        attention(2)
        out_stage("r_pb", 6, act_hi, act_lo, mix_in(2))

        def m2_in(pair):
            pe.wait_ge(pbl, pair + 1)

        out_stage("r_out", 6, m2_hi, m2_lo, m2_in)
        stat(5)
        s0, g0 = st["f_up"].s0, st["f_up"].g0
        for j in range(4):
            gemm(s0 + j, s0 + j, gwait(g0 + j), g0 + j, act_hi, act_lo, before_chunk=x_in(6) if j == 0 else None)
            if j == 0:
                stat(6)
        with pe.Fori(1, 6) as i:
            for j in range(4):
                gemm(s0 + i * 4 + j, s0 + j, gwait(g0 + j) + i * 2, g0 + j, act_hi, act_lo)
        s0, g0 = st["f_dn"].s0, st["f_dn"].g0
        for j in range(12):
            def ready(pair, r=j % 3):
                pe.wait_ge(ful, r * 4 + pair + 1)
            gemm(s0 + j, s0 + j, gwait(g0 + j // 3), g0 + j // 3, h2_hi, h2_lo, kc0=(j % 3) * 8, first=j % 3 == 0,
                 last=j % 3 == 2, before_pair=ready if j < 3 else None, tok_major=True)
            if j == 2:
                pe.wait_ge(x_new_p, 2)
                pe.wait_ge(sd_ok, 7)
                for tb in range(TB):
                    for c in range(NX):
                        ins = pe.transpose((ps_s, ps_o)[tb][:, c // 4, c % 4 * P:(c % 4 + 1) * P],
                                           x[:, c, tb * P:(tb + 1) * P], ident[:, :])
                ins.then_inc(x_tok, 1)


_NAMES = [
    "x", "bias_table", "norm_mix", "norm_mlp", "norm_final", "mlp_w1", "mlp_w2", "ev_w_in", "ev_w_out",
    "ev_cmp_pos_k", "ev_cmp_w1_k", "ev_cmp_w2_k", "ev_cmp_pos_v", "ev_cmp_w1_v", "ev_cmp_w2_v", "ev_lam_q1",
    "ev_lam_k1", "ev_lam_q2", "ev_lam_k2", "ev_subln", "od_w_in", "od_w_out", "mix_norm_pre_2",
    "mix_norm_post_2", "w_in_2", "conv_a_w_2", "conv_a_b_2", "w_rg_a_2", "b_rg_a_2", "w_rg_x_2", "b_rg_x_2",
    "lru_lambda_2", "b_forget_2", "b_merge_2", "w_proj_a_2", "w_proj_b_2", "w_out_2", "ffn_norm_pre_2",
    "ffn_norm_post_2", "w_up_2", "conv_f_w_2", "conv_f_b_2", "w_down_2",
]


def kernel(**inputs):
    import concourse.bacc as bacc
    from concourse.bass_utils import run_bass_kernel_spmd

    nc = bacc.Bacc("TRN2", target_bir_lowering=False, num_devices=1)
    arrays, t = {}, {}
    for name in _NAMES:
        a = np.ascontiguousarray(inputs[name])
        arrays[f"in_{name}"] = a
        t[name] = nc.dram_tensor(f"in_{name}", a.shape, mybir.dt.from_np(a.dtype), kind="ExternalInput").ap()
    rows = bucket_rows()
    arrays["bucket_rows"] = rows
    t["bucket"] = nc.dram_tensor("bucket_rows", rows.shape, F32, kind="ExternalInput").ap()
    out = nc.dram_tensor("out", (1, T, D), F32, kind="ExternalOutput").ap()
    with ExitStack() as ctx:
        build(nc, ctx, t, out)
    return run_bass_kernel_spmd(nc, [arrays], core_ids=[0]).results[0]["out"]
```
